# Optimizing a Trainium2 kernel written in Bass

```python
import math
import jax
import jax.numpy as jnp
from jax import lax
import numpy as np

D_MODEL = 1024
BATCH = 1
SEQ = 1024
DEPTH = 2

CHUNK = 64
Q_BLOCK = 128
RMS_EPS = 1e-6
MAX_POS_OFFSET = 4096

MIX_WIDTH = D_MODEL
GROUP_WIDTH = MIX_WIDTH // 4

CONV_A_WIDTH = 3
A_COLS = 3 * GROUP_WIDTH

FOX_HEAD_DIM = 64
FOX_HEADS = GROUP_WIDTH // FOX_HEAD_DIM
B_COLS = 3 * GROUP_WIDTH + FOX_HEADS

SSM_INNER = GROUP_WIDTH
SSM_HEAD_DIM = 64
SSM_HEADS = SSM_INNER // SSM_HEAD_DIM
SSM_GROUPS = 2
SSM_HEADS_PER_GROUP = SSM_HEADS // SSM_GROUPS
SSM_STATE = 64
SSM_CONV = 4
SSM_CONV_DIM = SSM_INNER + 2 * SSM_GROUPS * SSM_STATE
C_COLS = SSM_INNER + SSM_CONV_DIM + SSM_HEADS

MLA_HEADS = 4
MLA_NOPE = 64
MLA_ROPE = 32
MLA_V = GROUP_WIDTH // MLA_HEADS
MLA_Q_LORA = 256
MLA_KV_LORA = 128
ROPE_BASE = 10000.0
D_COLS = MLA_Q_LORA + MLA_KV_LORA + MLA_ROPE

IN_COLS = A_COLS + B_COLS + C_COLS + D_COLS
MIX_SPLITS = [A_COLS, A_COLS + B_COLS, A_COLS + B_COLS + C_COLS]

N_EXPERT_GROUPS = 4
EXPERTS_PER_GROUP = 8
N_EXPERTS = N_EXPERT_GROUPS * EXPERTS_PER_GROUP
TOP_K = 2
EXPERT_FF = 256
MOE_BLOCK = 128

kernel_name = "hybrid_chunk_causal_block"

def rms_norm(x, g):
    xf = x.astype(jnp.float32)
    y = xf * lax.rsqrt(jnp.mean(xf * xf, axis=-1, keepdims=True) + RMS_EPS)
    return (y * g.astype(jnp.float32)).astype(x.dtype)

def causal_depthwise_conv(x, w):
    k, c = w.shape
    return lax.conv_general_dilated(
        x, w.astype(x.dtype)[:, None, :], window_strides=(1,), padding=[(k - 1, 0)],
        dimension_numbers=('NWC', 'WIO', 'NWC'), feature_group_count=c)

def split_heads(t, n):
    b, s, _ = t.shape
    return t.reshape(b, s, n, -1).transpose(0, 2, 1, 3)

def merge_heads(t):
    b, h, s, d = t.shape
    return t.transpose(0, 2, 1, 3).reshape(b, s, h * d)

def frame_causal(tq, tk):
    return tk <= tq

def chunk_causal(tq, tk):
    return (tk // CHUNK) <= (tq // CHUNK)

def block_attention(q, k, v, allowed, log_decay=None):
    seq = q.shape[2]
    scale = q.shape[-1] ** -0.5
    outs = []
    for i in range(seq // Q_BLOCK):
        q0, q1 = i * Q_BLOCK, (i + 1) * Q_BLOCK
        s = jnp.einsum('bhqd,bhkd->bhqk', q[:, :, q0:q1], k[:, :, :q1]).astype(jnp.float32) * scale
        if log_decay is not None:
            s = s + (log_decay[:, :, q0:q1, None] - log_decay[:, :, None, :q1])
        tq = jnp.arange(q0, q1)[:, None]
        tk = jnp.arange(q1)[None, :]
        s = jnp.where(allowed(tq, tk), s, -jnp.inf)
        p = jax.nn.softmax(s, axis=-1).astype(v.dtype)
        outs.append(jnp.einsum('bhqk,bhkd->bhqd', p, v[:, :, :q1]))
    return jnp.concatenate(outs, axis=2)

def short_conv_mixer(p, conv_w):
    b_gate, c_gate, val = jnp.split(p, 3, axis=-1)
    return b_gate * causal_depthwise_conv(c_gate * val, conv_w)

def forgetting_attention(p, forget_bias):
    q, k, v, f_logit = jnp.split(p, [GROUP_WIDTH, 2 * GROUP_WIDTH, 3 * GROUP_WIDTH], axis=-1)
    log_f = jax.nn.log_sigmoid((f_logit + forget_bias).astype(jnp.float32))
    cum = jnp.cumsum(log_f, axis=1).transpose(0, 2, 1)
    out = block_attention(split_heads(q, FOX_HEADS), split_heads(k, FOX_HEADS),
                          split_heads(v, FOX_HEADS), frame_causal, cum)
    return merge_heads(out)

def segsum(a):
    t = a.shape[-1]
    ae = jnp.broadcast_to(a[..., None], a.shape + (t,))
    ae = jnp.where(jnp.tril(jnp.ones((t, t), bool), -1), ae, 0.0)
    ss = jnp.cumsum(ae, axis=-2)
    return jnp.where(jnp.tril(jnp.ones((t, t), bool), 0), ss, -jnp.inf)

def ssd_chunked(x, a, b, c):
    bsz, seq, h, pdim = x.shape
    n = b.shape[-1]
    nc = seq // CHUNK
    x = x.reshape(bsz, nc, CHUNK, h, pdim).astype(jnp.float32)
    b = b.reshape(bsz, nc, CHUNK, h, n).astype(jnp.float32)
    c = c.reshape(bsz, nc, CHUNK, h, n).astype(jnp.float32)
    a = a.reshape(bsz, nc, CHUNK, h).astype(jnp.float32).transpose(0, 3, 1, 2)
    a_cum = jnp.cumsum(a, axis=-1)
    decay_in = jnp.exp(segsum(a))
    y_diag = jnp.einsum('bclhn,bcshn,bhcls,bcshp->bclhp', c, b, decay_in, x)
    decay_states = jnp.exp(a_cum[..., -1:] - a_cum)
    states = jnp.einsum('bclhn,bhcl,bclhp->bchpn', b, decay_states, x)
    chunk_decay = jnp.exp(a_cum[..., -1])

    def step(carry, inp):
        st, dec = inp
        return carry * dec[..., None, None] + st, carry

    init = jnp.zeros((bsz, h, pdim, n), jnp.float32)
    _, prev = lax.scan(step, init, (states.transpose(1, 0, 2, 3, 4), chunk_decay.transpose(2, 0, 1)))
    prev = prev.transpose(1, 0, 2, 3, 4)
    y_off = jnp.einsum('bclhn,bchpn,bhcl->bclhp', c, prev, jnp.exp(a_cum))
    return (y_diag + y_off).reshape(bsz, seq, h, pdim)

def ssd_mixer(p, conv_w, conv_b, dt_bias, a_log, d_skip, norm_g):
    z, xbc, dt_raw = jnp.split(p, [SSM_INNER, SSM_INNER + SSM_CONV_DIM], axis=-1)
    xbc = jax.nn.silu(causal_depthwise_conv(xbc, conv_w) + conv_b)
    xs, bs, cs = jnp.split(xbc, [SSM_INNER, SSM_INNER + SSM_GROUPS * SSM_STATE], axis=-1)
    bsz, seq, _ = p.shape
    xs = xs.reshape(bsz, seq, SSM_HEADS, SSM_HEAD_DIM)
    bs = jnp.repeat(bs.reshape(bsz, seq, SSM_GROUPS, SSM_STATE), SSM_HEADS_PER_GROUP, axis=2)
    cs = jnp.repeat(cs.reshape(bsz, seq, SSM_GROUPS, SSM_STATE), SSM_HEADS_PER_GROUP, axis=2)
    dt = jax.nn.softplus((dt_raw + dt_bias).astype(jnp.float32))
    a = -jnp.exp(a_log.astype(jnp.float32))
    y = ssd_chunked(xs * dt[..., None], dt * a, bs, cs)
    y = y + d_skip.astype(jnp.float32)[:, None] * xs.astype(jnp.float32)
    y = y.reshape(bsz, seq, SSM_INNER).astype(p.dtype) * jax.nn.silu(z)
    return rms_norm(y, norm_g)

def rotary_cos_sin(positions, dim):
    inv_freq = ROPE_BASE ** (-jnp.arange(0, dim, 2, dtype=jnp.float32) / dim)
    ang = positions.astype(jnp.float32)[..., None] * inv_freq
    return jnp.cos(ang), jnp.sin(ang)

def apply_rotary(x, cos, sin):
    half = x.shape[-1] // 2
    xf = x.astype(jnp.float32)
    x1, x2 = xf[..., :half], xf[..., half:]
    return jnp.concatenate([x1 * cos - x2 * sin, x2 * cos + x1 * sin], axis=-1).astype(x.dtype)

def latent_attention(p, positions, q_norm, kv_norm, w_uq, w_ukv):
    bsz, seq, _ = p.shape
    c_q, c_kv, k_rope = jnp.split(p, [MLA_Q_LORA, MLA_Q_LORA + MLA_KV_LORA], axis=-1)
    q = (rms_norm(c_q, q_norm) @ w_uq).reshape(bsz, seq, MLA_HEADS, MLA_NOPE + MLA_ROPE)
    kv = (rms_norm(c_kv, kv_norm) @ w_ukv).reshape(bsz, seq, MLA_HEADS, MLA_NOPE + MLA_V)
    q_nope, q_rope = jnp.split(q, [MLA_NOPE], axis=-1)
    k_nope, v = jnp.split(kv, [MLA_NOPE], axis=-1)
    cos, sin = rotary_cos_sin(positions, MLA_ROPE)
    q_rope = apply_rotary(q_rope, cos[:, :, None, :], sin[:, :, None, :])
    k_rope = apply_rotary(k_rope, cos, sin)
    q = jnp.concatenate([q_nope, q_rope], axis=-1).transpose(0, 2, 1, 3)
    k = jnp.concatenate([k_nope, jnp.broadcast_to(k_rope[:, :, None, :], (bsz, seq, MLA_HEADS, MLA_ROPE))],
                        axis=-1).transpose(0, 2, 1, 3)
    out = block_attention(q, k, v.transpose(0, 2, 1, 3), chunk_causal)
    return merge_heads(out)

def grouped_expert_ffn(xf, expert_idx, weights, w_gate, w_up, w_down):
    t, d = xf.shape
    n_exp = w_gate.shape[0]
    n_slots = expert_idx.size
    n_blocks = -(-(n_slots + n_exp * (MOE_BLOCK - 1)) // MOE_BLOCK)
    n_rows = n_blocks * MOE_BLOCK
    flat_e = expert_idx.reshape(-1)
    flat_w = weights.reshape(-1)
    order = jnp.argsort(flat_e)
    sorted_e = flat_e[order]
    counts = jnp.zeros((n_exp,), jnp.int32).at[flat_e].add(1)
    padded = (counts + MOE_BLOCK - 1) // MOE_BLOCK * MOE_BLOCK
    start = jnp.cumsum(counts) - counts
    padded_end = jnp.cumsum(padded)
    padded_start = padded_end - padded
    dest = padded_start[sorted_e] + jnp.arange(n_slots, dtype=jnp.int32) - start[sorted_e]
    row_token = jnp.full((n_rows,), t, jnp.int32).at[dest].set((order // TOP_K).astype(jnp.int32))
    row_w = jnp.zeros((n_rows,), xf.dtype).at[dest].set(flat_w[order])
    block_expert = jnp.minimum(
        jnp.searchsorted(padded_end, jnp.arange(n_blocks, dtype=jnp.int32) * MOE_BLOCK, side='right'),
        n_exp - 1)
    x_rows = jnp.concatenate([xf, jnp.zeros((1, d), xf.dtype)], axis=0)[row_token]
    x_rows = x_rows.reshape(n_blocks, MOE_BLOCK, d)

    def expert_block(args):
        xb, e = args
        return (jax.nn.silu(xb @ w_gate[e]) * (xb @ w_up[e])) @ w_down[e]

    y_rows = lax.map(expert_block, (x_rows, block_expert)).reshape(n_rows, d)
    return jax.ops.segment_sum(y_rows * row_w[:, None], row_token, num_segments=t + 1)[:t]

def hierarchical_moe(h, rg_w, rg_b, re_w, re_b, w_gate, w_up, w_down):
    bsz, seq, d = h.shape
    t = bsz * seq
    xf = h.reshape(t, d)
    g_prob = jax.nn.softmax((xf @ rg_w + rg_b).astype(jnp.float32), axis=-1)
    g_w, g_idx = lax.top_k(g_prob, 1)
    e_logits = (xf @ re_w + re_b).astype(jnp.float32).reshape(t, N_EXPERT_GROUPS, EXPERTS_PER_GROUP)
    e_logits = jnp.take_along_axis(e_logits, g_idx[:, :, None], axis=1)[:, 0]
    e_prob = jax.nn.softmax(e_logits, axis=-1)
    e_w, e_local = lax.top_k(e_prob, TOP_K)
    e_w = e_w / jnp.sum(e_w, axis=-1, keepdims=True)
    weights = (g_w * e_w).astype(h.dtype)
    expert_idx = g_idx * EXPERTS_PER_GROUP + e_local
    y = grouped_expert_ffn(xf, expert_idx, weights, w_gate, w_up, w_down)
    return y.reshape(bsz, seq, d)

def setup_inputs(seed: int = 0) -> dict:
    key = jax.random.key(seed)
    ks = jax.random.split(key, 28)
    f32 = jnp.float32

    def nrm(k, shape, fan_in):
        return jax.random.normal(k, shape, f32) * fan_in ** -0.5

    def gain(k, shape):
        return 1.0 + 0.02 * jax.random.normal(k, shape, f32)

    x = jax.random.normal(ks[0], (BATCH, SEQ, D_MODEL), f32)
    offsets = jax.random.randint(ks[1], (BATCH, 1), 0, MAX_POS_OFFSET, jnp.int32)
    positions = offsets + jnp.arange(SEQ, dtype=jnp.int32)[None, :]
    dt_init = jnp.exp(jax.random.uniform(ks[9], (DEPTH, SSM_HEADS), f32, math.log(1e-3), math.log(1e-1)))
    return {
        'x': x,
        'positions': positions,
        'norm_mix': gain(ks[2], (DEPTH, D_MODEL)),
        'w_in': nrm(ks[3], (DEPTH, D_MODEL, IN_COLS), D_MODEL),
        'conv_a': nrm(ks[4], (DEPTH, CONV_A_WIDTH, GROUP_WIDTH), CONV_A_WIDTH),
        'fox_forget_bias': jax.random.uniform(ks[5], (DEPTH, FOX_HEADS), f32, 1.0, 4.0),
        'ssm_conv_w': nrm(ks[6], (DEPTH, SSM_CONV, SSM_CONV_DIM), SSM_CONV),
        'ssm_conv_b': 0.02 * jax.random.normal(ks[7], (DEPTH, SSM_CONV_DIM), f32),
        'ssm_dt_bias': dt_init + jnp.log(-jnp.expm1(-dt_init)),
        'ssm_a_log': jnp.log(jax.random.uniform(ks[10], (DEPTH, SSM_HEADS), f32, 1.0, 16.0)),
        'ssm_d': 1.0 + 0.1 * jax.random.normal(ks[11], (DEPTH, SSM_HEADS), f32),
        'ssm_norm': gain(ks[12], (DEPTH, SSM_INNER)),
        'mla_q_norm': gain(ks[13], (DEPTH, MLA_Q_LORA)),
        'mla_kv_norm': gain(ks[14], (DEPTH, MLA_KV_LORA)),
        'mla_w_uq': nrm(ks[15], (DEPTH, MLA_Q_LORA, MLA_HEADS * (MLA_NOPE + MLA_ROPE)), MLA_Q_LORA),
        'mla_w_ukv': nrm(ks[16], (DEPTH, MLA_KV_LORA, MLA_HEADS * (MLA_NOPE + MLA_V)), MLA_KV_LORA),
        'w_out': nrm(ks[17], (DEPTH, MIX_WIDTH, D_MODEL), MIX_WIDTH),
        'norm_ffn': gain(ks[18], (DEPTH, D_MODEL)),
        'router_group_w': nrm(ks[19], (DEPTH, D_MODEL, N_EXPERT_GROUPS), D_MODEL),
        'router_group_b': 0.01 * jax.random.normal(ks[20], (DEPTH, N_EXPERT_GROUPS), f32),
        'router_expert_w': nrm(ks[21], (DEPTH, D_MODEL, N_EXPERTS), D_MODEL),
        'router_expert_b': 0.01 * jax.random.normal(ks[22], (DEPTH, N_EXPERTS), f32),
        'expert_w_gate': nrm(ks[23], (DEPTH, N_EXPERTS, D_MODEL, EXPERT_FF), D_MODEL),
        'expert_w_up': nrm(ks[24], (DEPTH, N_EXPERTS, D_MODEL, EXPERT_FF), D_MODEL),
        'expert_w_down': nrm(ks[25], (DEPTH, N_EXPERTS, EXPERT_FF, D_MODEL), EXPERT_FF),
        'norm_final': gain(ks[26], (D_MODEL,)),
    }

def reference(x, positions, norm_mix, w_in, conv_a, fox_forget_bias, ssm_conv_w, ssm_conv_b,
              ssm_dt_bias, ssm_a_log, ssm_d, ssm_norm, mla_q_norm, mla_kv_norm, mla_w_uq, mla_w_ukv,
              w_out, norm_ffn, router_group_w, router_group_b, router_expert_w, router_expert_b,
              expert_w_gate, expert_w_up, expert_w_down, norm_final):
    for l in range(DEPTH):
        h = rms_norm(x, norm_mix[l])
        proj = h @ w_in[l]
        p_a, p_b, p_c, p_d = jnp.split(proj, MIX_SPLITS, axis=-1)
        y = jnp.concatenate([
            short_conv_mixer(p_a, conv_a[l]),
            forgetting_attention(p_b, fox_forget_bias[l]),
            ssd_mixer(p_c, ssm_conv_w[l], ssm_conv_b[l], ssm_dt_bias[l], ssm_a_log[l], ssm_d[l], ssm_norm[l]),
            latent_attention(p_d, positions, mla_q_norm[l], mla_kv_norm[l], mla_w_uq[l], mla_w_ukv[l]),
        ], axis=-1)
        x = x + y @ w_out[l]
        h = rms_norm(x, norm_ffn[l])
        x = x + hierarchical_moe(h, router_group_w[l], router_group_b[l], router_expert_w[l],
                                 router_expert_b[l], expert_w_gate[l], expert_w_up[l], expert_w_down[l])
    return rms_norm(x, norm_final)


_drawn_inputs = setup_inputs


def setup_inputs(seed=0):
    import zlib

    import numpy as np

    out = dict(_drawn_inputs(seed))
    spreads = {}
    factors = {'mla_q_norm': 8.0,
     'mla_kv_norm': 8.0,
     'router_group_b': 3.758,
     'router_expert_b': 4.347,
     'norm_final': 2.804}
    for name, (base, spread) in spreads.items():
        noise = np.random.default_rng([zlib.crc32(name.encode()), seed]).standard_normal(out[name].shape)
        drawn = base * np.exp(spread * noise) if base else spread * noise
        out[name] = jnp.asarray(drawn.astype(out[name].dtype))
    for name, factor in factors.items():
        out[name] = (out[name] * factor).astype(out[name].dtype)
    return out
```

```python
from contextlib import ExitStack

import numpy as np

import concourse.bass as bass
from concourse import mybir

ALU = mybir.AluOpType
ACT = mybir.ActivationFunctionType
AX = mybir.AxisListType.X
F32 = mybir.dt.float32
BF16 = mybir.dt.bfloat16
I32 = mybir.dt.int32

P = 128
LOG_P = 7
D = 1024
S = 1024
DEPTH = 2
T = S // P
KD = D // P
EPS = 1e-6
HALF = 512

GW = 256
HEADS = 4
HD = 64
FOX_K = HD + 2
MLA_D = 96
ROPE = 32
HR = ROPE // 2
TAPS_A = 3
TAPS_C = 4
STATE = 64

A0 = 0
B0 = 3 * GW
F0 = B0 + 3 * GW
C0 = F0 + HEADS
XBC0 = C0 + GW
DT0 = XBC0 + 512
D0 = DT0 + HEADS
KV0 = D0 + GW
IN_COLS = KV0 + P + ROPE

G = 4
EG = 8
E = G * EG
FF = 256
BLOCKS = 48
LEAST = 2 * S // P
BLK = 50
NEG = -1.0e30

PAIRS = [("xbc", 0, XBC0), ("xbc", 2, XBC0 + GW), ("cgate", 0, A0 + GW), ("val", 0, A0 + 2 * GW),
         ("bgate", 0, A0), ("q", 0, B0), ("k", 0, B0 + GW)]
GROUPS = [("z", C0, GW), ("vf", B0 + 2 * GW, GW + HEADS), ("dtq", DT0, HEADS + GW), ("kv", KV0, P + ROPE)]
WMAX = GW + HEADS

PARAMS = TAPS_C + 1 + TAPS_A + 13

CONST = {}


def constants():
    i = np.arange(P)
    parts = {
        "ident": np.eye(P),
        "le": i[:, None] <= i[None, :],
        "lt": i[:, None] < i[None, :],
        "gt": i[:, None] > i[None, :],
        "ones": np.ones((P, P)),
        "iota": np.broadcast_to(i, (P, P)),
        "mask_fox": np.where(i[None, :] > i[:, None], NEG, 0.0),
        "mask_mla": np.where((i[None, :] // 64) > (i[:, None] // 64), NEG, 0.0),
        "mask_ssd": np.where(i[None, :] < i[:, None], NEG, 0.0),
        "token": np.arange(T)[None, :] * P + i[:, None],
        "freq": np.broadcast_to(10000.0 ** (-np.arange(0, ROPE, 2) / ROPE), (P, HR)),
        "power": np.full((P, T), -0.5),
        "sign": np.broadcast_to(np.repeat([-1.0, 1.0], HEADS), (P, 2 * HEADS)),
        "rank4": np.broadcast_to(G - np.arange(G), (P, G)),
        "rank8": np.broadcast_to(EG - np.arange(EG), (P, EG)),
        "prefix": np.broadcast_to(np.tril(np.ones((E, E))).reshape(1, E * E), (P, E * E)),
    }
    at = 0
    for name, a in parts.items():
        CONST[name] = (at, a.shape[1])
        at += a.shape[1]
    return np.ascontiguousarray(np.concatenate([np.asarray(a, np.float32) for a in parts.values()], 1))


CONSTANTS = constants()


def linker(eng, sem):
    count = [0]

    def link(ins):
        count[0] += 1
        ins.then_inc(sem, 1)
        eng.wait_ge(sem, count[0])

    return link


class Core:
    pass


class Stage:

    def __init__(self, nc, pool_dmas=False):
        self.nc, self.ctx, self.sems, self.pool_dmas = nc, ExitStack(), [], pool_dmas

    def __enter__(self):
        return self

    def sem(self, name):
        s = self.ctx.enter_context(self.nc.semaphore(name))
        self.sems.append(s)
        return s

    def sb(self, name, shape, dtype=F32):
        return self.ctx.enter_context(self.nc.sbuf_tensor(name, shape, dtype))

    def __exit__(self, *_):
        nums = sorted(s.num for s in self.sems)
        assert nums[-1] - nums[0] + 1 == len(nums)
        if self.pool_dmas:
            self.nc.gpsimd.dma_reset(range(nums[0], nums[-1] + 1))
        self.nc.all_engine_barrier(sems_to_clear=range(nums[0], nums[-1] + 1))
        self.ctx.close()


def bc(ap, *shape):
    return ap.broadcast_to(list(shape))


def rstd(nc, k, link, ssq, n):
    link(nc.gpsimd.tensor_scalar(ssq, ssq, 1.0 / n, EPS, ALU.mult, ALU.add))
    return nc.gpsimd.tensor_tensor(ssq, ssq, k.c("power")[:, 0:ssq.shape[1]], ALU.pow)


def setup(nc, k):
    with Stage(nc) as st:
        consts_in, x_in, pos_in = st.sem("consts_in"), st.sem("x_in"), st.sem("pos_in")
        step, angle_ready, trig_done = st.sem("setup_step"), st.sem("angle_ready"), st.sem("trig_done")
        zeros_set = st.sem("zeros_set")
        pos_i = st.sb("pos_i", [P, T], I32)
        pos_f = st.sb("pos_f", [P, T])
        ang = st.sb("ang", [P, T, HR])
        turn = st.sb("turn", [P, T, HR])
        cosa = st.sb("cosa", [P, T, HR])
        with nc.Block() as block:
            @block.sync
            def _(sp):
                sp.dma_start(k.const[:, :], k.d_const[:, :]).then_inc(consts_in, 16)
                with nc.allow_non_contiguous_dma("positions, one to a partition"):
                    sp.dma_start(pos_i[:], k.positions.rearrange("b (t p) -> p (b t)", p=P)).then_inc(pos_in, 16)
                sp.dma_start(k.x[:], k.d_x.rearrange("b (t p) n -> p (b t) n", p=P)).then_inc(x_in, 16)
                sp.wait_ge(x_in, 16)

            @block.vector
            def _(dve):
                link = linker(dve, step)
                dve.wait_ge(consts_in, 16)
                for name, tile, reps in (("ident", k.ident_b, 1), ("mask_fox", k.mask_fox, 1), ("mask_mla", k.mask_mla, 1),
                                         ("mask_ssd", k.mask_ssd, HEADS)):
                    for r in range(reps):
                        nc.vector.tensor_copy(tile[:, r * P:(r + 1) * P], k.c(name))
                dve.wait_ge(pos_in, 16)
                link(nc.vector.tensor_copy(pos_f[:], pos_i[:]))
                link(nc.vector.tensor_tensor(ang[:], bc(pos_f[:].unsqueeze(2), P, T, HR),
                                             bc(k.c("freq").unsqueeze(1), P, T, HR), ALU.mult))
                big = 1.5 * 2.0 ** 23
                link(nc.vector.tensor_scalar(turn[:], ang[:], float(1.0 / (2 * np.pi)), None, ALU.mult))
                link(nc.vector.tensor_scalar(turn[:], turn[:], big, None, ALU.add))
                link(nc.vector.tensor_scalar(turn[:], turn[:], -big, None, ALU.add))
                c1 = 6.28125
                c2 = float(np.round((2 * np.pi - c1) * 2 ** 21) / 2 ** 21)
                c3 = float(2 * np.pi - c1 - c2)
                for c in (c1, c2, c3):
                    link(nc.vector.scalar_tensor_tensor(ang[:], turn[:], -c, ang[:], ALU.mult, ALU.add))
                link(nc.vector.tensor_scalar(cosa[:], ang[:], float(np.pi / 2), None, ALU.add))
                link(nc.vector.tensor_scalar(turn[:], cosa[:], float(np.pi), None, ALU.is_gt))
                link(nc.vector.scalar_tensor_tensor(cosa[:], turn[:], float(-2 * np.pi), cosa[:], ALU.mult, ALU.add))
                lim = 3.1415925
                link(nc.vector.tensor_scalar(cosa[:], cosa[:], lim, -lim, ALU.min, ALU.max))
                nc.vector.tensor_scalar(ang[:], ang[:], lim, -lim, ALU.min, ALU.max).then_inc(angle_ready, 1)

            @block.gpsimd
            def _(pool):
                nc.gpsimd.memset(k.zeros[:], 0.0).then_inc(zeros_set, 1)

            @block.scalar
            def _(act):
                act.wait_ge(zeros_set, 1)
                spare = k.d_y[LEAST * P:, :].rearrange("(b p) n -> p b n", p=P)
                act.dma_start(spare, bc(k.zeros[:].unsqueeze(1), P, BLOCKS - LEAST, D)).then_inc(k.spare_filled, 16)
                act.wait_ge(angle_ready, 1)
                nc.scalar.activation(k.trig[:, 1], ang[:], ACT.Sin)
                nc.scalar.activation(k.trig[:, 0], cosa[:], ACT.Sin).then_inc(trig_done, 1)
                act.wait_ge(trig_done, 1)


def project(nc, k, l):
    with Stage(nc) as st:
        params_in, gain_in = st.sem("params_in"), st.sem("gain_in")
        squares, norm_step, h_ready = st.sem("squares"), st.sem("norm_step"), st.sem("h_ready")
        rstd_ready = st.sem("rstd_ready")
        turned, ht_act, ht_dve = st.sem("turned"), st.sem("ht_act"), st.sem("ht_dve")
        w_in_sem = [st.sem("w_in_even"), st.sem("w_in_odd")]
        w_used, proj_ready = st.sem("w_used"), st.sem("proj_ready")
        act_took, dve_took = st.sem("act_took"), st.sem("dve_took")
        conv_step, conv_done, silu_done, a_done = (st.sem("conv_step"), st.sem("conv_done"), st.sem("silu_done"),
                                                   st.sem("a_done"))
        ring = st.sb("w_ring", [P, 2, KD, WMAX])
        ssq = st.sb("ssq", [P, T])
        over = k.over
        cbuf = over[:, 0:2 * S].rearrange("p (j s) -> p j s", j=2)
        upad = over[:, 2 * S:2 * S + 2 * (S + 2)].rearrange("p (j s) -> p j s", j=2)
        r0 = 4 * S + 4
        raw = over[:, r0:r0 + 2 * (S + 3)].rearrange("p (j s) -> p j s", j=2)
        hn = raw[:, :, 3:]
        loads = [(c0, GW) for _, _, c0 in PAIRS] + [(c0, n) for _, c0, n in GROUPS]

        taker = []
        for kind, _, _ in PAIRS:
            taker += [kind in ("val", "bgate")] * 4
        taker += [False] * (len(GROUPS) * T)

        def emptied(eng, q):
            sem = dve_took if taker[q] else act_took
            eng.wait_ge(sem, sum(t == taker[q] for t in taker[:q + 1]))

        with nc.Block() as block:
            @block.gpsimd
            def _(pool):
                link = linker(pool, norm_step)
                for t in range(T):
                    pool.wait_ge(squares, t + 1)
                    rstd(nc, k, link, ssq[:, t:t + 1], D).then_inc(rstd_ready, 1)

            @block.sync
            def _(sp):
                row = bass.ds(l, 1)
                sp.dma_start(k.gain[:], bc(k.norm_mix[row, :], P, D)).then_inc(gain_in, 16)

                def load_params():
                    def load(dst, src):
                        sp.dma_start(dst, src).then_inc(params_in, 16)

                    with nc.allow_non_contiguous_dma("small parameter tables"):
                        for tap in range(TAPS_C):
                            load(k.cw[:, :, tap], k.ssm_conv_w[row, tap].rearrange("a (j p) -> p (a j)", p=P))
                        load(k.cb[:], k.ssm_conv_b[row].rearrange("a (j p) -> p (a j)", p=P))
                        for tap in range(TAPS_A):
                            load(k.ca[:, :, tap], k.conv_a[row, tap].rearrange("a (j p) -> p (a j)", p=P))
                    load(k.bias8[:, 0:HEADS], bc(k.fox_forget_bias[row, :], P, HEADS))
                    load(k.bias8[:, HEADS:], bc(k.ssm_dt_bias[row, :], P, HEADS))
                    load(k.alog[:], bc(k.ssm_a_log[row, :], P, HEADS))
                    load(k.dskip[:], bc(k.ssm_d[row, :], P, HEADS))
                    load(k.sng[:], bc(k.ssm_norm[row, :], P, GW))
                    load(k.qng[:], bc(k.mla_q_norm[row, :], P, GW))
                    load(k.kvng[:], bc(k.mla_kv_norm[row, :], P, P))
                    load(k.rb[:, 0:G], bc(k.router_group_b[row, :], P, G))
                    load(k.rb[:, G:], bc(k.router_expert_b[row, :], P, E))
                    load(k.wuq[:], k.mla_w_uq[row].rearrange("a (c p) n -> p (a c) n", p=P))
                    load(k.wukv[:], k.mla_w_ukv[row].rearrange("a p n -> p (a n)"))
                    load(k.rw[:, :, 0:G], k.router_group_w[row].rearrange("a (c p) n -> p (a c) n", p=P))
                    load(k.rw[:, :, G:], k.router_expert_w[row].rearrange("a (c p) n -> p (a c) n", p=P))

                for i, (c0, n) in enumerate(loads):
                    if i == 2:
                        load_params()
                    if i >= 2:
                        sp.wait_ge(w_used, i - 1)
                    src = k.w_in[bass.ds(l, 1), :, c0:c0 + n].rearrange("a (c p) n -> p (a c) n", p=P)
                    sp.dma_start(ring[:, i % 2, :, 0:n], src).then_inc(w_in_sem[i % 2], 16)

            @block.tensor
            def _(pe):
                for t in range(T):
                    pe.wait_ge(h_ready, t + 1)
                    if t >= 2:
                        pe.wait_ge(ht_act, t - 1)
                        pe.wait_ge(ht_dve, t - 1)
                    for c in range(KD):
                        last = nc.tensor.transpose(k.ps[:, 2 * (t % 2) + c // 4, (c % 4) * P:(c % 4 + 1) * P],
                                                   hn[:, t % 2, c * P:(c + 1) * P], k.c("ident"))
                    last.then_inc(turned, 1)
                pe.wait_ge(ht_act, T)
                pe.wait_ge(ht_dve, T)
                q = 0
                for i in range(len(PAIRS)):
                    pe.wait_ge(w_in_sem[i % 2], 16 * (i // 2 + 1))
                    for j in range(2):
                        for n in range(2):
                            if q >= 4:
                                emptied(pe, q - 4)
                            for c in range(KD):
                                last = nc.tensor.matmul(k.ps[:, 4 + q % 4, :], ring[:, i % 2, c, j * P:(j + 1) * P],
                                                        k.hT[:, c, n * HALF:(n + 1) * HALF], start=(c == 0), stop=(c == KD - 1))
                            last.then_inc(proj_ready, 1)
                            q += 1
                    pe.wait_ge(proj_ready, q)
                    pe.sem_inc(w_used, 1)
                for g, (_, _, n) in enumerate(GROUPS):
                    i = len(PAIRS) + g
                    pe.wait_ge(w_in_sem[i % 2], 16 * (i // 2 + 1))
                    for t in range(T):
                        emptied(pe, q - 4)
                        for c in range(KD):
                            last = nc.tensor.matmul(k.ps[:, 4 + q % 4, 0:n], k.hT[:, c, t * P:(t + 1) * P],
                                                    ring[:, i % 2, c, 0:n], start=(c == 0), stop=(c == KD - 1))
                        last.then_inc(proj_ready, 1)
                        q += 1
                    if g < 2:
                        pe.wait_ge(proj_ready, q)
                        pe.sem_inc(w_used, 1)

            @block.scalar
            def _(act):
                def square(t):
                    if t >= 2:
                        act.wait_ge(squares, t - 1)
                    nc.scalar.activation(cbuf[:, t % 2, :], k.x[:, t, :], ACT.Square,
                                         accum_out=ssq[:, t:t + 1]).then_inc(squares, 1)

                square(0)
                square(1)
                for t in range(T):
                    act.wait_ge(turned, t + 1)
                    nc.scalar.activation(k.hT[:, 0:4, t * P:(t + 1) * P],
                                         k.ps[:, 2 * (t % 2), :].rearrange("p (c s) -> p c s", c=4), ACT.Copy).then_inc(ht_act, 1)
                    if t + 2 < T:
                        square(t + 2)
                q = 0
                act.wait_ge(squares, T)

                def silu(j):
                    if j == 0:
                        act.wait_ge(params_in, 16 * PARAMS)
                    act.wait_ge(conv_done, j + 1)
                    nc.scalar.activation(k.xbcT[:, j, :], k.xbcT[:, j, :], ACT.Silu, bias=k.cb[:, j:j + 1]).then_inc(silu_done, 1)

                for kind, j0, _ in PAIRS:
                    for j in range(j0, j0 + 2):
                        if kind == "xbc" and j >= 2:
                            act.wait_ge(conv_done, j - 1)
                        for n in range(2):
                            cols = slice(n * HALF, (n + 1) * HALF)
                            src = k.ps[:, 4 + q % 4, :]
                            q += 1
                            if kind in ("val", "bgate"):
                                continue
                            act.wait_ge(proj_ready, q)
                            if kind == "xbc":
                                ins = nc.scalar.activation(raw[:, j % 2, 3 + n * HALF:3 + (n + 1) * HALF], src, ACT.Copy)
                            elif kind == "cgate":
                                ins = nc.scalar.activation(cbuf[:, j, cols], src, ACT.Copy)
                            else:
                                dst, scale = (k.QT, HD ** -0.5) if kind == "q" else (k.KT, 1.0)
                                nc.scalar.activation(dst[0:HD, 2 * j, cols], src[0:HD, :], ACT.Copy, scale=scale)
                                ins = nc.scalar.activation(dst[0:HD, 2 * j + 1, cols], src[HD:P, :], ACT.Copy, scale=scale)
                            ins.then_inc(act_took, 1)
                    if kind == "xbc" and j0 == 2 or kind == "cgate":
                        silu(0 if kind == "xbc" else 2)
                        silu(1 if kind == "xbc" else 3)
                act.wait_ge(a_done, 1)
                for kind, _, n in GROUPS:
                    for t in range(T):
                        src = k.ps[:, 4 + q % 4, 0:n]
                        q += 1
                        act.wait_ge(proj_ready, q)
                        if kind == "z":
                            ins = nc.scalar.activation(k.z[:, t, :], src, ACT.Silu)
                        elif kind == "vf":
                            ins = nc.scalar.activation(k.vf[:, t, :], src, ACT.Copy)
                        elif kind == "dtq":
                            ins = nc.scalar.activation(k.low[:, t, 0:n], src, ACT.Copy)
                        else:
                            ins = nc.scalar.activation(k.low[:, t, WMAX:WMAX + n], src, ACT.Copy)
                        ins.then_inc(act_took, 1)

            @block.vector
            def _(dve):
                dve.wait_ge(gain_in, 16)
                for t in range(T):
                    dve.wait_ge(rstd_ready, t + 1)
                    if t >= 2:
                        dve.wait_ge(turned, t - 1)
                    nc.vector.scalar_tensor_tensor(hn[:, t % 2, :], k.x[:, t, :], ssq[:, t:t + 1], k.gain[:],
                                                   ALU.mult, ALU.mult).then_inc(h_ready, 1)
                    if t >= 1:
                        dve.wait_ge(turned, t)
                        nc.vector.tensor_copy(k.hT[:, 4:8, (t - 1) * P:t * P],
                                              k.ps[:, 2 * ((t - 1) % 2) + 1, :].rearrange("p (c s) -> p c s", c=4)).then_inc(ht_dve, 1)
                t = T - 1
                dve.wait_ge(turned, T)
                nc.vector.memset(raw[:, :, 0:3], 0.0)
                nc.vector.memset(upad[:, :, 0:2], 0.0)
                nc.vector.tensor_copy(k.hT[:, 4:8, t * P:(t + 1) * P],
                                      k.ps[:, 2 * (t % 2) + 1, :].rearrange("p (c s) -> p c s", c=4)).then_inc(ht_dve, 1)
                link = linker(dve, conv_step)
                dve.wait_ge(ht_dve, T)
                dve.wait_ge(params_in, 16 * PARAMS)
                for j in range(4):
                    dve.wait_ge(act_took, 2 * (j + 1))
                    acc = k.xbcT[:, j, :]
                    link(nc.vector.tensor_scalar(acc, raw[:, j % 2, 3:3 + S], k.cw[:, j, 3:4], None, ALU.mult))
                    for tap in (2, 1):
                        link(nc.vector.scalar_tensor_tensor(acc, raw[:, j % 2, tap:tap + S], k.cw[:, j, tap:tap + 1], acc,
                                                            ALU.mult, ALU.add))
                    nc.vector.scalar_tensor_tensor(acc, raw[:, j % 2, 0:S], k.cw[:, j, 0:1], acc,
                                                   ALU.mult, ALU.add).then_inc(conv_done, 1)
                q = 12
                for j in range(2):
                    dve.wait_ge(act_took, 12)
                    for n in range(2):
                        dve.wait_ge(proj_ready, q + 1)
                        ins = nc.vector.tensor_tensor(upad[:, j, 2 + n * HALF:2 + (n + 1) * HALF], k.ps[:, 4 + q % 4, :],
                                                cbuf[:, j, n * HALF:(n + 1) * HALF], ALU.mult)
                        ins.then_inc(dve_took, 1)
                        q += 1
                    dve.wait_ge(dve_took, q - 12)
                    acc = cbuf[:, j, :]
                    link(nc.vector.tensor_scalar(acc, upad[:, j, 2:2 + S], k.ca[:, j, 2:3], None, ALU.mult))
                    for tap in (1, 0):
                        link(nc.vector.scalar_tensor_tensor(acc, upad[:, j, tap:tap + S], k.ca[:, j, tap:tap + 1], acc,
                                                            ALU.mult, ALU.add))
                for j in range(2):
                    for n in range(2):
                        dve.wait_ge(proj_ready, q + 1)
                        cols = slice(n * HALF, (n + 1) * HALF)
                        nc.vector.tensor_tensor(k.yA[:, j, cols], k.ps[:, 4 + q % 4, :], cbuf[:, j, cols],
                                                ALU.mult).then_inc(dve_took, 1)
                        q += 1
                dve.wait_ge(dve_took, 8)
                dve.sem_inc(a_done, 1)
                dve.wait_ge(silu_done, 4)


def prepare(nc, k):
    with Stage(nc) as st:
        step, exp_in, exp_out = st.sem("gate_step"), st.sem("exp_in"), st.sem("exp_out")
        gates_ready, sums_ready, cum_ready = st.sem("gates_ready"), st.sem("sums_ready"), st.sem("cum_ready")
        rows_turned, rows_ready, rows_in, ones_set = (st.sem("rows_turned"), st.sem("rows_ready"), st.sem("rows_in"),
                                                      st.sem("ones_set"))
        decays_done = st.sem("decays_done")
        N8 = 2 * HEADS
        x8, mx, e8, t8, r8, z8, zz, pl = (st.sb(f"gate{i}", [P, T, N8]) for i in range(8))
        aneg = st.sb("aneg", [P, HEADS])
        la = st.sb("log_forget", [P, T, HEADS])
        cum = st.sb("cum", [P, T, HEADS])
        rows = st.sb("cum_rows", [HEADS, 2, S])
        with nc.Block() as block:
            @block.gpsimd
            def _(pool):
                nc.gpsimd.memset(k.QT[HD:HD + 2, :, :], 1.0).then_inc(ones_set, 1)
                nc.gpsimd.memset(k.KT[HD:HD + 2, :, :], 1.0).then_inc(ones_set, 1)

            @block.sync
            def _(sp):
                sp.wait_ge(ones_set, 2)
                sp.wait_ge(rows_ready, 4)
                for h in range(HEADS):
                    sp.dma_start(k.QT[HD:HD + 1, h, :], rows[h:h + 1, 0, :]).then_inc(rows_in, 16)
                    sp.dma_start(k.KT[HD + 1:HD + 2, h, :], rows[h:h + 1, 1, :]).then_inc(rows_in, 16)
                sp.wait_ge(rows_in, 16 * 2 * HEADS)

            @block.scalar
            def _(act):
                act.wait_ge(exp_in, 1)
                nc.scalar.activation(e8[:], t8[:], ACT.Exp, scale=-1.0).then_inc(exp_out, 1)
                nc.scalar.activation(aneg[:], k.alog[:], ACT.Exp).then_inc(exp_out, 1)
                act.wait_ge(sums_ready, 1)
                nc.scalar.activation(k.decay[:, 0:2], k.ps[:, 0, 32:96].rearrange("p (i n) -> p i n", i=2), ACT.Exp)
                nc.scalar.activation(k.carry[0:64, :, :], k.ps[0:64, 0, 96:128].rearrange("p (c h) -> p c h", h=HEADS)[:, :, 0:2], ACT.Exp)
                nc.scalar.activation(k.carry[64:P, :, :], k.ps[64:P, 0, 96:128].rearrange("p (c h) -> p c h", h=HEADS)[:, :, 2:4],
                                     ACT.Exp).then_inc(decays_done, 1)
                act.wait_ge(decays_done, 1)

            @block.tensor
            def _(pe):
                pe.wait_ge(gates_ready, 2)
                flat = la[:].rearrange("p t h -> p (t h)")
                adec = k.adec[:].rearrange("p t h -> p (t h)")
                nc.tensor.matmul(k.ps[:, 1, 0:32], k.c("le"), flat, start=True, stop=True)
                nc.tensor.matmul(k.ps[:, 1, 32:64], k.c("ones"), flat, start=True, stop=True)
                nc.tensor.matmul(k.ps[:, 0, 32:64], k.c("le"), adec, start=True, stop=True)
                nc.tensor.matmul(k.ps[:, 0, 64:96], k.c("gt"), adec, start=True, stop=True)
                nc.tensor.matmul(k.ps[:, 0, 96:128], k.c("ones"), adec, start=True, stop=True).then_inc(sums_ready, 1)
                pe.wait_ge(cum_ready, 1)
                for t in range(T):
                    last = nc.tensor.transpose(k.ps[0:HEADS, 2 + t // 4, (t % 4) * P:(t % 4 + 1) * P], cum[:, t, :], k.c("ident"))
                last.then_inc(rows_turned, 1)

            @block.vector
            def _(dve):
                link = linker(dve, step)
                link(nc.vector.tensor_copy(x8[:, :, 0:HEADS], k.vf[:, :, GW:GW + HEADS]))
                link(nc.vector.tensor_copy(x8[:, :, HEADS:], k.low[:, :, 0:HEADS]))
                link(nc.vector.tensor_tensor(x8[:], x8[:], bc(k.bias8[:].unsqueeze(1), P, T, N8), ALU.add))
                link(nc.vector.tensor_tensor(x8[:], x8[:], bc(k.c("sign").unsqueeze(1), P, T, N8), ALU.mult))
                link(nc.vector.tensor_scalar(mx[:], x8[:], 0.0, None, ALU.max))
                nc.vector.scalar_tensor_tensor(t8[:], x8[:], -1.0, x8[:], ALU.mult, ALU.max).then_inc(exp_in, 1)
                dve.wait_ge(exp_out, 2)
                link(nc.vector.tensor_scalar(r8[:], e8[:], 2.0, None, ALU.add))
                link(nc.vector.reciprocal(r8[:], r8[:]))
                link(nc.vector.tensor_tensor(z8[:], e8[:], r8[:], ALU.mult))
                link(nc.vector.tensor_tensor(zz[:], z8[:], z8[:], ALU.mult))
                link(nc.vector.tensor_scalar(pl[:], zz[:], 1.0 / 17, 1.0 / 15, ALU.mult, ALU.add))
                for n in (13, 11, 9, 7, 5, 3, 1):
                    link(nc.vector.tensor_tensor(pl[:], pl[:], zz[:], ALU.mult))
                    link(nc.vector.tensor_scalar(pl[:], pl[:], 1.0 / n, None, ALU.add))
                link(nc.vector.tensor_tensor(pl[:], pl[:], z8[:], ALU.mult))
                link(nc.vector.scalar_tensor_tensor(x8[:], pl[:], 2.0, mx[:], ALU.mult, ALU.add))
                nc.vector.tensor_scalar(la[:], x8[:, :, 0:HEADS], -1.0, None, ALU.mult).then_inc(gates_ready, 1)
                link(nc.vector.tensor_copy(k.dt[:], x8[:, :, HEADS:]))
                nc.vector.scalar_tensor_tensor(k.adec[:], k.dt[:], -1.0, bc(aneg[:].unsqueeze(1), P, T, HEADS),
                                               ALU.mult, ALU.mult).then_inc(gates_ready, 1)
                dve.wait_ge(sums_ready, 1)
                tot = k.ps[:, 1, 32:64].rearrange("p (t h) -> p t h", h=HEADS)
                link(nc.vector.memset(t8[:, 0, 0:HEADS], 0.0))
                for t in range(1, T):
                    link(nc.vector.tensor_tensor(t8[:, t, 0:HEADS], t8[:, t - 1, 0:HEADS], tot[:, t - 1, :], ALU.add))
                nc.vector.tensor_tensor(cum[:], k.ps[:, 1, 0:32].rearrange("p (t h) -> p t h", h=HEADS), t8[:, :, 0:HEADS],
                                        ALU.add).then_inc(cum_ready, 1)
                dve.wait_ge(rows_turned, 1)
                for n in range(2):
                    src = k.ps[0:HEADS, 2 + n, :]
                    nc.vector.tensor_copy(rows[:, 0, n * HALF:(n + 1) * HALF], src).then_inc(rows_ready, 1)
                    nc.vector.tensor_scalar(rows[:, 1, n * HALF:(n + 1) * HALF], src, -1.0, None, ALU.mult).then_inc(rows_ready, 1)


def prepare_mla(nc, k):
    with Stage(nc) as st:
        step, sq_done, normed = st.sem("norm_step"), st.sem("sq_done"), st.sem("normed")
        c_turned, c_ready, up_ready, qk_ready = st.sem("c_turned"), st.sem("c_ready"), st.sem("up_ready"), st.sem("qk_ready")
        v_took, qk_turned, q_took, k_took = st.sem("v_took"), st.sem("qk_turned"), st.sem("q_took"), st.sem("k_took")
        rstd_step, rstd_ready = st.sem("rstd_step"), st.sem("rstd_ready")
        ssq = st.sb("ssq2", [P, 2, T])
        junk = st.sb("junk", [P, 2, GW + P])
        cn = st.sb("cn", [P, 2, GW + P])
        cT = st.sb("cT", [P, 2, 3, P])
        qn = st.sb("qn", [P, 2, HEADS, MLA_D])
        kn = st.sb("kn", [P, 2, HEADS, MLA_D])
        rot = st.sb("rot", [P, 2, HEADS, 2, HR])
        krot = st.sb("krot", [P, 2, T, 2, HR])
        kr = st.sb("kr", [P, T, 2, HR])
        cq = k.low[:, :, HEADS:WMAX]
        ckv = k.low[:, :, WMAX:WMAX + P]
        ckr = k.low[:, :, WMAX + P:WMAX + P + ROPE].rearrange("p t (i r) -> p t i r", i=2)
        cos, sin = k.trig[:, 0], k.trig[:, 1]

        with nc.Block() as block:
            @block.gpsimd
            def _(pool):
                link = linker(pool, rstd_step)
                pool.wait_ge(sq_done, T)
                rstd(nc, k, link, ssq[:, 0], GW).then_inc(rstd_ready, 1)
                rstd(nc, k, link, ssq[:, 1], P).then_inc(rstd_ready, 1)

            @block.scalar
            def _(act):
                for t in range(T):
                    if t >= 2:
                        act.wait_ge(sq_done, t - 1)
                    nc.scalar.activation(junk[:, t % 2, 0:GW], cq[:, t, :], ACT.Square, accum_out=ssq[:, 0, t:t + 1])
                    nc.scalar.activation(junk[:, t % 2, GW:], ckv[:, t, :], ACT.Square, accum_out=ssq[:, 1, t:t + 1]).then_inc(sq_done, 1)
                for t in range(T + 1):
                    if t < T:
                        act.wait_ge(c_turned, t + 1)
                        nc.scalar.activation(cT[:, t % 2], k.ps[:, t % 2, 0:3 * P].rearrange("p (c s) -> p c s", c=3),
                                             ACT.Copy).then_inc(c_ready, 1)
                        act.wait_ge(up_ready, t + 1)
                        kv = k.ps[:, 4 + t % 2, :].rearrange("p (h i d) -> p h i d", h=HEADS, i=2)
                        nc.scalar.activation(k.vm[:, t].rearrange("p (h d) -> p h d", h=HEADS), kv[:, :, 1, :], ACT.Copy)
                        if t >= 2:
                            act.wait_ge(qk_turned, t - 1)
                        nc.scalar.activation(kn[:, t % 2, :, 0:HD], kv[:, :, 0, :], ACT.Copy).then_inc(v_took, 1)
                    if t >= 1:
                        u = t - 1
                        act.wait_ge(qk_turned, u + 1)
                        nc.scalar.activation(k.QT[0:MLA_D, :, u * P:(u + 1) * P],
                                             k.ps[0:MLA_D, 6, :].rearrange("p (h s) -> p h s", h=HEADS), ACT.Copy,
                                             scale=MLA_D ** -0.5).then_inc(q_took, 1)

            @block.tensor
            def _(pe):
                def up(t):
                    pe.wait_ge(normed, t + 1)
                    for c in range(3):
                        last = nc.tensor.transpose(k.ps[:, t % 2, c * P:(c + 1) * P], cn[:, t % 2, c * P:(c + 1) * P], k.c("ident"))
                    last.then_inc(c_turned, 1)
                    pe.wait_ge(c_ready, t + 1)
                    if t >= 2:
                        pe.wait_ge(qk_ready, t - 1)
                        pe.wait_ge(v_took, t - 1)
                    for c in range(2):
                        nc.tensor.matmul(k.ps[:, 2 + t % 2, 0:HEADS * MLA_D], cT[:, t % 2, c, :], k.wuq[:, c, :],
                                         start=(c == 0), stop=(c == 1))
                    nc.tensor.matmul(k.ps[:, 4 + t % 2, :], cT[:, t % 2, 2, :], k.wukv[:], start=True, stop=True).then_inc(up_ready, 1)

                def turn(t):
                    pe.wait_ge(qk_ready, t + 1)
                    pe.wait_ge(v_took, t + 1)
                    if t >= 1:
                        pe.wait_ge(q_took, t)
                        pe.wait_ge(k_took, t)
                    for h in range(HEADS):
                        nc.tensor.transpose(k.ps[0:MLA_D, 6, h * P:(h + 1) * P], qn[:, t % 2, h, :], k.c("ident"))
                        last = nc.tensor.transpose(k.ps[0:MLA_D, 7, h * P:(h + 1) * P], kn[:, t % 2, h, :], k.c("ident"))
                    last.then_inc(qk_turned, 1)

                for t in range(T):
                    up(t)
                    if t >= 1:
                        turn(t - 1)
                turn(T - 1)

            @block.vector
            def _(dve):
                link = linker(dve, step)
                bcos = bc(cos.unsqueeze(2), P, T, 2, HR)
                bsin = bc(sin.unsqueeze(2), P, T, 2, HR)
                link(nc.vector.tensor_tensor(krot[:, 0], ckr, bcos, ALU.mult))
                link(nc.vector.tensor_tensor(krot[:, 1], ckr, bsin, ALU.mult))
                link(nc.vector.tensor_tensor(kr[:, :, 0, :], krot[:, 0, :, 0, :], krot[:, 1, :, 1, :], ALU.subtract))
                link(nc.vector.tensor_tensor(kr[:, :, 1, :], krot[:, 0, :, 1, :], krot[:, 1, :, 0, :], ALU.add))
                dve.wait_ge(rstd_ready, 2)

                def norm(t):
                    if t >= 2:
                        dve.wait_ge(c_turned, t - 1)
                    nc.vector.scalar_tensor_tensor(cn[:, t % 2, 0:GW], cq[:, t, :], ssq[:, 0, t:t + 1], k.qng[:], ALU.mult, ALU.mult)
                    nc.vector.scalar_tensor_tensor(cn[:, t % 2, GW:], ckv[:, t, :], ssq[:, 1, t:t + 1], k.kvng[:],
                                                   ALU.mult, ALU.mult).then_inc(normed, 1)

                def rotate(t):
                    dve.wait_ge(up_ready, t + 1)
                    if t >= 1:
                        dve.wait_ge(qk_ready, t)
                    if t >= 2:
                        dve.wait_ge(qk_turned, t - 1)
                    q = k.ps[:, 2 + t % 2, 0:HEADS * MLA_D].rearrange("p (h d) -> p h d", h=HEADS)
                    qr = q[:, :, HD:].rearrange("p h (i r) -> p h i r", i=2)
                    nc.vector.tensor_copy(qn[:, t % 2, :, 0:HD], q[:, :, 0:HD])
                    c4 = bc(cos[:, t, :].unsqueeze(1).unsqueeze(1), P, HEADS, 2, HR)
                    s4 = bc(sin[:, t, :].unsqueeze(1).unsqueeze(1), P, HEADS, 2, HR)
                    nc.vector.tensor_tensor(rot[:, 0], qr, c4, ALU.mult)
                    link(nc.vector.tensor_tensor(rot[:, 1], qr, s4, ALU.mult))
                    nc.vector.tensor_tensor(qn[:, t % 2, :, HD:HD + HR], rot[:, 0, :, 0, :], rot[:, 1, :, 1, :], ALU.subtract)
                    nc.vector.tensor_tensor(qn[:, t % 2, :, HD + HR:], rot[:, 0, :, 1, :], rot[:, 1, :, 0, :], ALU.add)
                    nc.vector.tensor_copy(kn[:, t % 2, :, HD:],
                                          bc(kr[:, t].rearrange("p i r -> p (i r)").unsqueeze(1), P, HEADS, ROPE)).then_inc(qk_ready, 1)

                def take(t):
                    dve.wait_ge(qk_turned, t + 1)
                    nc.vector.tensor_copy(k.KT[0:MLA_D, :, t * P:(t + 1) * P],
                                          k.ps[0:MLA_D, 7, :].rearrange("p (h s) -> p h s", h=HEADS)).then_inc(k_took, 1)

                norm(0)
                for t in range(T):
                    if t + 1 < T:
                        norm(t + 1)
                    rotate(t)
                    if t >= 1:
                        take(t - 1)
                take(T - 1)
                dve.wait_ge(q_took, T)


def attend(nc, k, who, K, v, mask, chunk0):
    units = [(i, h) for i in range(T) for h in range(HEADS)]
    N = len(units)
    with Stage(nc) as st:
        scores, maxed, exped = st.sem("scores"), st.sem("maxed"), st.sem("exped")
        p_turned, pt_act, pt_dve = st.sem("p_turned"), st.sem("pt_act"), st.sem("pt_dve")
        out_ready, inv, out_took, y_turned, y_took = (st.sem("out_ready"), st.sem("inv"), st.sem("out_took"),
                                                      st.sem("y_turned"), st.sem("y_took"))
        probs = st.sb(f"probs_{who}", [P, 2, S])
        pT = st.sb(f"pT_{who}", [P, 2, T, P])
        nmax = st.sb(f"nmax_{who}", [P, 2])
        total = st.sb(f"total_{who}", [P, 4])
        rinv = st.sb(f"rinv_{who}", [P, 2])
        y = st.sb(f"y_nat_{who}", [P, 2, GW])

        groups = []
        for u, (i, h) in enumerate(units):
            for b0 in range(0, i + 1, 4):
                groups.append((u, b0, min(4, i + 1 - b0)))
        before = lambda u: sum(g[0] < u for g in groups)

        def emptied(eng, n):
            if (n + 1) // 2:
                eng.wait_ge(pt_act, (n + 1) // 2)
            if n // 2:
                eng.wait_ge(pt_dve, n // 2)

        def empty(eng, unit, u, par):
            for g in range(before(u), before(u + 1)):
                if g % 2 != par:
                    continue
                _, b0, m = groups[g]
                eng.wait_ge(p_turned, g + 1)
                if u >= 2:
                    eng.wait_ge(out_ready, u - 1)
                src = k.ps[:, 4 + g % 2, 0:m * P].rearrange("p (b s) -> p b s", b=m)
                dst = pT[:, u % 2, b0:b0 + m, :]
                if par == 0:
                    unit.activation(dst, src, ACT.Copy).then_inc(pt_act, 1)
                else:
                    unit.tensor_copy(dst, src).then_inc(pt_dve, 1)

        with nc.Block() as block:
            @block.tensor
            def _(pe):
                def score(u):
                    i, h = units[u]
                    if u >= 2:
                        pe.wait_ge(exped, u - 1)
                    for n in range(0, i + 1, 4):
                        m = min(4, i + 1 - n)
                        bank = k.ps[:, 2 * (u % 2) + n // 4, :]
                        last = nc.tensor.matmul(bank[:, 0:m * P], k.QT[0:K, h, i * P:(i + 1) * P], k.KT[0:K, h, n * P:(n + m) * P],
                                                start=True, stop=True)
                    last = nc.tensor.matmul(bank[:, (m - 1) * P:m * P], k.ident_b[:], mask[:], start=False, stop=True,
                                            skip_group_check=True)
                    last.then_inc(scores, 1)

                def turn(u):
                    pe.wait_ge(exped, u + 1)
                    for g in range(before(u), before(u + 1)):
                        _, b0, m = groups[g]
                        if g >= 2:
                            emptied(pe, g - 1)
                        for b in range(m):
                            last = nc.tensor.transpose(k.ps[:, 4 + g % 2, b * P:(b + 1) * P],
                                                       probs[:, u % 2, (b0 + b) * P:(b0 + b + 1) * P], k.c("ident"))
                        last.then_inc(p_turned, 1)

                def weigh(u):
                    i, h = units[u]
                    emptied(pe, before(u + 1))
                    if u >= 2:
                        pe.wait_ge(out_took, u - 1)
                    if u > HEADS and h == 1:
                        pe.wait_ge(y_took, i)
                    for b in range(i + 1):
                        last = nc.tensor.matmul(k.ps[:, 6 + u % 2, 0:HD], pT[:, u % 2, b, :],
                                                v(b, h), start=(b == 0), stop=(b == i))
                    last.then_inc(out_ready, 1)

                def turn_y(i):
                    pe.wait_ge(out_took, HEADS * (i + 1))
                    if i >= 1:
                        pe.wait_ge(y_took, i)
                    for c in range(2):
                        last = nc.tensor.transpose(k.ps[:, 7, c * P:(c + 1) * P], y[:, i % 2, c * P:(c + 1) * P], k.c("ident"))
                    last.then_inc(y_turned, 1)

                score(0)
                for u in range(N):
                    if u + 1 < N:
                        score(u + 1)
                    turn(u)
                    if u >= 1:
                        weigh(u - 1)
                    if u >= 2 and (u - 2) % HEADS == HEADS - 1:
                        turn_y((u - 2) // HEADS)
                weigh(N - 1)
                turn_y(T - 1)

            @block.scalar
            def _(act):
                for u in range(N + 1):
                    if u < N:
                        i, h = units[u]
                        act.wait_ge(maxed, u + 1)
                        if u >= 2:
                            act.wait_ge(p_turned, before(u - 1))
                        nk = (i + 1) * P
                        nc.scalar.activation(probs[:, u % 2, 0:nk], k.ps[:, 2 * (u % 2):2 * (u % 2) + 2, :].rearrange("p b n -> p (b n)")[:, 0:nk],
                                             ACT.Exp, bias=nmax[:, u % 2:u % 2 + 1], accum_out=total[:, u % 4:u % 4 + 1]).then_inc(exped, 1)
                    if u >= 1:
                        empty(act, nc.scalar, u - 1, 0)

            @block.vector
            def _(dve):
                def finish(u):
                    i, h = units[u]
                    nc.vector.reciprocal(rinv[:, u % 2:u % 2 + 1], total[:, u % 4:u % 4 + 1]).then_inc(inv, 1)
                    dve.wait_ge(out_ready, u + 1)
                    dve.wait_ge(inv, u + 1)
                    if i >= 2 and h == 0:
                        dve.wait_ge(y_turned, i - 1)
                    nc.vector.tensor_scalar(y[:, i % 2, h * HD:(h + 1) * HD], k.ps[:, 6 + u % 2, 0:HD],
                                            rinv[:, u % 2:u % 2 + 1], None, ALU.mult).then_inc(out_took, 1)

                def take_y(i):
                    dve.wait_ge(y_turned, i + 1)
                    nc.vector.tensor_copy(k.yT[:, chunk0:chunk0 + 2, i * P:(i + 1) * P],
                                          k.ps[:, 7, 0:2 * P].rearrange("p (c s) -> p c s", c=2)).then_inc(y_took, 1)

                for u in range(N + 2):
                    if u < N:
                        i, h = units[u]
                        nk = (i + 1) * P
                        dve.wait_ge(scores, u + 1)
                        if u >= 2:
                            dve.wait_ge(exped, u - 1)
                        nc.vector.tensor_reduce(nmax[:, u % 2:u % 2 + 1],
                                                k.ps[:, 2 * (u % 2):2 * (u % 2) + 2, :].rearrange("p b n -> p (b n)")[:, 0:nk],
                                                AX, ALU.max, negate=True).then_inc(maxed, 1)
                    if 1 <= u <= N:
                        empty(dve, nc.vector, u - 1, 1)
                    if u >= 2:
                        finish(u - 2)
                    if u >= 3 and (u - 3) % HEADS == HEADS - 1:
                        take_y((u - 3) // HEADS)
                take_y(T - 1)


def ssd(nc, k):
    with Stage(nc) as st:
        bx_turned, b_took, xs_ready = st.sem("bx_turned"), st.sem("b_took"), st.sem("xs_ready")
        cuts_ready, gd_ready, exped, m_ready = st.sem("cuts_ready"), st.sem("gd_ready"), st.sem("exped"), st.sem("m_ready")
        y_ready, state_ready, step, y_took = st.sem("y_ready"), st.sem("state_ready"), st.sem("ssd_step"), st.sem("y_took")
        yn_ready, yn_turned, yt_took, zeroed = st.sem("yn_ready"), st.sem("yn_turned"), st.sem("yt_took"), st.sem("zeroed")
        cleared, apart = st.sem("cleared"), st.sem("apart")
        squared, rstd_step, rstd_ready = st.sem("squared"), st.sem("rstd_step"), st.sem("rstd_ready")
        Bn = st.sb("Bn", [P, 2, P])
        xdt = st.sb("xdt", [P, 2, HEADS, HD])
        xds = st.sb("xds", [P, 2, HEADS, HD])
        skip = st.sb("skip", [P, 2, HEADS, HD])
        cuts = st.sb("cuts", [P, 2, HEADS, P])
        eD = st.sb("eD", [P, 2, HEADS, P])
        M = st.sb("M", [P, 2, HEADS, P])
        Cg = st.sb("Cg", [P, 2, 2, P])
        prev = st.sb("prev", [P, 2, HEADS, HD])
        yc = st.sb("yc", [P, 3, HEADS, HD])
        ssq = st.sb("ssq3", [P, T])
        junk = st.sb("junk3", [P, GW])
        gt4 = bc(k.c("gt").unsqueeze(1), P, HEADS, P)

        def col(ap):
            return bc(ap.unsqueeze(2), P, HEADS, HD)

        with nc.Block() as block:
            @block.gpsimd
            def _(pool):
                link = linker(pool, rstd_step)
                nc.gpsimd.memset(Cg[:], 0.0).then_inc(cleared, 1)
                pool.wait_ge(cleared, 1)
                for c in range(T + 2):
                    if 2 <= c < T:
                        pool.wait_ge(gd_ready, c - 1)
                    if 3 <= c < T:
                        pool.wait_ge(rstd_ready, c - 2)
                    if c < T:
                        for g in range(2):
                            r = slice(g * STATE, (g + 1) * STATE)
                            nc.gpsimd.tensor_copy(Cg[r, c % 2, g, :], k.xbcT[r, 3, c * P:(c + 1) * P]).then_inc(apart, 1)
                    if c >= 2:
                        pool.wait_ge(apart, 2 * min(c + 1, T))
                        pool.wait_ge(squared, c - 1)
                        rstd(nc, k, link, ssq[:, c - 2:c - 1], GW).then_inc(rstd_ready, 1)

            @block.tensor
            def _(pe):
                def front(c):
                    s = slice(c * P, (c + 1) * P)
                    if c >= 1:
                        pe.wait_ge(b_took, c)
                        pe.wait_ge(xs_ready, c)
                    for bank, n, j in ((0, 0, 0), (0, 1, 1), (1, 0, 2)):
                        last = nc.tensor.transpose(k.ps[:, bank, n * P:(n + 1) * P], k.xbcT[:, j, s], k.c("ident"))
                    last.then_inc(bx_turned, 1)
                    pe.wait_ge(cuts_ready, c + 1)
                    if c >= 1:
                        pe.wait_ge(m_ready, c)
                    pe.wait_ge(apart, 2 * (c + 1))
                    nc.tensor.matmul(k.ps[:, 2, 0:2 * P], k.xbcT[:, 2, s], Cg[:, c % 2].rearrange("p g s -> p (g s)"),
                                     start=True, stop=True)
                    for h in range(HEADS):
                        nc.tensor.matmul(k.ps[:, 3 + c % 2, h * P:(h + 1) * P], cuts[:, c % 2, h, :], k.c("le"),
                                         start=(h == 0), stop=False, skip_group_check=True)
                    nc.tensor.matmul(k.ps[:, 3 + c % 2, :], k.ident_b[:], k.mask_ssd[:],
                                     start=False, stop=True, skip_group_check=True).then_inc(gd_ready, 1)

                def back(c):
                    s = slice(c * P, (c + 1) * P)
                    pe.wait_ge(m_ready, c + 1)
                    if c == 0:
                        pe.wait_ge(zeroed, 1)
                    else:
                        pe.wait_ge(y_took, c)
                    for h in range(HEADS):
                        nc.tensor.matmul(k.ps[:, 5, h * HD:(h + 1) * HD], M[:, c % 2, h, :], xdt[:, c % 2, h, :], start=True, stop=True)
                    nc.tensor.matmul(k.ps[:, 5, GW:], k.xbcT[:, 3, s], prev[:, c % 2].rearrange("p h d -> p (h d)"), start=True, stop=True)
                    last = nc.tensor.matmul(k.ps[:, 6, 0:GW], Bn[:, c % 2], xds[:, c % 2].rearrange("p h d -> p (h d)"), start=True, stop=True)
                    last.then_inc(y_ready, 1)

                def turn_y(c):
                    pe.wait_ge(yn_ready, c + 1)
                    if c >= 1:
                        pe.wait_ge(yt_took, c)
                    for j in range(2):
                        last = nc.tensor.transpose(k.ps[:, 7, j * P:(j + 1) * P],
                                                   yc[:, c % 3].rearrange("p h d -> p (h d)")[:, j * P:(j + 1) * P], k.c("ident"))
                    last.then_inc(yn_turned, 1)

                front(0)
                for c in range(T):
                    if c + 1 < T:
                        front(c + 1)
                    back(c)
                    if c >= 2:
                        turn_y(c - 2)
                turn_y(T - 2)
                turn_y(T - 1)

            @block.scalar
            def _(act):
                def take_yt(c):
                    act.wait_ge(yn_turned, c + 1)
                    nc.scalar.activation(k.yT[:, 2:4, c * P:(c + 1) * P], k.ps[:, 7, 0:2 * P].rearrange("p (j s) -> p j s", j=2),
                                         ACT.Copy).then_inc(yt_took, 1)

                for c in range(T):
                    act.wait_ge(bx_turned, c + 1)
                    if c >= 2:
                        act.wait_ge(y_ready, c - 1)
                    nc.scalar.activation(Bn[:, c % 2, :], k.ps[:, 1, 0:P], ACT.Copy).then_inc(b_took, 1)
                    act.wait_ge(gd_ready, c + 1)
                    if c >= 2:
                        act.wait_ge(m_ready, c - 1)
                    nc.scalar.activation(eD[:, c % 2], k.ps[:, 3 + c % 2, :].rearrange("p (h s) -> p h s", h=HEADS), ACT.Exp).then_inc(exped, 1)
                    if c >= 3:
                        take_yt(c - 3)
                for c in range(T - 3, T):
                    take_yt(c)

            @block.vector
            def _(dve):
                link = linker(dve, step)
                nc.vector.memset(prev[:], 0.0).then_inc(zeroed, 1)

                def front(c):
                    if c >= 2:
                        dve.wait_ge(gd_ready, c - 1)
                    nc.vector.tensor_tensor(cuts[:, c % 2], gt4, bc(k.adec[:, c, :].unsqueeze(2), P, HEADS, P), ALU.mult).then_inc(cuts_ready, 1)
                    dve.wait_ge(bx_turned, c + 1)
                    xs = k.ps[:, 0, 0:2 * P].rearrange("p (h d) -> p h d", h=HEADS)
                    if c >= 2:
                        dve.wait_ge(y_ready, c - 1)
                    link(nc.vector.tensor_tensor(xdt[:, c % 2], xs, col(k.dt[:, c, :]), ALU.mult))
                    nc.vector.tensor_tensor(xds[:, c % 2], xdt[:, c % 2], col(k.decay[:, 1, c * HEADS:(c + 1) * HEADS]), ALU.mult)
                    nc.vector.tensor_tensor(skip[:, c % 2], xs, col(k.dskip[:]), ALU.mult).then_inc(xs_ready, 1)
                    dve.wait_ge(exped, c + 1)
                    gg = k.ps[:, 2, 0:2 * P].rearrange("p (g s) -> p g s", g=2)
                    nc.vector.tensor_tensor(M[:, c % 2].rearrange("p (g j) s -> p g j s", g=2),
                                            eD[:, c % 2].rearrange("p (g j) s -> p g j s", g=2),
                                            bc(gg.unsqueeze(2), P, 2, 2, P), ALU.mult).then_inc(m_ready, 1)

                def back(c):
                    dve.wait_ge(y_ready, c + 1)
                    dve.wait_ge(zeroed, 1)
                    for h in range(HEADS):
                        r = slice(h // 2 * STATE, (h // 2 + 1) * STATE)
                        link(nc.vector.scalar_tensor_tensor(prev[r, (c + 1) % 2, h, :], prev[r, c % 2, h, :], k.carry[r, c, h % 2:h % 2 + 1],
                                                            k.ps[r, 6, h * HD:(h + 1) * HD], ALU.mult, ALU.add))
                    if c >= 3:
                        dve.wait_ge(yn_turned, c - 2)
                    yv = yc[:, c % 3]
                    link(nc.vector.tensor_tensor(yv, k.ps[:, 5, GW:].rearrange("p (h d) -> p h d", h=HEADS),
                                                 col(k.decay[:, 0, c * HEADS:(c + 1) * HEADS]), ALU.mult))
                    nc.vector.tensor_tensor(yv, yv, k.ps[:, 5, 0:GW].rearrange("p (h d) -> p h d", h=HEADS), ALU.add).then_inc(y_took, 1)
                    dve.wait_ge(y_took, c + 1)
                    link(nc.vector.tensor_tensor(yv, yv, skip[:, c % 2], ALU.add))
                    flat = yv.rearrange("p h d -> p (h d)")
                    link(nc.vector.tensor_tensor(flat, flat, k.z[:, c, :], ALU.mult))
                    if c >= 1:
                        dve.wait_ge(squared, c)
                    nc.vector.tensor_tensor_reduce(junk[:], flat, flat, 1.0, 0.0, ALU.mult, ALU.add, ssq[:, c:c + 1]).then_inc(squared, 1)

                def norm(c):
                    flat = yc[:, c % 3].rearrange("p h d -> p (h d)")
                    dve.wait_ge(rstd_ready, c + 1)
                    nc.vector.scalar_tensor_tensor(flat, flat, ssq[:, c:c + 1], k.sng[:], ALU.mult, ALU.mult).then_inc(yn_ready, 1)

                front(0)
                for c in range(T):
                    if c + 1 < T:
                        front(c + 1)
                    back(c)
                    if c >= 1:
                        norm(c - 1)
                norm(T - 1)


def join(nc, k, l):
    with Stage(nc) as st:
        w_in, gain_in = st.sem("w_out_in"), st.sem("gain_in")
        o_ready, x_ready, sq, step = st.sem("o_ready"), st.sem("x_ready"), st.sem("sq"), st.sem("join_step")
        h_ready, h_stored, turned, ht_ready, lg_ready, lg_took = (st.sem("h_ready"), st.sem("h_stored"), st.sem("turned"),
                                                         st.sem("ht_ready"), st.sem("lg_ready"), st.sem("lg_took"))
        wo = k.QK[:].rearrange("p a h s -> p (a h s)").rearrange("p (c n) -> p c n", c=KD)
        h = k.over[:, 0:2 * D].rearrange("p (b n) -> p b n", b=2)
        hT2 = k.over[:, 2 * D:4 * D].rearrange("p (b c s) -> p b c s", b=2, c=KD)
        junk = k.over[:, 4 * D:5 * D]
        rstd_ready = st.sem("rstd_ready")
        ssq = st.sb("ssq4", [P, T])

        def yT(c, t):
            src = k.yA[:, c] if c < 2 else k.yT[:, c - 2]
            return src[:, t * P:(t + 1) * P]

        with nc.Block() as block:
            @block.gpsimd
            def _(pool):
                link = linker(pool, step)
                for t in range(T):
                    pool.wait_ge(sq, t + 1)
                    rstd(nc, k, link, ssq[:, t:t + 1], D).then_inc(rstd_ready, 1)

            @block.sync
            def _(sp):
                sp.dma_start(k.gain[:], bc(k.norm_ffn[bass.ds(l, 1), :], P, D)).then_inc(gain_in, 16)
                sp.dma_start(wo, k.w_out[bass.ds(l, 1)].rearrange("a (c p) n -> p (a c) n", p=P)).then_inc(w_in, 16)
                for t in range(T):
                    sp.wait_ge(h_ready, t + 1)
                    sp.dma_start(k.d_h[t * P:(t + 1) * P, :], h[:, t % 2, :]).then_inc(h_stored, 16)
                    if t + 1 == T:
                        sp.wait_ge(h_stored, 16 * T)

            @block.tensor
            def _(pe):
                pe.wait_ge(w_in, 16)

                def router(t):
                    pe.wait_ge(h_ready, t + 1)
                    if t >= 1:
                        pe.wait_ge(ht_ready, 2 * t)
                    for c in range(KD):
                        last = nc.tensor.transpose(k.ps[:, 4 + c // 4, (c % 4) * P:(c % 4 + 1) * P], h[:, t % 2, c * P:(c + 1) * P],
                                                   k.c("ident"))
                    last.then_inc(turned, 1)
                    pe.wait_ge(ht_ready, 2 * (t + 1))
                    if t >= 1:
                        pe.wait_ge(lg_took, t)
                    for c in range(KD):
                        last = nc.tensor.matmul(k.ps[:, 6, 0:G + E], hT2[:, t % 2, c, :], k.rw[:, c, :], start=(c == 0), stop=(c == KD - 1))
                    last.then_inc(lg_ready, 1)

                for t in range(T):
                    if t >= 2:
                        pe.wait_ge(x_ready, t - 1)
                    for n in range(2):
                        for c in range(KD):
                            last = nc.tensor.matmul(k.ps[:, 2 * (t % 2) + n, :], yT(c, t), wo[:, c, n * HALF:(n + 1) * HALF],
                                                    start=(c == 0), stop=(c == KD - 1))
                    last.then_inc(o_ready, 1)
                    if t >= 1:
                        router(t - 1)
                router(T - 1)

            @block.scalar
            def _(act):
                for t in range(T):
                    act.wait_ge(x_ready, t + 1)
                    if t >= 1:
                        act.wait_ge(sq, t)
                    nc.scalar.activation(junk, k.x[:, t, :], ACT.Square, accum_out=ssq[:, t:t + 1]).then_inc(sq, 1)
                    act.wait_ge(turned, t + 1)
                    for n in range(2):
                        if t >= 2:
                            act.wait_ge(lg_ready, t - 1)
                        nc.scalar.activation(hT2[:, t % 2, 4 * n:4 * n + 4, :], k.ps[:, 4 + n, :].rearrange("p (c s) -> p c s", c=4),
                                             ACT.Copy).then_inc(ht_ready, 1)

            @block.vector
            def _(dve):
                dve.wait_ge(gain_in, 16)
                for t in range(T + 1):
                    if t < T:
                        dve.wait_ge(o_ready, t + 1)
                        nc.vector.tensor_tensor(k.x[:, t, :], k.x[:, t, :],
                                                k.ps[:, 2 * (t % 2):2 * (t % 2) + 2, :].rearrange("p b n -> p (b n)"),
                                                ALU.add).then_inc(x_ready, 1)
                    if t >= 1:
                        dve.wait_ge(lg_ready, t)
                        nc.vector.tensor_tensor(k.logits[:, t - 1, :], k.ps[:, 6, 0:G + E], k.rb[:], ALU.add).then_inc(lg_took, 1)
                    if t < T:
                        dve.wait_ge(rstd_ready, t + 1)
                        if t >= 2:
                            dve.wait_ge(h_stored, 16 * t)
                            dve.wait_ge(turned, t - 1)
                        nc.vector.scalar_tensor_tensor(h[:, t % 2, :], k.x[:, t, :], ssq[:, t:t + 1], k.gain[:],
                                                       ALU.mult, ALU.mult).then_inc(h_ready, 1)


def route(nc, k):
    with Stage(nc) as st:
        step, exp_in, exp_out, sel_ready, ranks_ready, hot_ready, rows_ready = (
            st.sem("route_step"), st.sem("exp_in"), st.sem("exp_out"), st.sem("sel_ready"), st.sem("ranks_ready"),
            st.sem("hot_ready"), st.sem("rows_ready"))
        gm, gs, gx, m1, m2, ss, e2, den = (st.sb(f"tok{i}", [P, T]) for i in range(8))
        gd, goh = st.sb("gd", [P, T, G]), st.sb("goh", [P, T, G])
        el, el2, o1, o2, t8 = (st.sb(f"exp{i}", [P, T, EG]) for i in range(5))
        big = st.sb("big", [P, T, G, EG])
        M1, M2, MM = (st.sb(f"sel{i}", [P, T, G, EG]) for i in range(3))
        R = st.sb("R", [P, T, E])
        base = st.sb("base", [P, T, E])
        cnt, nb, pe_, start = (st.sb(f"cnt{i}", [P, E]) for i in range(4))
        ni = st.sb("ni", [P, E], I32)
        pmi, pbi = st.sb("pmi", [P, T, 2], I32), st.sb("pbi", [P, T, 2], I32)
        cmp = st.sb("cmp", [P, BLK, E])
        pos = st.sb("pos", [P, T, 2])
        pm, pb = st.sb("pm", [P, T, 2]), st.sb("pb", [P, T, 2])
        hotp = st.sb("hotp", [P, T, 2, P])
        hotb = st.sb("hotb", [P, T, 2, BLK])
        be = st.sb("be", [P, BLK])
        lgG = k.logits[:, :, 0:G]
        lgE = k.logits[:, :, G:].rearrange("p t (g e) -> p t g e", g=G)

        with nc.Block() as block:
            @block.sync
            def _(sp):
                sp.wait_ge(k.spare_filled, 16)

            @block.scalar
            def _(act):
                act.wait_ge(exp_in, 1)
                nc.scalar.activation(gd[:], gd[:], ACT.Exp).then_inc(exp_out, 1)
                act.wait_ge(exp_in, 2)
                nc.scalar.activation(t8[:], t8[:], ACT.Exp).then_inc(exp_out, 1)
                act.wait_ge(exp_in, 3)
                nc.scalar.activation(e2[:], e2[:], ACT.Exp).then_inc(exp_out, 1)

            @block.tensor
            def _(pe):
                pe.wait_ge(sel_ready, 1)
                flat = MM[:].rearrange("p t g e -> p (t g e)")
                nc.tensor.matmul(k.ps[:, 0, 0:T * E], k.c("lt"), flat, start=True, stop=True)
                nc.tensor.matmul(k.ps[:, 1, 0:T * E], k.c("ones"), flat, start=True, stop=True).then_inc(ranks_ready, 1)
                pe.wait_ge(hot_ready, 1)
                n = 0
                for t in range(T):
                    for i in range(2):
                        last = nc.tensor.matmul(k.ps[:, 2, 0:BLK], hotp[:, t, i, :], hotb[:, t, i, :], start=(n == 0), stop=(n == 2 * T - 1))
                        n += 1
                last.then_inc(rows_ready, 1)

            @block.vector
            def _(dve):
                link = linker(dve, step)
                V = nc.vector

                def b3(a, n):
                    return bc(a.unsqueeze(2), P, T, n)

                def pick(dst, val, best, rank, n, tmp):
                    link(V.tensor_tensor(tmp, val, b3(best, n), ALU.is_equal))
                    link(V.tensor_tensor(tmp, tmp, bc(rank.unsqueeze(1), P, T, n), ALU.mult))
                    link(V.tensor_reduce(gx[:], tmp, AX, ALU.max))
                    link(V.tensor_tensor(dst, tmp, b3(gx[:], n), ALU.is_equal))

                link(V.tensor_reduce(gm[:], lgG, AX, ALU.max))
                pick(goh[:], lgG, gm[:], k.c("rank4"), G, gd[:])
                V.tensor_tensor(gd[:], lgG, b3(gm[:], G), ALU.subtract).then_inc(exp_in, 1)
                link(V.tensor_tensor(big[:], lgE, bc(goh[:].unsqueeze(3), P, T, G, EG), ALU.mult))
                link(V.tensor_reduce(el[:], big[:].rearrange("p t g e -> p t e g"), AX, ALU.add))
                link(V.tensor_reduce(m1[:], el[:], AX, ALU.max))
                pick(o1[:], el[:], m1[:], k.c("rank8"), EG, t8[:])
                link(V.scalar_tensor_tensor(el2[:], o1[:], NEG, el[:], ALU.mult, ALU.add))
                link(V.tensor_reduce(m2[:], el2[:], AX, ALU.max))
                pick(o2[:], el2[:], m2[:], k.c("rank8"), EG, t8[:])
                V.tensor_tensor(t8[:], el[:], b3(m1[:], EG), ALU.subtract).then_inc(exp_in, 1)
                V.tensor_tensor(e2[:], m2[:], m1[:], ALU.subtract).then_inc(exp_in, 1)
                dve.wait_ge(exp_out, 1)
                link(V.tensor_reduce(gs[:], gd[:], AX, ALU.add))
                link(V.reciprocal(gs[:], gs[:]))
                dve.wait_ge(exp_out, 3)
                link(V.tensor_reduce(ss[:], t8[:], AX, ALU.add))
                link(V.reciprocal(ss[:], ss[:]))
                link(V.tensor_tensor(e2[:], e2[:], ss[:], ALU.mult))
                link(V.tensor_tensor(den[:], e2[:], ss[:], ALU.add))
                link(V.reciprocal(den[:], den[:]))
                link(V.tensor_tensor(den[:], den[:], gs[:], ALU.mult))
                V.tensor_tensor(k.wts[:, :, 0], ss[:], den[:], ALU.mult)
                V.tensor_tensor(k.wts[:, :, 1], e2[:], den[:], ALU.mult)
                for o, m in ((o1, M1), (o2, M2)):
                    link(V.tensor_tensor(m[:], bc(goh[:].unsqueeze(3), P, T, G, EG), bc(o[:].unsqueeze(2), P, T, G, EG), ALU.mult))
                V.tensor_tensor(MM[:], M1[:], M2[:], ALU.add).then_inc(sel_ready, 1)
                dve.wait_ge(ranks_ready, 1)
                tot = k.ps[:, 1, 0:T * E].rearrange("p (t e) -> p t e", t=T)
                link(V.tensor_reduce(cnt[:], tot.rearrange("p t e -> p e t"), AX, ALU.add))
                link(V.tensor_scalar(ni[:], cnt[:], float(P - 1), None, ALU.add))
                link(V.tensor_scalar(ni[:], ni[:], LOG_P, None, ALU.arith_shift_right))
                link(V.tensor_copy(nb[:], ni[:]))
                link(V.tensor_tensor(cmp[:, 0:E, :], k.c("prefix").rearrange("p (a b) -> p a b", a=E), bc(nb[:].unsqueeze(1), P, E, E), ALU.mult))
                link(V.tensor_reduce(pe_[:], cmp[:, 0:E, :], AX, ALU.add))
                link(V.tensor_tensor(start[:], pe_[:], nb[:], ALU.subtract))
                link(V.tensor_scalar(base[:, 0, :], start[:], float(P), None, ALU.mult))
                for t in range(1, T):
                    link(V.tensor_tensor(base[:, t, :], base[:, t - 1, :], tot[:, t - 1, :], ALU.add))
                link(V.tensor_tensor(R[:], base[:], k.ps[:, 0, 0:T * E].rearrange("p (t e) -> p t e", t=T), ALU.add))
                for i, m in enumerate((M1, M2)):
                    mf = m[:].rearrange("p t g e -> p t (g e)")
                    link(V.tensor_tensor(mf, mf, R[:], ALU.mult))
                    link(V.tensor_reduce(pos[:, :, i:i + 1], mf, AX, ALU.add))
                link(V.tensor_copy(k.pos_i[:], pos[:]))
                link(V.tensor_scalar(pmi[:], k.pos_i[:], P - 1, None, ALU.bitwise_and))
                link(V.tensor_scalar(pbi[:], k.pos_i[:], LOG_P, None, ALU.arith_shift_right))
                link(V.tensor_copy(pm[:], pmi[:]))
                link(V.tensor_copy(pb[:], pbi[:]))
                iota = k.c("iota")
                link(V.tensor_tensor(hotp[:], bc(iota.unsqueeze(1).unsqueeze(1), P, T, 2, P), bc(pm[:].unsqueeze(3), P, T, 2, P), ALU.is_equal))
                link(V.tensor_tensor(hotb[:], bc(iota[:, 0:BLK].unsqueeze(1).unsqueeze(1), P, T, 2, BLK), bc(pb[:].unsqueeze(3), P, T, 2, BLK),
                                     ALU.is_equal))
                V.tensor_tensor(hotb[:], hotb[:], bc(k.c("token").unsqueeze(2).unsqueeze(3), P, T, 2, BLK), ALU.mult).then_inc(hot_ready, 1)
                link(V.tensor_tensor(cmp[:], bc(pe_[:].unsqueeze(1), P, BLK, E), bc(iota[:, 0:BLK].unsqueeze(2), P, BLK, E), ALU.is_le))
                link(V.tensor_reduce(be[:], cmp[:], AX, ALU.add))
                link(V.tensor_scalar(be[:], be[:], float(E - 1), None, ALU.min))
                V.tensor_copy(k.expert_i[:], be[:])
                link(V.tensor_scalar(k.npair_i[:], pe_[:, E - 1:E], 1.0, None, ALU.add))
                link(V.tensor_scalar(k.npair_i[:], k.npair_i[:], 1, None, ALU.arith_shift_right))
                dve.wait_ge(rows_ready, 1)
                link(V.tensor_copy(k.rows_i[:], k.ps[:, 2, 0:BLK]))


def wait_past(eng, sem, value):
    if not isinstance(value, int) or value > 0:
        eng.wait_ge(sem, value)


def experts(nc, k, l):
    with Stage(nc, pool_dmas=True) as st:
        idx_ready = st.sem("idx_ready")
        x_in = [st.sem("x_in0"), st.sem("x_in1")]
        gu_in = [st.sem("gu_in0"), st.sem("gu_in1")]
        dn_in = [st.sem("dn_in0"), st.sem("dn_in1")]
        x_turned, xt_ready, gu_ready, silued, h_ready = (st.sem("x_turned"), st.sem("xt_ready"), st.sem("gu_ready"),
                                                         st.sem("silued"), st.sem("h_ready"))
        h_turned, ht_ready, y_ready, y_act, y_dve = (st.sem("h_turned"), st.sem("ht_ready"), st.sem("y_ready"), st.sem("y_act"),
                                                     st.sem("y_dve"))
        y_out = [st.sem("y_out0"), st.sem("y_out1")]
        all_stored, gather_due = st.sem("all_stored"), st.sem("gather_due")
        idx = st.sb("idx", [P, 2], I32)
        xg = st.sb("xg", [P, 2, D])
        xT = st.sb("xT", [P, 2, KD, P])
        wgu = st.sb("wgu", [P, 2, KD, 2 * FF])
        wd = st.sb("wd", [P, 2, 2, D])
        sg = st.sb("sg", [P, 2, FF])
        hh = st.sb("hh", [P, 2, FF])
        hT = st.sb("hT_ff", [P, 2, 2, P])
        y = st.sb("y_out", [P, 2, D])

        def turns(eng, turn):
            n = eng.value_load(k.npair_i[0:1, 0:1], min_val=LEAST // 2, max_val=BLOCKS // 2)
            turn(0)
            with eng.Fori(1, n) as p:
                turn(p)
            return n

        def column(table, b):
            return table[:, b:b + 1] if isinstance(b, int) else table[:, bass.ds(b, 1)]

        with nc.Block() as block:
            @block.gpsimd
            def _(pool):
                def gather(s, b):
                    nc.gpsimd.tensor_copy(idx[:, s:s + 1], column(k.rows_i, b)).then_inc(idx_ready, 1)
                    pool.wait_ge(idx_ready, b + 1)
                    pool.sem_inc(gather_due, 1)
                    pool.indirect_dma_start(xg[:, s, :], None, k.d_h[:, :],
                                            bass.IndirectOffsetOnAxis(idx[:, s:s + 1], axis=0)).then_inc(x_in[s], 16)

                def turn(p):
                    for s in range(2):
                        b = p * 2 + s
                        wait_past(pool, x_turned, b)
                        gather(1 - s, b + 1)

                gather(0, 0)
                n = turns(pool, turn)
                for s in range(2):
                    pool.wait_ge(x_in[s], (n + 1 - s) * 16)
                    pool.sem_inc(gather_due, 1)

            @block.sync
            def _(sp):
                def turn(p):
                    for s in range(2):
                        b = p * 2 + s
                        e = sp.value_load(column(k.expert_i[0:1, :], b), min_val=0, max_val=E - 1)
                        w = bass.ds(l * E + e, 1)
                        wait_past(sp, gu_ready, b - 1)
                        sp.dma_start(wgu[:, s, :, 0:FF], k.w_gate[w].rearrange("a (c p) n -> p (a c) n", p=P)).then_inc(gu_in[s], 16)
                        sp.dma_start(wgu[:, s, :, FF:], k.w_up[w].rearrange("a (c p) n -> p (a c) n", p=P)).then_inc(gu_in[s], 16)
                        wait_past(sp, y_ready, b - 1)
                        sp.dma_start(wd[:, s], k.w_down[w].rearrange("a (c p) n -> p (a c) n", p=P)).then_inc(dn_in[s], 16)

                turns(sp, turn)

            @block.tensor
            def _(pe):
                def turn_x(s, nth, b):
                    pe.wait_ge(x_in[s], nth * 16)
                    wait_past(pe, xt_ready, b * 2)
                    for c in range(KD):
                        last = nc.tensor.transpose(k.ps[:, c // 4, (c % 4) * P:(c % 4 + 1) * P], xg[:, s, c * P:(c + 1) * P], k.c("ident"))
                    last.then_inc(x_turned, 1)

                def turn(p):
                    for s in range(2):
                        b = p * 2 + s
                        pe.wait_ge(gu_in[s], p * 32 + 32)
                        pe.wait_ge(xt_ready, b * 2 + 2)
                        for c in range(KD):
                            last = nc.tensor.matmul(k.ps[:, 2 + s, :], xT[:, s, c, :], wgu[:, s, c, :], start=(c == 0), stop=(c == KD - 1))
                        last.then_inc(gu_ready, 1)
                        turn_x(1 - s, p + 1 + s, b + 1)
                        pe.wait_ge(h_ready, b + 1)
                        for c in range(2):
                            last = nc.tensor.transpose(k.ps[:, 4, c * P:(c + 1) * P], hh[:, s, c * P:(c + 1) * P], k.c("ident"))
                        last.then_inc(h_turned, 1)
                        pe.wait_ge(ht_ready, b + 1)
                        pe.wait_ge(dn_in[s], p * 16 + 16)
                        wait_past(pe, y_act, b)
                        wait_past(pe, y_dve, b)
                        for m in range(2):
                            for c in range(2):
                                last = nc.tensor.matmul(k.ps[:, 5 + m, :], hT[:, s, c, :], wd[:, s, c, m * HALF:(m + 1) * HALF],
                                                        start=(c == 0), stop=(c == 1))
                        last.then_inc(y_ready, 1)

                turn_x(0, 1, 0)
                turns(pe, turn)

            @block.scalar
            def _(act):
                def take_x(s, b):
                    act.wait_ge(x_turned, b + 1)
                    for m in range(2):
                        nc.scalar.activation(xT[:, s, 4 * m:4 * m + 4, :], k.ps[:, m, :].rearrange("p (c s) -> p c s", c=4),
                                             ACT.Copy).then_inc(xt_ready, 1)

                def turn(p):
                    for s in range(2):
                        b = p * 2 + s
                        act.wait_ge(gu_ready, b + 1)
                        nc.scalar.activation(sg[:, s, :], k.ps[:, 2 + s, 0:FF], ACT.Silu).then_inc(silued, 1)
                        take_x(1 - s, b + 1)
                        act.wait_ge(h_turned, b + 1)
                        nc.scalar.activation(hT[:, s], k.ps[:, 4, 0:2 * P].rearrange("p (c s) -> p c s", c=2), ACT.Copy).then_inc(ht_ready, 1)
                        act.wait_ge(y_ready, b + 1)
                        wait_past(act, y_out[s], p * 16)
                        nc.scalar.activation(y[:, s, 0:HALF], k.ps[:, 5, :], ACT.Copy).then_inc(y_act, 1)
                        act.wait_ge(y_act, b + 1)
                        act.wait_ge(y_dve, b + 1)
                        rows = k.d_y[b * P:(b + 1) * P, :] if isinstance(b, int) else k.d_y[bass.ds(b * P, P), :]
                        act.dma_start(rows, y[:, s, :]).then_inc(y_out[s], 16)

                take_x(0, 0)
                n = turns(act, turn)
                for s in range(2):
                    act.wait_ge(y_out[s], n * 16)
                    act.sem_inc(all_stored, 1)
                act.wait_ge(all_stored, 2)

            @block.vector
            def _(dve):
                def turn(p):
                    for s in range(2):
                        b = p * 2 + s
                        dve.wait_ge(silued, b + 1)
                        nc.vector.tensor_tensor(hh[:, s, :], sg[:, s, :], k.ps[:, 2 + s, FF:], ALU.mult).then_inc(h_ready, 1)
                        dve.wait_ge(y_ready, b + 1)
                        wait_past(dve, y_out[s], p * 16)
                        nc.vector.tensor_copy(y[:, s, HALF:], k.ps[:, 6, :]).then_inc(y_dve, 1)

                turns(dve, turn)


def combine(nc, k):
    with Stage(nc, pool_dmas=True) as st:
        y_in = [st.sem(f"y_in{i}") for i in range(4)]
        first, added = st.sem("first"), st.sem("added")
        yg = st.sb("yg", [P, 4, D])
        with nc.Block() as block:
            @block.gpsimd
            def _(pool):
                for n in range(2 * T):
                    t, i = n // 2, n % 2
                    if n >= 4:
                        pool.wait_ge((first, added)[i], t - 1)
                    pool.indirect_dma_start(yg[:, n % 4, :], None, k.d_y[:, :],
                                            bass.IndirectOffsetOnAxis(k.pos_i[:, t, i:i + 1], axis=0)).then_inc(y_in[n % 4], 16)
                for n in range(4):
                    pool.wait_ge(y_in[n], 16 * (2 * T // 4))

            @block.vector
            def _(dve):
                for n in range(2 * T):
                    t, i = n // 2, n % 2
                    dve.wait_ge(y_in[n % 4], 16 * (n // 4 + 1))
                    if i:
                        dve.wait_ge(first, t + 1)
                    nc.vector.scalar_tensor_tensor(k.x[:, t, :], yg[:, n % 4, :], k.wts[:, t, i:i + 1], k.x[:, t, :],
                                                   ALU.mult, ALU.add).then_inc((first, added)[i], 1)
                dve.wait_ge(added, T)


def final(nc, k):
    with Stage(nc) as st:
        gain_in, sq, step, ready, stored = st.sem("gain_in"), st.sem("sq"), st.sem("final_step"), st.sem("ready"), st.sem("stored")
        rstd_ready = st.sem("rstd_ready")
        ssq = st.sb("ssq5", [P, T])
        junk = st.sb("junk5", [P, 2, D])
        out = k.out.rearrange("b (t p) n -> p (b t) n", p=P)
        with nc.Block() as block:
            @block.gpsimd
            def _(pool):
                link = linker(pool, step)
                for t in range(T):
                    pool.wait_ge(sq, t + 1)
                    rstd(nc, k, link, ssq[:, t:t + 1], D).then_inc(rstd_ready, 1)

            @block.sync
            def _(sp):
                sp.dma_start(k.gain[:], bc(k.norm_final.unsqueeze(0), P, D)).then_inc(gain_in, 16)
                for t in range(T):
                    sp.wait_ge(ready, t + 1)
                    sp.dma_start(out[:, t, :], k.x[:, t, :]).then_inc(stored, 16)
                sp.wait_ge(stored, 16 * T)

            @block.scalar
            def _(act):
                for t in range(T):
                    if t >= 2:
                        act.wait_ge(sq, t - 1)
                    nc.scalar.activation(junk[:, t % 2, :], k.x[:, t, :], ACT.Square, accum_out=ssq[:, t:t + 1]).then_inc(sq, 1)

            @block.vector
            def _(dve):
                dve.wait_ge(gain_in, 16)
                for t in range(T):
                    dve.wait_ge(rstd_ready, t + 1)
                    nc.vector.scalar_tensor_tensor(k.x[:, t, :], k.x[:, t, :], ssq[:, t:t + 1], k.gain[:],
                                                   ALU.mult, ALU.mult).then_inc(ready, 1)


def program(nc, d_const, x, positions, norm_mix, w_in, conv_a, fox_forget_bias, ssm_conv_w, ssm_conv_b, ssm_dt_bias,
            ssm_a_log, ssm_d, ssm_norm, mla_q_norm, mla_kv_norm, mla_w_uq, mla_w_ukv, w_out, norm_ffn, router_group_w,
            router_group_b, router_expert_w, router_expert_b, expert_w_gate, expert_w_up, expert_w_down, norm_final, out):
    with ExitStack() as ctx:
        def sb(name, shape, dtype=F32):
            return ctx.enter_context(nc.sbuf_tensor(name, shape, dtype))

        k = Core()
        k.d_const, k.d_x, k.positions, k.out = d_const, x, positions, out
        k.norm_mix, k.norm_ffn, k.norm_final = norm_mix, norm_ffn, norm_final
        k.w_in, k.w_out, k.conv_a, k.fox_forget_bias = w_in, w_out, conv_a, fox_forget_bias
        k.ssm_conv_w, k.ssm_conv_b, k.ssm_dt_bias, k.ssm_a_log = ssm_conv_w, ssm_conv_b, ssm_dt_bias, ssm_a_log
        k.ssm_d, k.ssm_norm = ssm_d, ssm_norm
        k.mla_q_norm, k.mla_kv_norm, k.mla_w_uq, k.mla_w_ukv = mla_q_norm, mla_kv_norm, mla_w_uq, mla_w_ukv
        k.router_group_w, k.router_group_b = router_group_w, router_group_b
        k.router_expert_w, k.router_expert_b = router_expert_w, router_expert_b
        k.w_gate, k.w_up, k.w_down = (w.rearrange("l e k n -> (l e) k n") for w in (expert_w_gate, expert_w_up, expert_w_down))
        k.d_h = nc.dram_tensor("h_rows", (S, D), F32).ap()
        k.d_y = nc.dram_tensor("y_rows", (BLOCKS * P, D), F32).ap()
        k.ps = ctx.enter_context(nc.psum_tensor("banks", [P, 8, HALF], F32))

        k.spare_filled = ctx.enter_context(nc.semaphore("spare_filled"))
        k.x = sb("x_res", [P, T, D])
        k.zeros = sb("zeros", [P, D])
        k.const = sb("const", [P, CONSTANTS.shape[1]])
        k.c = lambda name: k.const[:, CONST[name][0]:CONST[name][0] + CONST[name][1]]
        k.ident_b = sb("ident_b", [P, P], BF16)
        k.mask_fox = sb("mask_fox", [P, P], BF16)
        k.mask_mla = sb("mask_mla", [P, P], BF16)
        k.mask_ssd = sb("mask_ssd", [P, HEADS * P], BF16)
        k.trig = sb("trig", [P, 2, T, HR])
        k.gain = sb("gain", [P, D])
        k.cw, k.cb, k.ca = sb("cw", [P, 4, TAPS_C]), sb("cb", [P, 4]), sb("ca", [P, 2, TAPS_A])
        k.bias8, k.alog, k.dskip = sb("bias8", [P, 2 * HEADS]), sb("alog", [P, HEADS]), sb("dskip", [P, HEADS])
        k.sng, k.qng, k.kvng = sb("sng", [P, GW]), sb("qng", [P, GW]), sb("kvng", [P, P])
        k.rb, k.rw = sb("rb", [P, G + E]), sb("rw", [P, KD, G + E])
        k.wuq, k.wukv = sb("wuq", [P, 2, HEADS * MLA_D]), sb("wukv", [P, HALF])
        k.logits = sb("logits", [P, T, G + E])
        k.wts, k.pos_i = sb("wts", [P, T, 2]), sb("pos_rows", [P, T, 2], I32)
        k.expert_i, k.npair_i, k.rows_i = sb("expert_i", [P, BLK], I32), sb("npair_i", [P, 1], I32), sb("rows_i", [P, BLK], I32)

        setup(nc, k)
        with nc.Fori(0, DEPTH) as l:
            with ExitStack() as mix:
                def sm(name, shape):
                    return mix.enter_context(nc.sbuf_tensor(name, shape, F32))

                k.hT = sm("hT", [P, KD, S])
                k.yT = k.hT[:, 0:6, :]
                k.vm = k.hT[:, 6:8, :].rearrange("p a s -> p (a s)").rearrange("p (t n) -> p t n", t=T)
                k.QK = sm("QK", [P, 2, HEADS, S])
                k.QT, k.KT = k.QK[:, 0], k.QK[:, 1]
                k.yA = sm("yA", [P, 2, S])
                k.xbcT = sm("xbcT", [P, 4, S])
                lows = WMAX + P + ROPE
                k.over = sm("over", [P, T * (GW + WMAX + lows)])
                k.z = k.over[:, 0:T * GW].rearrange("p (t n) -> p t n", t=T)
                k.vf = k.over[:, T * GW:T * (GW + WMAX)].rearrange("p (t n) -> p t n", t=T)
                k.low = k.over[:, T * (GW + WMAX):].rearrange("p (t n) -> p t n", t=T)
                k.dt, k.adec = sm("dt", [P, T, HEADS]), sm("adec", [P, T, HEADS])
                k.decay, k.carry = sm("decay", [P, 2, T * HEADS]), sm("carry", [P, T, 2])

                project(nc, k, l)
                prepare(nc, k)
                attend(nc, k, "fox", FOX_K, lambda b, h: k.vf[:, b, h * HD:(h + 1) * HD], k.mask_fox, 0)
                ssd(nc, k)
                prepare_mla(nc, k)
                attend(nc, k, "mla", MLA_D, lambda b, h: k.vm[:, b, h * HD:(h + 1) * HD], k.mask_mla, 4)
                join(nc, k, l)
            route(nc, k)
            experts(nc, k, l)
            combine(nc, k)
        final(nc, k)


_INS = ['x', 'positions', 'norm_mix', 'w_in', 'conv_a', 'fox_forget_bias', 'ssm_conv_w', 'ssm_conv_b', 'ssm_dt_bias',
        'ssm_a_log', 'ssm_d', 'ssm_norm', 'mla_q_norm', 'mla_kv_norm', 'mla_w_uq', 'mla_w_ukv', 'w_out', 'norm_ffn',
        'router_group_w', 'router_group_b', 'router_expert_w', 'router_expert_b', 'expert_w_gate', 'expert_w_up',
        'expert_w_down', 'norm_final']


def kernel(**inputs):
    import concourse.bacc as _bacc
    from concourse.bass_utils import run_bass_kernel_spmd as _run

    nc = _bacc.Bacc("TRN2", target_bir_lowering=False, num_devices=1)
    arrays = {"in_const_dram": CONSTANTS}
    args = [nc.dram_tensor("in_const_dram", CONSTANTS.shape, F32, kind="ExternalInput").ap()]
    for name in _INS:
        a = np.ascontiguousarray(inputs[name])
        arrays[f"in_{name}_dram"] = a
        args.append(nc.dram_tensor(f"in_{name}_dram", a.shape, mybir.dt.from_np(a.dtype), kind="ExternalInput").ap())
    args.append(nc.dram_tensor("out_0_dram", (1, S, D), F32, kind="ExternalOutput").ap())
    program(nc, *args)
    r = _run(nc, [arrays], core_ids=[0])
    return r.results[0]["out_0_dram"]
```

```python
from contextlib import ExitStack

import numpy as np

import concourse.bass as bass
from concourse import mybir

ALU = mybir.AluOpType
ACT = mybir.ActivationFunctionType
AX = mybir.AxisListType.X
F32 = mybir.dt.float32
BF16 = mybir.dt.bfloat16
F32R = mybir.dt.float32r
I32 = mybir.dt.int32

P = 128
LOG_P = 7
D = 1024
S = 1024
DEPTH = 2
T = S // P
KD = D // P
EPS = 1e-6
HALF = 512

GW = 256
HEADS = 4
HD = 64
FOX_K = HD + 2
MLA_D = 96
ROPE = 32
HR = ROPE // 2
TAPS_A = 3
TAPS_C = 4
STATE = 64

A0 = 0
B0 = 3 * GW
F0 = B0 + 3 * GW
C0 = F0 + HEADS
XBC0 = C0 + GW
DT0 = XBC0 + 512
D0 = DT0 + HEADS
KV0 = D0 + GW
IN_COLS = KV0 + P + ROPE

G = 4
EG = 8
E = G * EG
FF = 256
BLOCKS = 48
LEAST = 2 * S // P
BLK = 50
NEG = -1.0e30

PAIRS = [("xbc", 0, XBC0), ("xbc", 2, XBC0 + GW), ("cgate", 0, A0 + GW), ("val", 0, A0 + 2 * GW),
         ("bgate", 0, A0), ("q", 0, B0), ("k", 0, B0 + GW)]
GROUPS = [("z", C0, GW), ("vf", B0 + 2 * GW, GW + HEADS), ("dtq", DT0, HEADS + GW), ("kv", IN_COLS - GW, GW)]
WMAX = GW + HEADS
KV_AT = GW - P - ROPE

PARAMS = TAPS_C + 1 + TAPS_A + 13

CONST = {}


def constants():
    i = np.arange(P)
    parts = {
        "ident": np.eye(P),
        "le": i[:, None] <= i[None, :],
        "lt": i[:, None] < i[None, :],
        "gt": i[:, None] > i[None, :],
        "ones": np.ones((P, P)),
        "iota": np.broadcast_to(i, (P, P)),
        "mask_fox": np.where(i[None, :] > i[:, None], NEG, 0.0),
        "mask_mla": np.where((i[None, :] // 64) > (i[:, None] // 64), NEG, 0.0),
        "mask_ssd": np.where(i[None, :] < i[:, None], NEG, 0.0),
        "token": np.arange(T)[None, :] * P + i[:, None],
        "freq": np.broadcast_to(10000.0 ** (-np.arange(0, ROPE, 2) / ROPE), (P, HR)),
        "power": np.full((P, T), -0.5),
        "sign": np.broadcast_to(np.repeat([-1.0, 1.0], HEADS), (P, 2 * HEADS)),
        "rank4": np.broadcast_to(G - np.arange(G), (P, G)),
        "rank8": np.broadcast_to(EG - np.arange(EG), (P, EG)),
    }
    at = 0
    for name, a in parts.items():
        CONST[name] = (at, a.shape[1])
        at += a.shape[1]
    return np.ascontiguousarray(np.concatenate([np.asarray(a, np.float32) for a in parts.values()], 1))


CONSTANTS = constants()


def linker(eng, sem):
    count = [0]

    def link(ins):
        count[0] += 1
        ins.then_inc(sem, 1)
        eng.wait_ge(sem, count[0])

    return link


class Core:
    pass


class Stage:

    def __init__(self, nc, pool_dmas=False):
        self.nc, self.ctx, self.sems, self.pool_dmas = nc, ExitStack(), [], pool_dmas

    def __enter__(self):
        return self

    def sem(self, name):
        s = self.ctx.enter_context(self.nc.semaphore(name))
        self.sems.append(s)
        return s

    def sb(self, name, shape, dtype=F32):
        return self.ctx.enter_context(self.nc.sbuf_tensor(name, shape, dtype))

    def __exit__(self, *_):
        nums = sorted(s.num for s in self.sems)
        assert nums[-1] - nums[0] + 1 == len(nums)
        if self.pool_dmas:
            self.nc.gpsimd.dma_reset(range(nums[0], nums[-1] + 1))
        self.nc.all_engine_barrier(sems_to_clear=range(nums[0], nums[-1] + 1))
        self.ctx.close()


def bc(ap, *shape):
    return ap.broadcast_to(list(shape))


def ends_at(nc):
    return nc.sbuf_base


def over_again(nc, name, shape, dtype, end):
    size = 4 * int(np.prod(shape[1:]))
    return nc.alloc_sbuf_tensor_at(name, shape, dtype, offset=end - size)


def rstd(nc, k, link, ssq, n):
    link(nc.gpsimd.tensor_scalar(ssq, ssq, 1.0 / n, EPS, ALU.mult, ALU.add))
    return nc.gpsimd.tensor_tensor(ssq, ssq, k.c("power")[:, 0:ssq.shape[1]], ALU.pow)


def setup(nc, k):
    with Stage(nc) as st:
        consts_in, x_in, pos_in = st.sem("consts_in"), st.sem("x_in"), st.sem("pos_in")
        step, angle_ready, trig_done = st.sem("setup_step"), st.sem("angle_ready"), st.sem("trig_done")
        pos_i = st.sb("pos_i", [P, T], I32)
        pos_f = st.sb("pos_f", [P, T])
        ang = st.sb("ang", [P, T, HR])
        turn = st.sb("turn", [P, T, HR])
        cosa = st.sb("cosa", [P, T, HR])
        with nc.Block() as block:
            @block.sync
            def _(sp):
                sp.dma_start(k.const[:, :], k.d_const[:, :]).then_inc(consts_in, 16)
                with nc.allow_non_contiguous_dma("positions, one to a partition"):
                    sp.dma_start(pos_i[:], k.positions.rearrange("b (t p) -> p (b t)", p=P)).then_inc(pos_in, 16)
                sp.dma_start(k.x[:], k.d_x.rearrange("b (t p) n -> p (b t) n", p=P)).then_inc(x_in, 16)
                sp.wait_ge(x_in, 16)

            @block.vector
            def _(dve):
                link = linker(dve, step)
                dve.wait_ge(consts_in, 16)
                for name, tile, reps in (("ident", k.ident_b, 1), ("mask_fox", k.mask_fox, 1), ("mask_mla", k.mask_mla, 1),
                                         ("mask_ssd", k.mask_ssd, HEADS)):
                    for r in range(reps):
                        nc.vector.tensor_copy(tile[:, r * P:(r + 1) * P], k.c(name))
                dve.wait_ge(pos_in, 16)
                link(nc.vector.tensor_copy(pos_f[:], pos_i[:]))
                link(nc.vector.tensor_tensor(ang[:], bc(pos_f[:].unsqueeze(2), P, T, HR),
                                             bc(k.c("freq").unsqueeze(1), P, T, HR), ALU.mult))
                big = 1.5 * 2.0 ** 23
                link(nc.vector.tensor_scalar(turn[:], ang[:], float(1.0 / (2 * np.pi)), None, ALU.mult))
                link(nc.vector.tensor_scalar(turn[:], turn[:], big, None, ALU.add))
                link(nc.vector.tensor_scalar(turn[:], turn[:], -big, None, ALU.add))
                c1 = 6.28125
                c2 = float(np.round((2 * np.pi - c1) * 2 ** 21) / 2 ** 21)
                c3 = float(2 * np.pi - c1 - c2)
                for c in (c1, c2, c3):
                    link(nc.vector.scalar_tensor_tensor(ang[:], turn[:], -c, ang[:], ALU.mult, ALU.add))
                link(nc.vector.tensor_scalar(cosa[:], ang[:], float(np.pi / 2), None, ALU.add))
                link(nc.vector.tensor_scalar(turn[:], cosa[:], float(np.pi), None, ALU.is_gt))
                link(nc.vector.scalar_tensor_tensor(cosa[:], turn[:], float(-2 * np.pi), cosa[:], ALU.mult, ALU.add))
                lim = 3.1415925
                link(nc.vector.tensor_scalar(cosa[:], cosa[:], lim, -lim, ALU.min, ALU.max))
                nc.vector.tensor_scalar(ang[:], ang[:], lim, -lim, ALU.min, ALU.max).then_inc(angle_ready, 1)

            @block.scalar
            def _(act):
                act.wait_ge(angle_ready, 1)
                nc.scalar.activation(k.trig[:, 1], ang[:], ACT.Sin)
                nc.scalar.activation(k.trig[:, 0], cosa[:], ACT.Sin).then_inc(trig_done, 1)
                act.wait_ge(trig_done, 1)


def project(nc, k, l):
    with Stage(nc) as st:
        params_in, gain_in = st.sem("params_in"), st.sem("gain_in")
        squares, norm_step, h_ready = st.sem("squares"), st.sem("norm_step"), st.sem("h_ready")
        rstd_ready = st.sem("rstd_ready")
        turned, ht_hi, ht_lo = st.sem("turned"), st.sem("ht_hi"), st.sem("ht_lo")
        x_saved, w_hi_set, w_lo_set = [st.sem("x_saved0"), st.sem("x_saved1")], st.sem("w_hi_set"), st.sem("w_lo_set")
        w_in_sem = [st.sem("w_in_even"), st.sem("w_in_odd")]
        w_used, proj_ready = st.sem("w_used"), st.sem("proj_ready")
        act_took, dve_took = st.sem("act_took"), st.sem("dve_took")
        conv_step, conv_done, silu_done, a_done = (st.sem("conv_step"), st.sem("conv_done"), st.sem("silu_done"),
                                                   st.sem("a_done"))
        ring = st.sb("w_ring", [P, 2, KD, WMAX])
        w_lo = over_again(nc, "w_lo", [P, 2, KD, WMAX], F32R, ends_at(nc))
        w_hi = st.sb("w_hi", [P, 2, KD, WMAX], F32R)
        h_hi = over_again(nc, "h_hi", [P, KD, S], F32R, k.hT_end)
        h_lo = over_again(nc, "h_lo", [P, T, KD, P], F32R, k.x_end)
        ssq = st.sb("ssq", [P, T])
        over = k.over
        cbuf = over[:, 0:2 * S].rearrange("p (j s) -> p j s", j=2)
        upad = over[:, 2 * S:2 * S + 2 * (S + 2)].rearrange("p (j s) -> p j s", j=2)
        r0 = 4 * S + 4
        raw = over[:, r0:r0 + 2 * (S + 3)].rearrange("p (j s) -> p j s", j=2)
        hn = raw[:, :, 3:]
        loads = [(c0, GW) for _, _, c0 in PAIRS] + [(c0, n) for _, c0, n in GROUPS]

        taker = []
        for kind, _, _ in PAIRS:
            taker += [kind in ("val", "bgate")] * 4
        taker += [False] * (len(GROUPS) * T)

        def order(i):
            return [(j, n) for n in range(2) for j in range(2)] if i == 0 else [(j, n) for j in range(2) for n in range(2)]

        def emptied(eng, q):
            sem = dve_took if taker[q] else act_took
            eng.wait_ge(sem, sum(t == taker[q] for t in taker[:q + 1]))

        with nc.Block() as block:
            @block.gpsimd
            def _(pool):
                link = linker(pool, norm_step)
                for t in range(T):
                    pool.wait_ge(squares, t + 1)
                    rstd(nc, k, link, ssq[:, t:t + 1], D).then_inc(rstd_ready, 1)

            @block.sync
            def _(sp):
                row = bass.ds(l, 1)
                sp.dma_start(k.gain[:], bc(k.norm_mix[row, :], P, D)).then_inc(gain_in, 16)

                def save(m):
                    half = slice(m * T // 2, (m + 1) * T // 2)
                    sp.dma_start(k.d_xs[:, half, :], k.x[:, half, :]).then_inc(x_saved[m], 16)

                save(0)

                def load_params():
                    def load(dst, src):
                        sp.dma_start(dst, src).then_inc(params_in, 16)

                    with nc.allow_non_contiguous_dma("small parameter tables"):
                        for tap in range(TAPS_C):
                            load(k.cw[:, :, tap], k.ssm_conv_w[row, tap].rearrange("a (j p) -> p (a j)", p=P))
                        load(k.cb[:], k.ssm_conv_b[row].rearrange("a (j p) -> p (a j)", p=P))
                        for tap in range(TAPS_A):
                            load(k.ca[:, :, tap], k.conv_a[row, tap].rearrange("a (j p) -> p (a j)", p=P))
                    load(k.bias8[:, 0:HEADS], bc(k.fox_forget_bias[row, :], P, HEADS))
                    load(k.bias8[:, HEADS:], bc(k.ssm_dt_bias[row, :], P, HEADS))
                    load(k.alog[:], bc(k.ssm_a_log[row, :], P, HEADS))
                    load(k.dskip[:], bc(k.ssm_d[row, :], P, HEADS))
                    load(k.sng[:], bc(k.ssm_norm[row, :], P, GW))
                    load(k.qng[:], bc(k.mla_q_norm[row, :], P, GW))
                    load(k.kvng[:], bc(k.mla_kv_norm[row, :], P, P))
                    load(k.rb[:, 0:G], bc(k.router_group_b[row, :], P, G))
                    load(k.rb[:, G:], bc(k.router_expert_b[row, :], P, E))
                    load(k.wuq[:], k.mla_w_uq[row].rearrange("a (c p) n -> p (a c) n", p=P))
                    load(k.wukv[:], k.mla_w_ukv[row].rearrange("a p n -> p (a n)"))
                    load(k.rw[:, :, 0:G], k.router_group_w[row].rearrange("a (c p) n -> p (a c) n", p=P))
                    load(k.rw[:, :, G:], k.router_expert_w[row].rearrange("a (c p) n -> p (a c) n", p=P))

                for i, (c0, n) in enumerate(loads):
                    if i == 1:
                        save(1)
                    if i == 2:
                        load_params()
                    if i >= 2:
                        sp.wait_ge(w_used, i - 1)
                    src = k.w_in[bass.ds(l, 1), :, c0:c0 + n].rearrange("a (c p) n -> p (a c) n", p=P)
                    sp.dma_start(ring[:, i % 2, :, 0:n], src).then_inc(w_in_sem[i % 2], 16)

            @block.tensor
            def _(pe):
                def turn(t):
                    pe.wait_ge(h_ready, t + 1)
                    if t >= 2:
                        pe.wait_ge(ht_lo, t - 1)
                    for c in range(KD):
                        last = nc.tensor.transpose(k.ps[:, 2 * (t % 2) + c // 4, (c % 4) * P:(c % 4 + 1) * P],
                                                   hn[:, t % 2, c * P:(c + 1) * P], k.c("ident"))
                    last.then_inc(turned, 1)

                for t in range(T // 2):
                    turn(t)
                q = 0
                for i in range(len(PAIRS)):
                    pe.wait_ge(w_lo_set, i + 1)
                    for step, (j, n) in enumerate(order(i)):
                        if i == 0:
                            pe.wait_ge(ht_lo, T // 2 * (n + 1))
                        if q >= 4:
                            emptied(pe, q - 4)
                        out = k.ps[:, 4 + q % 4, :].rearrange("p (t s) -> p t s", t=T // 2)
                        w = slice(j * P, (j + 1) * P)
                        for c in range(KD):
                            hi = h_hi[:, c, n * HALF:(n + 1) * HALF].rearrange("p (t s) -> p t s", t=T // 2)
                            lo = h_lo[:, n * T // 2:(n + 1) * T // 2, c, :]
                            nc.tensor.matmul(out, w_hi[:, i % 2, c, w], hi, start=(c == 0), stop=False)
                            nc.tensor.matmul(out, w_hi[:, i % 2, c, w], lo, start=False, stop=False)
                            last = nc.tensor.matmul(out, w_lo[:, i % 2, c, w], hi, start=False, stop=(c == KD - 1))
                        last.then_inc(proj_ready, 1)
                        q += 1
                        if i == 0 and n == 0:
                            turn(T // 2 + 2 * step)
                            turn(T // 2 + 2 * step + 1)
                    pe.wait_ge(proj_ready, q)
                    pe.sem_inc(w_used, 1)
                for g, (_, _, n) in enumerate(GROUPS):
                    i = len(PAIRS) + g
                    pe.wait_ge(w_lo_set, i + 1)
                    for t in range(T):
                        emptied(pe, q - 4)
                        out = k.ps[:, 4 + q % 4, 0:n]
                        for c in range(KD):
                            hi, lo = h_hi[:, c, t * P:(t + 1) * P], h_lo[:, t, c, :]
                            nc.tensor.matmul(out, hi, w_hi[:, i % 2, c, 0:n], start=(c == 0), stop=False)
                            nc.tensor.matmul(out, hi, w_lo[:, i % 2, c, 0:n], start=False, stop=False)
                            last = nc.tensor.matmul(out, lo, w_hi[:, i % 2, c, 0:n], start=False, stop=(c == KD - 1))
                        last.then_inc(proj_ready, 1)
                        q += 1
                    if g < 2:
                        pe.wait_ge(proj_ready, q)
                        pe.sem_inc(w_used, 1)

            @block.scalar
            def _(act):
                def square(t):
                    if t >= 2:
                        act.wait_ge(squares, t - 1)
                    nc.scalar.activation(cbuf[:, t % 2, :], k.x[:, t, :], ACT.Square,
                                         accum_out=ssq[:, t:t + 1]).then_inc(squares, 1)

                def high(i):
                    n = loads[i][1]
                    act.wait_ge(w_in_sem[i % 2], 16 * (i // 2 + 1))
                    nc.scalar.activation(w_hi[:, i % 2, :, 0:n], ring[:, i % 2, :, 0:n], ACT.Copy).then_inc(w_hi_set, 1)

                square(0)
                square(1)
                for t in range(T):
                    act.wait_ge(turned, t + 1)
                    for m in range(2):
                        ins = nc.scalar.activation(h_hi[:, 4 * m:4 * m + 4, t * P:(t + 1) * P],
                                                   k.ps[:, 2 * (t % 2) + m, :].rearrange("p (c s) -> p c s", c=4), ACT.Copy)
                    ins.then_inc(ht_hi, 1)
                    if t + 2 < T:
                        square(t + 2)
                    if t == 1:
                        high(0)
                q = 0
                act.wait_ge(squares, T)

                def silu(j):
                    if j == 0:
                        act.wait_ge(params_in, 16 * PARAMS)
                    act.wait_ge(conv_done, j + 1)
                    nc.scalar.activation(k.xbcT[:, j, :], k.xbcT[:, j, :], ACT.Silu, bias=k.cb[:, j:j + 1]).then_inc(silu_done, 1)

                for i, (kind, j0, _) in enumerate(PAIRS):
                    for step, (j, n) in enumerate(order(i)):
                        if step == 2:
                            high(i + 1)
                        if kind == "xbc" and j0 == 2 and n == 0:
                            act.wait_ge(conv_done, j + 1)
                        cols = slice(n * HALF, (n + 1) * HALF)
                        src = k.ps[:, 4 + q % 4, :]
                        q += 1
                        if kind in ("val", "bgate"):
                            continue
                        act.wait_ge(proj_ready, q)
                        if kind == "xbc":
                            ins = nc.scalar.activation(raw[:, j, 3 + n * HALF:3 + (n + 1) * HALF], src, ACT.Copy)
                        elif kind == "cgate":
                            ins = nc.scalar.activation(cbuf[:, j, cols], src, ACT.Copy)
                        else:
                            dst, scale = (k.QT, HD ** -0.5) if kind == "q" else (k.KT, 1.0)
                            nc.scalar.activation(dst[0:HD, 2 * j, cols], src[0:HD, :], ACT.Copy, scale=scale)
                            ins = nc.scalar.activation(dst[0:HD, 2 * j + 1, cols], src[HD:P, :], ACT.Copy, scale=scale)
                        ins.then_inc(act_took, 1)
                    if kind == "xbc" and j0 == 2 or kind == "cgate":
                        silu(0 if kind == "xbc" else 2)
                        silu(1 if kind == "xbc" else 3)
                act.wait_ge(a_done, 1)
                for g, (kind, _, n) in enumerate(GROUPS):
                    for t in range(T):
                        if t == T // 2 and g + 1 < len(GROUPS):
                            high(len(PAIRS) + g + 1)
                        src = k.ps[:, 4 + q % 4, 0:n]
                        q += 1
                        act.wait_ge(proj_ready, q)
                        if kind == "z":
                            ins = nc.scalar.activation(k.z[:, t, :], src, ACT.Silu)
                        elif kind == "vf":
                            ins = nc.scalar.activation(k.vf[:, t, :], src, ACT.Copy)
                        elif kind == "dtq":
                            ins = nc.scalar.activation(k.low[:, t, 0:n], src, ACT.Copy)
                        else:
                            ins = nc.scalar.activation(k.low[:, t, WMAX:], src[:, KV_AT:], ACT.Copy)
                        ins.then_inc(act_took, 1)

            @block.vector
            def _(dve):
                def low(i):
                    n = loads[i][1]
                    dve.wait_ge(w_hi_set, i + 1)
                    nc.vector.tensor_tensor(w_lo[:, i % 2, :, 0:n], ring[:, i % 2, :, 0:n], w_hi[:, i % 2, :, 0:n],
                                            ALU.subtract).then_inc(w_lo_set, 1)

                def low_h(t):
                    dve.wait_ge(x_saved[2 * t // T], 16)
                    dve.wait_ge(ht_hi, t + 1)
                    for m in range(2):
                        ins = nc.vector.tensor_tensor(h_lo[:, t, 4 * m:4 * m + 4, :],
                                                      k.ps[:, 2 * (t % 2) + m, :].rearrange("p (c s) -> p c s", c=4),
                                                      h_hi[:, 4 * m:4 * m + 4, t * P:(t + 1) * P], ALU.subtract)
                    ins.then_inc(ht_lo, 1)

                dve.wait_ge(gain_in, 16)
                for t in range(T):
                    dve.wait_ge(rstd_ready, t + 1)
                    if t >= 2:
                        dve.wait_ge(turned, t - 1)
                    nc.vector.scalar_tensor_tensor(hn[:, t % 2, :], k.x[:, t, :], ssq[:, t:t + 1], k.gain[:],
                                                   ALU.mult, ALU.mult).then_inc(h_ready, 1)
                    if t >= 1:
                        low_h(t - 1)
                    if t == 3:
                        low(0)
                dve.wait_ge(turned, T)
                nc.vector.memset(raw[:, :, 0:3], 0.0)
                nc.vector.memset(upad[:, :, 0:2], 0.0)
                low_h(T - 1)
                link = linker(dve, conv_step)
                dve.wait_ge(ht_lo, T)
                dve.wait_ge(params_in, 16 * PARAMS)
                for j in range(4):
                    if j % 2 == 0:
                        low(1 + j // 2)
                    dve.wait_ge(act_took, (3, 4, 6, 8)[j])
                    acc = k.xbcT[:, j, :]
                    link(nc.vector.tensor_scalar(acc, raw[:, j % 2, 3:3 + S], k.cw[:, j, 3:4], None, ALU.mult))
                    for tap in (2, 1):
                        link(nc.vector.scalar_tensor_tensor(acc, raw[:, j % 2, tap:tap + S], k.cw[:, j, tap:tap + 1], acc,
                                                            ALU.mult, ALU.add))
                    nc.vector.scalar_tensor_tensor(acc, raw[:, j % 2, 0:S], k.cw[:, j, 0:1], acc,
                                                   ALU.mult, ALU.add).then_inc(conv_done, 1)
                low(3)
                q = 12
                for j in range(2):
                    dve.wait_ge(act_took, 12)
                    for n in range(2):
                        dve.wait_ge(proj_ready, q + 1)
                        ins = nc.vector.tensor_tensor(upad[:, j, 2 + n * HALF:2 + (n + 1) * HALF], k.ps[:, 4 + q % 4, :],
                                                cbuf[:, j, n * HALF:(n + 1) * HALF], ALU.mult)
                        ins.then_inc(dve_took, 1)
                        q += 1
                    if j == 0:
                        low(4)
                    dve.wait_ge(dve_took, q - 12)
                    acc = cbuf[:, j, :]
                    link(nc.vector.tensor_scalar(acc, upad[:, j, 2:2 + S], k.ca[:, j, 2:3], None, ALU.mult))
                    for tap in (1, 0):
                        link(nc.vector.scalar_tensor_tensor(acc, upad[:, j, tap:tap + S], k.ca[:, j, tap:tap + 1], acc,
                                                            ALU.mult, ALU.add))
                for j in range(2):
                    for n in range(2):
                        dve.wait_ge(proj_ready, q + 1)
                        cols = slice(n * HALF, (n + 1) * HALF)
                        nc.vector.tensor_tensor(k.yA[:, j, cols], k.ps[:, 4 + q % 4, :], cbuf[:, j, cols],
                                                ALU.mult).then_inc(dve_took, 1)
                        q += 1
                    if j == 0:
                        low(5)
                dve.wait_ge(dve_took, 8)
                dve.sem_inc(a_done, 1)
                for i in range(6, len(loads)):
                    low(i)
                dve.wait_ge(silu_done, 4)


def prepare(nc, k):
    with Stage(nc) as st:
        step, exp_in, exp_out = st.sem("gate_step"), st.sem("exp_in"), st.sem("exp_out")
        gates_ready, sums_ready, cum_ready = st.sem("gates_ready"), st.sem("sums_ready"), st.sem("cum_ready")
        rows_turned, rows_ready, rows_in, ones_set = (st.sem("rows_turned"), st.sem("rows_ready"), st.sem("rows_in"),
                                                      st.sem("ones_set"))
        decays_done = st.sem("decays_done")
        N8 = 2 * HEADS
        x8, mx, e8, t8, r8, z8, zz, pl = (st.sb(f"gate{i}", [P, T, N8]) for i in range(8))
        aneg = st.sb("aneg", [P, HEADS])
        la = st.sb("log_forget", [P, T, HEADS])
        cum = st.sb("cum", [P, T, HEADS])
        rows = st.sb("cum_rows", [HEADS, 2, S])
        with nc.Block() as block:
            @block.gpsimd
            def _(pool):
                nc.gpsimd.memset(k.QT[HD:HD + 2, :, :], 1.0).then_inc(ones_set, 1)
                nc.gpsimd.memset(k.KT[HD:HD + 2, :, :], 1.0).then_inc(ones_set, 1)

            @block.sync
            def _(sp):
                sp.wait_ge(ones_set, 2)
                sp.wait_ge(rows_ready, 4)
                for h in range(HEADS):
                    sp.dma_start(k.QT[HD:HD + 1, h, :], rows[h:h + 1, 0, :]).then_inc(rows_in, 16)
                    sp.dma_start(k.KT[HD + 1:HD + 2, h, :], rows[h:h + 1, 1, :]).then_inc(rows_in, 16)
                sp.wait_ge(rows_in, 16 * 2 * HEADS)

            @block.scalar
            def _(act):
                act.wait_ge(exp_in, 1)
                nc.scalar.activation(e8[:], t8[:], ACT.Exp, scale=-1.0).then_inc(exp_out, 1)
                nc.scalar.activation(aneg[:], k.alog[:], ACT.Exp).then_inc(exp_out, 1)
                act.wait_ge(sums_ready, 1)
                nc.scalar.activation(k.decay[:, 0:2], k.ps[:, 0, 32:96].rearrange("p (i n) -> p i n", i=2), ACT.Exp)
                nc.scalar.activation(k.carry[0:64, :, :], k.ps[0:64, 0, 96:128].rearrange("p (c h) -> p c h", h=HEADS)[:, :, 0:2], ACT.Exp)
                nc.scalar.activation(k.carry[64:P, :, :], k.ps[64:P, 0, 96:128].rearrange("p (c h) -> p c h", h=HEADS)[:, :, 2:4],
                                     ACT.Exp).then_inc(decays_done, 1)
                act.wait_ge(decays_done, 1)

            @block.tensor
            def _(pe):
                pe.wait_ge(gates_ready, 2)
                flat = la[:].rearrange("p t h -> p (t h)")
                adec = k.adec[:].rearrange("p t h -> p (t h)")
                nc.tensor.matmul(k.ps[:, 1, 0:32], k.c("le"), flat, start=True, stop=True)
                nc.tensor.matmul(k.ps[:, 1, 32:64], k.c("ones"), flat, start=True, stop=True)
                nc.tensor.matmul(k.ps[:, 0, 32:64], k.c("le"), adec, start=True, stop=True)
                nc.tensor.matmul(k.ps[:, 0, 64:96], k.c("gt"), adec, start=True, stop=True)
                nc.tensor.matmul(k.ps[:, 0, 96:128], k.c("ones"), adec, start=True, stop=True).then_inc(sums_ready, 1)
                pe.wait_ge(cum_ready, 1)
                for t in range(T):
                    last = nc.tensor.transpose(k.ps[0:HEADS, 2 + t // 4, (t % 4) * P:(t % 4 + 1) * P], cum[:, t, :], k.c("ident"))
                last.then_inc(rows_turned, 1)

            @block.vector
            def _(dve):
                link = linker(dve, step)
                link(nc.vector.tensor_copy(x8[:, :, 0:HEADS], k.vf[:, :, GW:GW + HEADS]))
                link(nc.vector.tensor_copy(x8[:, :, HEADS:], k.low[:, :, 0:HEADS]))
                link(nc.vector.tensor_tensor(x8[:], x8[:], bc(k.bias8[:].unsqueeze(1), P, T, N8), ALU.add))
                link(nc.vector.tensor_tensor(x8[:], x8[:], bc(k.c("sign").unsqueeze(1), P, T, N8), ALU.mult))
                link(nc.vector.tensor_scalar(mx[:], x8[:], 0.0, None, ALU.max))
                nc.vector.scalar_tensor_tensor(t8[:], x8[:], -1.0, x8[:], ALU.mult, ALU.max).then_inc(exp_in, 1)
                dve.wait_ge(exp_out, 2)
                link(nc.vector.tensor_scalar(r8[:], e8[:], 2.0, None, ALU.add))
                link(nc.vector.reciprocal(r8[:], r8[:]))
                link(nc.vector.tensor_tensor(z8[:], e8[:], r8[:], ALU.mult))
                link(nc.vector.tensor_tensor(zz[:], z8[:], z8[:], ALU.mult))
                link(nc.vector.tensor_scalar(pl[:], zz[:], 1.0 / 17, 1.0 / 15, ALU.mult, ALU.add))
                for n in (13, 11, 9, 7, 5, 3, 1):
                    link(nc.vector.tensor_tensor(pl[:], pl[:], zz[:], ALU.mult))
                    link(nc.vector.tensor_scalar(pl[:], pl[:], 1.0 / n, None, ALU.add))
                link(nc.vector.tensor_tensor(pl[:], pl[:], z8[:], ALU.mult))
                link(nc.vector.scalar_tensor_tensor(x8[:], pl[:], 2.0, mx[:], ALU.mult, ALU.add))
                nc.vector.tensor_scalar(la[:], x8[:, :, 0:HEADS], -1.0, None, ALU.mult).then_inc(gates_ready, 1)
                link(nc.vector.tensor_copy(k.dt[:], x8[:, :, HEADS:]))
                nc.vector.scalar_tensor_tensor(k.adec[:], k.dt[:], -1.0, bc(aneg[:].unsqueeze(1), P, T, HEADS),
                                               ALU.mult, ALU.mult).then_inc(gates_ready, 1)
                dve.wait_ge(sums_ready, 1)
                tot = k.ps[:, 1, 32:64].rearrange("p (t h) -> p t h", h=HEADS)
                link(nc.vector.memset(t8[:, 0, 0:HEADS], 0.0))
                for t in range(1, T):
                    link(nc.vector.tensor_tensor(t8[:, t, 0:HEADS], t8[:, t - 1, 0:HEADS], tot[:, t - 1, :], ALU.add))
                nc.vector.tensor_tensor(cum[:], k.ps[:, 1, 0:32].rearrange("p (t h) -> p t h", h=HEADS), t8[:, :, 0:HEADS],
                                        ALU.add).then_inc(cum_ready, 1)
                dve.wait_ge(rows_turned, 1)
                for n in range(2):
                    src = k.ps[0:HEADS, 2 + n, :]
                    nc.vector.tensor_copy(rows[:, 0, n * HALF:(n + 1) * HALF], src).then_inc(rows_ready, 1)
                    nc.vector.tensor_scalar(rows[:, 1, n * HALF:(n + 1) * HALF], src, -1.0, None, ALU.mult).then_inc(rows_ready, 1)


def prepare_mla(nc, k):
    with Stage(nc) as st:
        step, sq_done, normed = st.sem("norm_step"), st.sem("sq_done"), st.sem("normed")
        c_turned, c_ready, up_ready, qk_ready = st.sem("c_turned"), st.sem("c_ready"), st.sem("up_ready"), st.sem("qk_ready")
        v_took, qk_turned, q_took, k_took = st.sem("v_took"), st.sem("qk_turned"), st.sem("q_took"), st.sem("k_took")
        rstd_step, rstd_ready = st.sem("rstd_step"), st.sem("rstd_ready")
        ssq = st.sb("ssq2", [P, 2, T])
        junk = st.sb("junk", [P, 2, GW + P])
        cn = st.sb("cn", [P, 2, GW + P])
        cT = st.sb("cT", [P, 2, 3, P])
        qn = st.sb("qn", [P, 2, HEADS, MLA_D])
        kn = st.sb("kn", [P, 2, HEADS, MLA_D])
        rot = st.sb("rot", [P, 2, HEADS, 2, HR])
        krot = st.sb("krot", [P, 2, T, 2, HR])
        kr = st.sb("kr", [P, T, 2, HR])
        cq = k.low[:, :, HEADS:WMAX]
        ckv = k.low[:, :, WMAX:WMAX + P]
        ckr = k.low[:, :, WMAX + P:WMAX + P + ROPE].rearrange("p t (i r) -> p t i r", i=2)
        cos, sin = k.trig[:, 0], k.trig[:, 1]

        with nc.Block() as block:
            @block.gpsimd
            def _(pool):
                link = linker(pool, rstd_step)
                pool.wait_ge(sq_done, T)
                rstd(nc, k, link, ssq[:, 0], GW).then_inc(rstd_ready, 1)
                rstd(nc, k, link, ssq[:, 1], P).then_inc(rstd_ready, 1)

            @block.scalar
            def _(act):
                for t in range(T):
                    if t >= 2:
                        act.wait_ge(sq_done, t - 1)
                    nc.scalar.activation(junk[:, t % 2, 0:GW], cq[:, t, :], ACT.Square, accum_out=ssq[:, 0, t:t + 1])
                    nc.scalar.activation(junk[:, t % 2, GW:], ckv[:, t, :], ACT.Square, accum_out=ssq[:, 1, t:t + 1]).then_inc(sq_done, 1)
                for t in range(T + 1):
                    if t < T:
                        act.wait_ge(c_turned, t + 1)
                        nc.scalar.activation(cT[:, t % 2], k.ps[:, t % 2, 0:3 * P].rearrange("p (c s) -> p c s", c=3),
                                             ACT.Copy).then_inc(c_ready, 1)
                        act.wait_ge(up_ready, t + 1)
                        kv = k.ps[:, 4 + t % 2, :].rearrange("p (h i d) -> p h i d", h=HEADS, i=2)
                        nc.scalar.activation(k.vm[:, t].rearrange("p (h d) -> p h d", h=HEADS), kv[:, :, 1, :], ACT.Copy)
                        if t >= 2:
                            act.wait_ge(qk_turned, t - 1)
                        nc.scalar.activation(kn[:, t % 2, :, 0:HD], kv[:, :, 0, :], ACT.Copy).then_inc(v_took, 1)
                    if t >= 1:
                        u = t - 1
                        act.wait_ge(qk_turned, u + 1)
                        nc.scalar.activation(k.QT[0:MLA_D, :, u * P:(u + 1) * P],
                                             k.ps[0:MLA_D, 6, :].rearrange("p (h s) -> p h s", h=HEADS), ACT.Copy,
                                             scale=MLA_D ** -0.5).then_inc(q_took, 1)

            @block.tensor
            def _(pe):
                def up(t):
                    pe.wait_ge(normed, t + 1)
                    for c in range(3):
                        last = nc.tensor.transpose(k.ps[:, t % 2, c * P:(c + 1) * P], cn[:, t % 2, c * P:(c + 1) * P], k.c("ident"))
                    last.then_inc(c_turned, 1)
                    pe.wait_ge(c_ready, t + 1)
                    if t >= 2:
                        pe.wait_ge(qk_ready, t - 1)
                        pe.wait_ge(v_took, t - 1)
                    for c in range(2):
                        nc.tensor.matmul(k.ps[:, 2 + t % 2, 0:HEADS * MLA_D], cT[:, t % 2, c, :], k.wuq[:, c, :],
                                         start=(c == 0), stop=(c == 1))
                    nc.tensor.matmul(k.ps[:, 4 + t % 2, :], cT[:, t % 2, 2, :], k.wukv[:], start=True, stop=True).then_inc(up_ready, 1)

                def turn(t):
                    pe.wait_ge(qk_ready, t + 1)
                    pe.wait_ge(v_took, t + 1)
                    if t >= 1:
                        pe.wait_ge(q_took, t)
                        pe.wait_ge(k_took, t)
                    for h in range(HEADS):
                        nc.tensor.transpose(k.ps[0:MLA_D, 6, h * P:(h + 1) * P], qn[:, t % 2, h, :], k.c("ident"))
                        last = nc.tensor.transpose(k.ps[0:MLA_D, 7, h * P:(h + 1) * P], kn[:, t % 2, h, :], k.c("ident"))
                    last.then_inc(qk_turned, 1)

                for t in range(T):
                    up(t)
                    if t >= 1:
                        turn(t - 1)
                turn(T - 1)

            @block.vector
            def _(dve):
                link = linker(dve, step)
                bcos = bc(cos.unsqueeze(2), P, T, 2, HR)
                bsin = bc(sin.unsqueeze(2), P, T, 2, HR)
                link(nc.vector.tensor_tensor(krot[:, 0], ckr, bcos, ALU.mult))
                link(nc.vector.tensor_tensor(krot[:, 1], ckr, bsin, ALU.mult))
                link(nc.vector.tensor_tensor(kr[:, :, 0, :], krot[:, 0, :, 0, :], krot[:, 1, :, 1, :], ALU.subtract))
                link(nc.vector.tensor_tensor(kr[:, :, 1, :], krot[:, 0, :, 1, :], krot[:, 1, :, 0, :], ALU.add))
                dve.wait_ge(rstd_ready, 2)

                def norm(t):
                    if t >= 2:
                        dve.wait_ge(c_turned, t - 1)
                    nc.vector.scalar_tensor_tensor(cn[:, t % 2, 0:GW], cq[:, t, :], ssq[:, 0, t:t + 1], k.qng[:], ALU.mult, ALU.mult)
                    nc.vector.scalar_tensor_tensor(cn[:, t % 2, GW:], ckv[:, t, :], ssq[:, 1, t:t + 1], k.kvng[:],
                                                   ALU.mult, ALU.mult).then_inc(normed, 1)

                def rotate(t):
                    dve.wait_ge(up_ready, t + 1)
                    if t >= 1:
                        dve.wait_ge(qk_ready, t)
                    if t >= 2:
                        dve.wait_ge(qk_turned, t - 1)
                    q = k.ps[:, 2 + t % 2, 0:HEADS * MLA_D].rearrange("p (h d) -> p h d", h=HEADS)
                    qr = q[:, :, HD:].rearrange("p h (i r) -> p h i r", i=2)
                    nc.vector.tensor_copy(qn[:, t % 2, :, 0:HD], q[:, :, 0:HD])
                    c4 = bc(cos[:, t, :].unsqueeze(1).unsqueeze(1), P, HEADS, 2, HR)
                    s4 = bc(sin[:, t, :].unsqueeze(1).unsqueeze(1), P, HEADS, 2, HR)
                    nc.vector.tensor_tensor(rot[:, 0], qr, c4, ALU.mult)
                    link(nc.vector.tensor_tensor(rot[:, 1], qr, s4, ALU.mult))
                    nc.vector.tensor_tensor(qn[:, t % 2, :, HD:HD + HR], rot[:, 0, :, 0, :], rot[:, 1, :, 1, :], ALU.subtract)
                    nc.vector.tensor_tensor(qn[:, t % 2, :, HD + HR:], rot[:, 0, :, 1, :], rot[:, 1, :, 0, :], ALU.add)
                    nc.vector.tensor_copy(kn[:, t % 2, :, HD:],
                                          bc(kr[:, t].rearrange("p i r -> p (i r)").unsqueeze(1), P, HEADS, ROPE)).then_inc(qk_ready, 1)

                def take(t):
                    dve.wait_ge(qk_turned, t + 1)
                    nc.vector.tensor_copy(k.KT[0:MLA_D, :, t * P:(t + 1) * P],
                                          k.ps[0:MLA_D, 7, :].rearrange("p (h s) -> p h s", h=HEADS)).then_inc(k_took, 1)

                norm(0)
                for t in range(T):
                    if t + 1 < T:
                        norm(t + 1)
                    rotate(t)
                    if t >= 1:
                        take(t - 1)
                take(T - 1)
                dve.wait_ge(q_took, T)


def fox_loads(nc, k, st):
    x_back, zeros_set, spare_filled = st.sem("x_back"), st.sem("zeros_set"), st.sem("spare_filled")
    zeros = st.sb("zeros", [P, D])

    def pool_part(pool):
        nc.gpsimd.memset(zeros[:], 0.0).then_inc(zeros_set, 1)

    def sp_part(sp):
        sp.dma_start(k.x[:], k.d_xs[:, :, :]).then_inc(x_back, 16)
        sp.wait_ge(zeros_set, 1)
        spare = k.d_y[LEAST * P:, :].rearrange("(b p) n -> p b n", p=P)
        sp.dma_start(spare, bc(zeros[:].unsqueeze(1), P, BLOCKS - LEAST, D)).then_inc(spare_filled, 16)
        sp.wait_ge(x_back, 16)
        sp.wait_ge(spare_filled, 16)

    return pool_part, sp_part


def attend(nc, k, who, K, v, mask, chunk0, loads=None):
    units = [(i, h) for i in range(T) for h in range(HEADS)]
    N = len(units)
    with Stage(nc) as st:
        scores, maxed, exped, inv, normed = st.sem("scores"), st.sem("maxed"), st.sem("exped"), st.sem("inv"), st.sem("normed")
        p_turned, pt_act, pt_dve = st.sem("p_turned"), st.sem("pt_act"), st.sem("pt_dve")
        out_ready, out_took = st.sem("out_ready"), st.sem("out_took")
        probs = st.sb(f"probs_{who}", [P, 3, S])
        pT = st.sb(f"pT_{who}", [P, 2, T, P])
        nmax = st.sb(f"nmax_{who}", [P, 2])
        total = st.sb(f"total_{who}", [P, 4])

        groups = []
        for u, (i, h) in enumerate(units):
            for b0 in range(0, i + 1, 4):
                groups.append((u, b0, min(4, i + 1 - b0)))
        before = lambda u: sum(g[0] < u for g in groups)

        def emptied(eng, n):
            if (n + 1) // 2:
                eng.wait_ge(pt_act, (n + 1) // 2)
            if n // 2:
                eng.wait_ge(pt_dve, n // 2)

        def empty(eng, unit, u, par):
            for g in range(before(u), before(u + 1)):
                if g % 2 != par:
                    continue
                _, b0, m = groups[g]
                eng.wait_ge(p_turned, g + 1)
                if u >= 2:
                    eng.wait_ge(out_ready, u - 1)
                src = k.ps[:, 4 + g % 2, 0:m * P].rearrange("p (b s) -> p b s", b=m)
                dst = pT[:, u % 2, b0:b0 + m, :]
                if par == 0:
                    unit.activation(dst, src, ACT.Copy).then_inc(pt_act, 1)
                else:
                    unit.tensor_copy(dst, src).then_inc(pt_dve, 1)

        def row(u, buf):
            nk = (units[u][0] + 1) * P
            return buf[:, 0:nk] if buf is not None else k.ps[:, 2 * (u % 2):2 * (u % 2) + 2, :].rearrange("p b n -> p (b n)")[:, 0:nk]

        beside = loads(nc, k, st) if loads else None
        with nc.Block() as block:
            if beside:
                @block.gpsimd
                def _(pool):
                    beside[0](pool)

                @block.sync
                def _(sp):
                    beside[1](sp)

            @block.tensor
            def _(pe):
                def score(u):
                    i, h = units[u]
                    if u >= 2:
                        pe.wait_ge(exped, u - 1)
                    for n in range(0, i + 1, 4):
                        m = min(4, i + 1 - n)
                        bank = k.ps[:, 2 * (u % 2) + n // 4, :]
                        nc.tensor.matmul(bank[:, 0:m * P], k.QT[0:K, h, i * P:(i + 1) * P], k.KT[0:K, h, n * P:(n + m) * P],
                                         start=True, stop=True)
                    nc.tensor.matmul(bank[:, (m - 1) * P:m * P], k.ident_b[:], mask[:], start=False, stop=True,
                                     skip_group_check=True).then_inc(scores, 1)

                def turn(u):
                    pe.wait_ge(normed, u + 1)
                    for g in range(before(u), before(u + 1)):
                        _, b0, m = groups[g]
                        if g >= 2:
                            emptied(pe, g - 1)
                        for b in range(m):
                            last = nc.tensor.transpose(k.ps[:, 4 + g % 2, b * P:(b + 1) * P],
                                                       probs[:, u % 3, (b0 + b) * P:(b0 + b + 1) * P], k.c("ident"))
                        last.then_inc(p_turned, 1)

                def weigh(u):
                    i, h = units[u]
                    emptied(pe, before(u + 1))
                    if u >= 4 and h % 2 == 0:
                        pe.wait_ge(out_took, u // 2 - 1)
                    r = slice(h % 2 * HD, (h % 2 + 1) * HD)
                    for b in range(i + 1):
                        last = nc.tensor.matmul(k.ps[r, 6 + u // 2 % 2, 0:P], v(b, h), pT[:, u % 2, b, :],
                                                start=(b == 0), stop=(b == i))
                    last.then_inc(out_ready, 1)

                score(0)
                for u in range(N + 2):
                    if u + 1 < N:
                        score(u + 1)
                    if 1 <= u <= N:
                        turn(u - 1)
                    if u >= 2:
                        weigh(u - 2)

            @block.scalar
            def _(act):
                for u in range(N + 4):
                    if u < N:
                        act.wait_ge(maxed, u + 1)
                        if u >= 3:
                            act.wait_ge(p_turned, before(u - 2))
                        nc.scalar.activation(row(u, probs[:, u % 3]), row(u, None), ACT.Exp, bias=nmax[:, u % 2:u % 2 + 1],
                                             accum_out=total[:, u % 4:u % 4 + 1]).then_inc(exped, 1)
                    if 2 <= u < N + 2:
                        empty(act, nc.scalar, u - 2, 0)
                    if u >= 4 and u % 2 == 1:
                        i, h = units[u - 4]
                        act.wait_ge(out_ready, u - 3)
                        nc.scalar.activation(k.yT[:, chunk0 + h // 2, i * P:(i + 1) * P], k.ps[:, 6 + (u - 4) // 2 % 2, 0:P],
                                             ACT.Copy).then_inc(out_took, 1)

            @block.vector
            def _(dve):
                def normalise(u):
                    dve.wait_ge(exped, u + 1)
                    t = total[:, u % 4:u % 4 + 1]
                    nc.vector.reciprocal(t, t).then_inc(inv, 1)
                    dve.wait_ge(inv, u + 1)
                    r = row(u, probs[:, u % 3])
                    nc.vector.tensor_scalar(r, r, t, None, ALU.mult).then_inc(normed, 1)

                for u in range(N + 2):
                    if u < N:
                        dve.wait_ge(scores, u + 1)
                        if u >= 2:
                            dve.wait_ge(exped, u - 1)
                        nc.vector.tensor_reduce(nmax[:, u % 2:u % 2 + 1], row(u, None), AX, ALU.max, negate=True).then_inc(maxed, 1)
                    if 1 <= u <= N:
                        normalise(u - 1)
                    if u >= 2:
                        empty(dve, nc.vector, u - 2, 1)


def ssd(nc, k):
    with Stage(nc) as st:
        bx_turned, b_took, xs_ready = st.sem("bx_turned"), st.sem("b_took"), st.sem("xs_ready")
        cuts_ready, gd_ready, exped, m_ready = st.sem("cuts_ready"), st.sem("gd_ready"), st.sem("exped"), st.sem("m_ready")
        y_ready, state_ready, step, y_took = st.sem("y_ready"), st.sem("state_ready"), st.sem("ssd_step"), st.sem("y_took")
        yn_ready, yn_turned, yt_took, zeroed = st.sem("yn_ready"), st.sem("yn_turned"), st.sem("yt_took"), st.sem("zeroed")
        cleared, apart = st.sem("cleared"), st.sem("apart")
        squared, rstd_step, rstd_ready = st.sem("squared"), st.sem("rstd_step"), st.sem("rstd_ready")
        Bn = st.sb("Bn", [P, 2, P])
        xdt = st.sb("xdt", [P, 2, HEADS, HD])
        xds = st.sb("xds", [P, 2, HEADS, HD])
        skip = st.sb("skip", [P, 2, HEADS, HD])
        cuts = st.sb("cuts", [P, 2, HEADS, P])
        eD = st.sb("eD", [P, 2, HEADS, P])
        M = st.sb("M", [P, 2, HEADS, P])
        Cg = st.sb("Cg", [P, 2, 2, P])
        prev = st.sb("prev", [P, 2, HEADS, HD])
        yc = st.sb("yc", [P, 3, HEADS, HD])
        ssq = st.sb("ssq3", [P, T])
        junk = st.sb("junk3", [P, GW])
        gt4 = bc(k.c("gt").unsqueeze(1), P, HEADS, P)

        def col(ap):
            return bc(ap.unsqueeze(2), P, HEADS, HD)

        with nc.Block() as block:
            @block.gpsimd
            def _(pool):
                link = linker(pool, rstd_step)
                nc.gpsimd.memset(Cg[:], 0.0).then_inc(cleared, 1)
                pool.wait_ge(cleared, 1)
                for c in range(T + 2):
                    if 2 <= c < T:
                        pool.wait_ge(gd_ready, c - 1)
                    if 3 <= c < T:
                        pool.wait_ge(rstd_ready, c - 2)
                    if c < T:
                        for g in range(2):
                            r = slice(g * STATE, (g + 1) * STATE)
                            nc.gpsimd.tensor_copy(Cg[r, c % 2, g, :], k.xbcT[r, 3, c * P:(c + 1) * P]).then_inc(apart, 1)
                    if c >= 2:
                        pool.wait_ge(apart, 2 * min(c + 1, T))
                        pool.wait_ge(squared, c - 1)
                        rstd(nc, k, link, ssq[:, c - 2:c - 1], GW).then_inc(rstd_ready, 1)

            @block.tensor
            def _(pe):
                def front(c):
                    s = slice(c * P, (c + 1) * P)
                    if c >= 1:
                        pe.wait_ge(b_took, c)
                        pe.wait_ge(xs_ready, c)
                    for bank, n, j in ((0, 0, 0), (0, 1, 1), (1, 0, 2)):
                        last = nc.tensor.transpose(k.ps[:, bank, n * P:(n + 1) * P], k.xbcT[:, j, s], k.c("ident"))
                    last.then_inc(bx_turned, 1)
                    pe.wait_ge(cuts_ready, c + 1)
                    if c >= 1:
                        pe.wait_ge(m_ready, c)
                    pe.wait_ge(apart, 2 * (c + 1))
                    nc.tensor.matmul(k.ps[:, 2, 0:2 * P], k.xbcT[:, 2, s], Cg[:, c % 2].rearrange("p g s -> p (g s)"),
                                     start=True, stop=True)
                    for h in range(HEADS):
                        nc.tensor.matmul(k.ps[:, 3 + c % 2, h * P:(h + 1) * P], cuts[:, c % 2, h, :], k.c("le"),
                                         start=(h == 0), stop=False, skip_group_check=True)
                    nc.tensor.matmul(k.ps[:, 3 + c % 2, :], k.ident_b[:], k.mask_ssd[:],
                                     start=False, stop=True, skip_group_check=True).then_inc(gd_ready, 1)

                def back(c):
                    s = slice(c * P, (c + 1) * P)
                    pe.wait_ge(m_ready, c + 1)
                    if c == 0:
                        pe.wait_ge(zeroed, 1)
                    else:
                        pe.wait_ge(y_took, c)
                    for h in range(HEADS):
                        nc.tensor.matmul(k.ps[:, 5, h * HD:(h + 1) * HD], M[:, c % 2, h, :], xdt[:, c % 2, h, :], start=True, stop=True)
                    nc.tensor.matmul(k.ps[:, 5, GW:], k.xbcT[:, 3, s], prev[:, c % 2].rearrange("p h d -> p (h d)"), start=True, stop=True)
                    last = nc.tensor.matmul(k.ps[:, 6, 0:GW], Bn[:, c % 2], xds[:, c % 2].rearrange("p h d -> p (h d)"), start=True, stop=True)
                    last.then_inc(y_ready, 1)

                def turn_y(c):
                    pe.wait_ge(yn_ready, c + 1)
                    if c >= 1:
                        pe.wait_ge(yt_took, c)
                    for j in range(2):
                        last = nc.tensor.transpose(k.ps[:, 7, j * P:(j + 1) * P],
                                                   yc[:, c % 3].rearrange("p h d -> p (h d)")[:, j * P:(j + 1) * P], k.c("ident"))
                    last.then_inc(yn_turned, 1)

                front(0)
                for c in range(T):
                    if c + 1 < T:
                        front(c + 1)
                    back(c)
                    if c >= 2:
                        turn_y(c - 2)
                turn_y(T - 2)
                turn_y(T - 1)

            @block.scalar
            def _(act):
                def take_yt(c):
                    act.wait_ge(yn_turned, c + 1)
                    nc.scalar.activation(k.yT[:, 2:4, c * P:(c + 1) * P], k.ps[:, 7, 0:2 * P].rearrange("p (j s) -> p j s", j=2),
                                         ACT.Copy).then_inc(yt_took, 1)

                for c in range(T):
                    act.wait_ge(bx_turned, c + 1)
                    if c >= 2:
                        act.wait_ge(y_ready, c - 1)
                    nc.scalar.activation(Bn[:, c % 2, :], k.ps[:, 1, 0:P], ACT.Copy).then_inc(b_took, 1)
                    act.wait_ge(gd_ready, c + 1)
                    if c >= 2:
                        act.wait_ge(m_ready, c - 1)
                    nc.scalar.activation(eD[:, c % 2], k.ps[:, 3 + c % 2, :].rearrange("p (h s) -> p h s", h=HEADS), ACT.Exp).then_inc(exped, 1)
                    if c >= 3:
                        take_yt(c - 3)
                for c in range(T - 3, T):
                    take_yt(c)

            @block.vector
            def _(dve):
                link = linker(dve, step)
                nc.vector.memset(prev[:], 0.0).then_inc(zeroed, 1)

                def front(c):
                    if c >= 2:
                        dve.wait_ge(gd_ready, c - 1)
                    nc.vector.tensor_tensor(cuts[:, c % 2], gt4, bc(k.adec[:, c, :].unsqueeze(2), P, HEADS, P), ALU.mult).then_inc(cuts_ready, 1)
                    dve.wait_ge(bx_turned, c + 1)
                    xs = k.ps[:, 0, 0:2 * P].rearrange("p (h d) -> p h d", h=HEADS)
                    if c >= 2:
                        dve.wait_ge(y_ready, c - 1)
                    link(nc.vector.tensor_tensor(xdt[:, c % 2], xs, col(k.dt[:, c, :]), ALU.mult))
                    nc.vector.tensor_tensor(xds[:, c % 2], xdt[:, c % 2], col(k.decay[:, 1, c * HEADS:(c + 1) * HEADS]), ALU.mult)
                    nc.vector.tensor_tensor(skip[:, c % 2], xs, col(k.dskip[:]), ALU.mult).then_inc(xs_ready, 1)
                    dve.wait_ge(exped, c + 1)
                    gg = k.ps[:, 2, 0:2 * P].rearrange("p (g s) -> p g s", g=2)
                    nc.vector.tensor_tensor(M[:, c % 2].rearrange("p (g j) s -> p g j s", g=2),
                                            eD[:, c % 2].rearrange("p (g j) s -> p g j s", g=2),
                                            bc(gg.unsqueeze(2), P, 2, 2, P), ALU.mult).then_inc(m_ready, 1)

                def back(c):
                    dve.wait_ge(y_ready, c + 1)
                    dve.wait_ge(zeroed, 1)
                    for h in range(HEADS):
                        r = slice(h // 2 * STATE, (h // 2 + 1) * STATE)
                        link(nc.vector.scalar_tensor_tensor(prev[r, (c + 1) % 2, h, :], prev[r, c % 2, h, :], k.carry[r, c, h % 2:h % 2 + 1],
                                                            k.ps[r, 6, h * HD:(h + 1) * HD], ALU.mult, ALU.add))
                    if c >= 3:
                        dve.wait_ge(yn_turned, c - 2)
                    yv = yc[:, c % 3]
                    link(nc.vector.tensor_tensor(yv, k.ps[:, 5, GW:].rearrange("p (h d) -> p h d", h=HEADS),
                                                 col(k.decay[:, 0, c * HEADS:(c + 1) * HEADS]), ALU.mult))
                    nc.vector.tensor_tensor(yv, yv, k.ps[:, 5, 0:GW].rearrange("p (h d) -> p h d", h=HEADS), ALU.add).then_inc(y_took, 1)
                    dve.wait_ge(y_took, c + 1)
                    link(nc.vector.tensor_tensor(yv, yv, skip[:, c % 2], ALU.add))
                    flat = yv.rearrange("p h d -> p (h d)")
                    link(nc.vector.tensor_tensor(flat, flat, k.z[:, c, :], ALU.mult))
                    if c >= 1:
                        dve.wait_ge(squared, c)
                    nc.vector.tensor_tensor_reduce(junk[:], flat, flat, 1.0, 0.0, ALU.mult, ALU.add, ssq[:, c:c + 1]).then_inc(squared, 1)

                def norm(c):
                    flat = yc[:, c % 3].rearrange("p h d -> p (h d)")
                    dve.wait_ge(rstd_ready, c + 1)
                    nc.vector.scalar_tensor_tensor(flat, flat, ssq[:, c:c + 1], k.sng[:], ALU.mult, ALU.mult).then_inc(yn_ready, 1)

                front(0)
                for c in range(T):
                    if c + 1 < T:
                        front(c + 1)
                    back(c)
                    if c >= 1:
                        norm(c - 1)
                norm(T - 1)


def join(nc, k, l):
    with Stage(nc) as st:
        w_in, gain_in = st.sem("w_out_in"), st.sem("gain_in")
        o_ready, x_ready, sq, step = st.sem("o_ready"), st.sem("x_ready"), st.sem("sq"), st.sem("join_step")
        h_ready, h_stored, turned, ht_ready, lg_ready, lg_took = (st.sem("h_ready"), st.sem("h_stored"), st.sem("turned"),
                                                         st.sem("ht_ready"), st.sem("lg_ready"), st.sem("lg_took"))
        wo = k.QK[:].rearrange("p a h s -> p (a h s)").rearrange("p (c n) -> p c n", c=KD)
        h = k.over[:, 0:2 * D].rearrange("p (b n) -> p b n", b=2)
        hT2 = k.over[:, 2 * D:4 * D].rearrange("p (b c s) -> p b c s", b=2, c=KD)
        junk = k.over[:, 4 * D:5 * D]
        rstd_ready = st.sem("rstd_ready")
        ssq = st.sb("ssq4", [P, T])

        def yT(c, t):
            src = k.yA[:, c] if c < 2 else k.yT[:, c - 2]
            return src[:, t * P:(t + 1) * P]

        with nc.Block() as block:
            @block.gpsimd
            def _(pool):
                link = linker(pool, step)
                for t in range(T):
                    pool.wait_ge(sq, t + 1)
                    rstd(nc, k, link, ssq[:, t:t + 1], D).then_inc(rstd_ready, 1)

            @block.sync
            def _(sp):
                sp.dma_start(k.gain[:], bc(k.norm_ffn[bass.ds(l, 1), :], P, D)).then_inc(gain_in, 16)
                sp.dma_start(wo, k.w_out[bass.ds(l, 1)].rearrange("a (c p) n -> p (a c) n", p=P)).then_inc(w_in, 16)
                for t in range(T):
                    sp.wait_ge(h_ready, t + 1)
                    sp.dma_start(k.d_h[t * P:(t + 1) * P, :], h[:, t % 2, :]).then_inc(h_stored, 16)
                    if t + 1 == T:
                        sp.wait_ge(h_stored, 16 * T)

            @block.tensor
            def _(pe):
                pe.wait_ge(w_in, 16)

                def router(t):
                    pe.wait_ge(h_ready, t + 1)
                    if t >= 1:
                        pe.wait_ge(ht_ready, 2 * t)
                    for c in range(KD):
                        last = nc.tensor.transpose(k.ps[:, 4 + c // 4, (c % 4) * P:(c % 4 + 1) * P], h[:, t % 2, c * P:(c + 1) * P],
                                                   k.c("ident"))
                    last.then_inc(turned, 1)
                    pe.wait_ge(ht_ready, 2 * (t + 1))
                    if t >= 1:
                        pe.wait_ge(lg_took, t)
                    for c in range(KD):
                        last = nc.tensor.matmul(k.ps[:, 6, 0:G + E], hT2[:, t % 2, c, :], k.rw[:, c, :], start=(c == 0), stop=(c == KD - 1))
                    last.then_inc(lg_ready, 1)

                for t in range(T):
                    if t >= 2:
                        pe.wait_ge(x_ready, t - 1)
                    for n in range(2):
                        for c in range(KD):
                            last = nc.tensor.matmul(k.ps[:, 2 * (t % 2) + n, :], yT(c, t), wo[:, c, n * HALF:(n + 1) * HALF],
                                                    start=(c == 0), stop=(c == KD - 1))
                    last.then_inc(o_ready, 1)
                    if t >= 1:
                        router(t - 1)
                router(T - 1)

            @block.scalar
            def _(act):
                for t in range(T):
                    act.wait_ge(x_ready, t + 1)
                    if t >= 1:
                        act.wait_ge(sq, t)
                    nc.scalar.activation(junk, k.x[:, t, :], ACT.Square, accum_out=ssq[:, t:t + 1]).then_inc(sq, 1)
                    act.wait_ge(turned, t + 1)
                    for n in range(2):
                        if t >= 2:
                            act.wait_ge(lg_ready, t - 1)
                        nc.scalar.activation(hT2[:, t % 2, 4 * n:4 * n + 4, :], k.ps[:, 4 + n, :].rearrange("p (c s) -> p c s", c=4),
                                             ACT.Copy).then_inc(ht_ready, 1)

            @block.vector
            def _(dve):
                dve.wait_ge(gain_in, 16)
                for t in range(T + 1):
                    if t < T:
                        dve.wait_ge(o_ready, t + 1)
                        nc.vector.tensor_tensor(k.x[:, t, :], k.x[:, t, :],
                                                k.ps[:, 2 * (t % 2):2 * (t % 2) + 2, :].rearrange("p b n -> p (b n)"),
                                                ALU.add).then_inc(x_ready, 1)
                    if t >= 1:
                        dve.wait_ge(lg_ready, t)
                        nc.vector.tensor_tensor(k.logits[:, t - 1, :], k.ps[:, 6, 0:G + E], k.rb[:], ALU.add).then_inc(lg_took, 1)
                    if t < T:
                        dve.wait_ge(rstd_ready, t + 1)
                        if t >= 2:
                            dve.wait_ge(h_stored, 16 * t)
                            dve.wait_ge(turned, t - 1)
                        nc.vector.scalar_tensor_tensor(h[:, t % 2, :], k.x[:, t, :], ssq[:, t:t + 1], k.gain[:],
                                                       ALU.mult, ALU.mult).then_inc(h_ready, 1)


def route(nc, k):
    with Stage(nc) as st:
        step, exp_in, exp_out, sel_ready, ranks_ready, hot_ready, rows_ready = (
            st.sem("route_step"), st.sem("exp_in"), st.sem("exp_out"), st.sem("sel_ready"), st.sem("ranks_ready"),
            st.sem("hot_ready"), st.sem("rows_ready"))
        gm, gs, gx, m1, m2, ss, e2, den = (st.sb(f"tok{i}", [P, T]) for i in range(8))
        gd, goh = st.sb("gd", [P, T, G]), st.sb("goh", [P, T, G])
        el, el2, o1, o2, t8 = (st.sb(f"exp{i}", [P, T, EG]) for i in range(5))
        big = st.sb("big", [P, T, G, EG])
        M1, M2, MM = (st.sb(f"sel{i}", [P, T, G, EG]) for i in range(3))
        R = st.sb("R", [P, T, E])
        base = st.sb("base", [P, T, E])
        cnt, nb, pe_, start = (st.sb(f"cnt{i}", [P, E]) for i in range(4))
        ni = st.sb("ni", [P, E], I32)
        pmi, pbi = st.sb("pmi", [P, T, 2], I32), st.sb("pbi", [P, T, 2], I32)
        cmp = st.sb("cmp", [P, BLK, E])
        pos = st.sb("pos", [P, T, 2])
        pm, pb = st.sb("pm", [P, T, 2]), st.sb("pb", [P, T, 2])
        hotp = st.sb("hotp", [P, T, 2, P])
        hotb = st.sb("hotb", [P, T, 2, BLK])
        be = st.sb("be", [P, BLK])
        lgG = k.logits[:, :, 0:G]
        lgE = k.logits[:, :, G:].rearrange("p t (g e) -> p t g e", g=G)

        with nc.Block() as block:
            @block.scalar
            def _(act):
                act.wait_ge(exp_in, 1)
                nc.scalar.activation(gd[:], gd[:], ACT.Exp).then_inc(exp_out, 1)
                act.wait_ge(exp_in, 2)
                nc.scalar.activation(t8[:], t8[:], ACT.Exp).then_inc(exp_out, 1)
                act.wait_ge(exp_in, 3)
                nc.scalar.activation(e2[:], e2[:], ACT.Exp).then_inc(exp_out, 1)

            @block.tensor
            def _(pe):
                pe.wait_ge(sel_ready, 1)
                flat = MM[:].rearrange("p t g e -> p (t g e)")
                nc.tensor.matmul(k.ps[:, 0, 0:T * E], k.c("lt"), flat, start=True, stop=True)
                nc.tensor.matmul(k.ps[:, 1, 0:T * E], k.c("ones"), flat, start=True, stop=True).then_inc(ranks_ready, 1)
                pe.wait_ge(hot_ready, 1)
                n = 0
                for t in range(T):
                    for i in range(2):
                        last = nc.tensor.matmul(k.ps[:, 2, 0:BLK], hotp[:, t, i, :], hotb[:, t, i, :], start=(n == 0), stop=(n == 2 * T - 1))
                        n += 1
                last.then_inc(rows_ready, 1)

            @block.vector
            def _(dve):
                link = linker(dve, step)
                V = nc.vector

                def b3(a, n):
                    return bc(a.unsqueeze(2), P, T, n)

                def pick(dst, val, best, rank, n, tmp):
                    link(V.tensor_tensor(tmp, val, b3(best, n), ALU.is_equal))
                    link(V.tensor_tensor(tmp, tmp, bc(rank.unsqueeze(1), P, T, n), ALU.mult))
                    link(V.tensor_reduce(gx[:], tmp, AX, ALU.max))
                    link(V.tensor_tensor(dst, tmp, b3(gx[:], n), ALU.is_equal))

                link(V.tensor_reduce(gm[:], lgG, AX, ALU.max))
                pick(goh[:], lgG, gm[:], k.c("rank4"), G, gd[:])
                V.tensor_tensor(gd[:], lgG, b3(gm[:], G), ALU.subtract).then_inc(exp_in, 1)
                link(V.tensor_tensor(big[:], lgE, bc(goh[:].unsqueeze(3), P, T, G, EG), ALU.mult))
                link(V.tensor_reduce(el[:], big[:].rearrange("p t g e -> p t e g"), AX, ALU.add))
                link(V.tensor_reduce(m1[:], el[:], AX, ALU.max))
                pick(o1[:], el[:], m1[:], k.c("rank8"), EG, t8[:])
                link(V.scalar_tensor_tensor(el2[:], o1[:], NEG, el[:], ALU.mult, ALU.add))
                link(V.tensor_reduce(m2[:], el2[:], AX, ALU.max))
                pick(o2[:], el2[:], m2[:], k.c("rank8"), EG, t8[:])
                V.tensor_tensor(t8[:], el[:], b3(m1[:], EG), ALU.subtract).then_inc(exp_in, 1)
                V.tensor_tensor(e2[:], m2[:], m1[:], ALU.subtract).then_inc(exp_in, 1)
                dve.wait_ge(exp_out, 1)
                link(V.tensor_reduce(gs[:], gd[:], AX, ALU.add))
                link(V.reciprocal(gs[:], gs[:]))
                dve.wait_ge(exp_out, 3)
                link(V.tensor_reduce(ss[:], t8[:], AX, ALU.add))
                link(V.reciprocal(ss[:], ss[:]))
                link(V.tensor_tensor(e2[:], e2[:], ss[:], ALU.mult))
                link(V.tensor_tensor(den[:], e2[:], ss[:], ALU.add))
                link(V.reciprocal(den[:], den[:]))
                link(V.tensor_tensor(den[:], den[:], gs[:], ALU.mult))
                V.tensor_tensor(k.wts[:, :, 0], ss[:], den[:], ALU.mult)
                V.tensor_tensor(k.wts[:, :, 1], e2[:], den[:], ALU.mult)
                for o, m in ((o1, M1), (o2, M2)):
                    link(V.tensor_tensor(m[:], bc(goh[:].unsqueeze(3), P, T, G, EG), bc(o[:].unsqueeze(2), P, T, G, EG), ALU.mult))
                V.tensor_tensor(MM[:], M1[:], M2[:], ALU.add).then_inc(sel_ready, 1)
                dve.wait_ge(ranks_ready, 1)
                tot = k.ps[:, 1, 0:T * E].rearrange("p (t e) -> p t e", t=T)
                link(V.tensor_reduce(cnt[:], tot.rearrange("p t e -> p e t"), AX, ALU.add))
                link(V.tensor_scalar(ni[:], cnt[:], float(P - 1), None, ALU.add))
                link(V.tensor_scalar(ni[:], ni[:], LOG_P, None, ALU.arith_shift_right))
                link(V.tensor_copy(nb[:], ni[:]))
                first = k.c("iota")[:, 0:E]
                link(V.tensor_tensor(cmp[:, 0:E, :], bc(first.unsqueeze(1), P, E, E), bc(first.unsqueeze(2), P, E, E), ALU.is_le))
                link(V.tensor_tensor(cmp[:, 0:E, :], cmp[:, 0:E, :], bc(nb[:].unsqueeze(1), P, E, E), ALU.mult))
                link(V.tensor_reduce(pe_[:], cmp[:, 0:E, :], AX, ALU.add))
                link(V.tensor_tensor(start[:], pe_[:], nb[:], ALU.subtract))
                link(V.tensor_scalar(base[:, 0, :], start[:], float(P), None, ALU.mult))
                for t in range(1, T):
                    link(V.tensor_tensor(base[:, t, :], base[:, t - 1, :], tot[:, t - 1, :], ALU.add))
                link(V.tensor_tensor(R[:], base[:], k.ps[:, 0, 0:T * E].rearrange("p (t e) -> p t e", t=T), ALU.add))
                for i, m in enumerate((M1, M2)):
                    mf = m[:].rearrange("p t g e -> p t (g e)")
                    link(V.tensor_tensor(mf, mf, R[:], ALU.mult))
                    link(V.tensor_reduce(pos[:, :, i:i + 1], mf, AX, ALU.add))
                link(V.tensor_copy(k.pos_i[:], pos[:]))
                link(V.tensor_scalar(pmi[:], k.pos_i[:], P - 1, None, ALU.bitwise_and))
                link(V.tensor_scalar(pbi[:], k.pos_i[:], LOG_P, None, ALU.arith_shift_right))
                link(V.tensor_copy(pm[:], pmi[:]))
                link(V.tensor_copy(pb[:], pbi[:]))
                iota = k.c("iota")
                link(V.tensor_tensor(hotp[:], bc(iota.unsqueeze(1).unsqueeze(1), P, T, 2, P), bc(pm[:].unsqueeze(3), P, T, 2, P), ALU.is_equal))
                link(V.tensor_tensor(hotb[:], bc(iota[:, 0:BLK].unsqueeze(1).unsqueeze(1), P, T, 2, BLK), bc(pb[:].unsqueeze(3), P, T, 2, BLK),
                                     ALU.is_equal))
                V.tensor_tensor(hotb[:], hotb[:], bc(k.c("token").unsqueeze(2).unsqueeze(3), P, T, 2, BLK), ALU.mult).then_inc(hot_ready, 1)
                link(V.tensor_tensor(cmp[:], bc(pe_[:].unsqueeze(1), P, BLK, E), bc(iota[:, 0:BLK].unsqueeze(2), P, BLK, E), ALU.is_le))
                link(V.tensor_reduce(be[:], cmp[:], AX, ALU.add))
                link(V.tensor_scalar(be[:], be[:], float(E - 1), None, ALU.min))
                V.tensor_copy(k.expert_i[:], be[:])
                link(V.tensor_scalar(k.npair_i[:], pe_[:, E - 1:E], 1.0, None, ALU.add))
                link(V.tensor_scalar(k.npair_i[:], k.npair_i[:], 1, None, ALU.arith_shift_right))
                dve.wait_ge(rows_ready, 1)
                link(V.tensor_copy(k.rows_i[:], k.ps[:, 2, 0:BLK]))


def wait_past(eng, sem, value):
    if not isinstance(value, int) or value > 0:
        eng.wait_ge(sem, value)


def experts(nc, k, l):
    with Stage(nc, pool_dmas=True) as st:
        idx_ready = st.sem("idx_ready")
        x_in = [st.sem("x_in0"), st.sem("x_in1")]
        gu_in = [st.sem("gu_in0"), st.sem("gu_in1")]
        dn_in = [st.sem("dn_in0"), st.sem("dn_in1")]
        x_turned, xt_ready, gu_ready, silued, h_ready = (st.sem("x_turned"), st.sem("xt_ready"), st.sem("gu_ready"),
                                                         st.sem("silued"), st.sem("h_ready"))
        h_turned, ht_ready, y_ready, y_act, y_dve = (st.sem("h_turned"), st.sem("ht_ready"), st.sem("y_ready"), st.sem("y_act"),
                                                     st.sem("y_dve"))
        y_out = [st.sem("y_out0"), st.sem("y_out1")]
        all_stored, gather_due = st.sem("all_stored"), st.sem("gather_due")
        idx = st.sb("idx", [P, 2], I32)
        xg = st.sb("xg", [P, 2, D])
        xT = st.sb("xT", [P, 2, KD, P])
        wgu = st.sb("wgu", [P, 2, KD, 2 * FF])
        wd = st.sb("wd", [P, 2, 2, D])
        sg = st.sb("sg", [P, 2, FF])
        hh = st.sb("hh", [P, 2, FF])
        hT = st.sb("hT_ff", [P, 2, 2, P])
        y = st.sb("y_out", [P, 2, D])

        def turns(eng, turn):
            n = eng.value_load(k.npair_i[0:1, 0:1], min_val=LEAST // 2, max_val=BLOCKS // 2)
            turn(0)
            with eng.Fori(1, n) as p:
                turn(p)
            return n

        def column(table, b):
            return table[:, b:b + 1] if isinstance(b, int) else table[:, bass.ds(b, 1)]

        with nc.Block() as block:
            @block.gpsimd
            def _(pool):
                def gather(s, b):
                    nc.gpsimd.tensor_copy(idx[:, s:s + 1], column(k.rows_i, b)).then_inc(idx_ready, 1)
                    pool.wait_ge(idx_ready, b + 1)
                    pool.sem_inc(gather_due, 1)
                    pool.indirect_dma_start(xg[:, s, :], None, k.d_h[:, :],
                                            bass.IndirectOffsetOnAxis(idx[:, s:s + 1], axis=0)).then_inc(x_in[s], 16)

                def turn(p):
                    for s in range(2):
                        b = p * 2 + s
                        wait_past(pool, x_turned, b)
                        gather(1 - s, b + 1)

                gather(0, 0)
                n = turns(pool, turn)
                for s in range(2):
                    pool.wait_ge(x_in[s], (n + 1 - s) * 16)
                    pool.sem_inc(gather_due, 1)

            @block.sync
            def _(sp):
                def turn(p):
                    for s in range(2):
                        b = p * 2 + s
                        e = sp.value_load(column(k.expert_i[0:1, :], b), min_val=0, max_val=E - 1)
                        w = bass.ds(l * E + e, 1)
                        wait_past(sp, gu_ready, b - 1)
                        sp.dma_start(wgu[:, s, :, 0:FF], k.w_gate[w].rearrange("a (c p) n -> p (a c) n", p=P)).then_inc(gu_in[s], 16)
                        sp.dma_start(wgu[:, s, :, FF:], k.w_up[w].rearrange("a (c p) n -> p (a c) n", p=P)).then_inc(gu_in[s], 16)
                        wait_past(sp, y_ready, b - 1)
                        sp.dma_start(wd[:, s], k.w_down[w].rearrange("a (c p) n -> p (a c) n", p=P)).then_inc(dn_in[s], 16)

                turns(sp, turn)

            @block.tensor
            def _(pe):
                def turn_x(s, nth, b):
                    pe.wait_ge(x_in[s], nth * 16)
                    wait_past(pe, xt_ready, b * 2)
                    for c in range(KD):
                        last = nc.tensor.transpose(k.ps[:, c // 4, (c % 4) * P:(c % 4 + 1) * P], xg[:, s, c * P:(c + 1) * P], k.c("ident"))
                    last.then_inc(x_turned, 1)

                def down(s, nth, b):
                    pe.wait_ge(ht_ready, b + 1)
                    pe.wait_ge(dn_in[s], nth * 16)
                    pe.wait_ge(y_act, b + 1)
                    pe.wait_ge(y_dve, b + 1)
                    for m in range(2):
                        for c in range(2):
                            last = nc.tensor.matmul(k.ps[:, 5 + m, :], hT[:, s, c, :], wd[:, s, c, m * HALF:(m + 1) * HALF],
                                                    start=(c == 0), stop=(c == 1))
                    last.then_inc(y_ready, 1)

                def turn(p):
                    for s in range(2):
                        b = p * 2 + s
                        pe.wait_ge(gu_in[s], p * 32 + 32)
                        pe.wait_ge(xt_ready, b * 2 + 2)
                        for c in range(KD):
                            last = nc.tensor.matmul(k.ps[:, 2 + s, :], xT[:, s, c, :], wgu[:, s, c, :], start=(c == 0), stop=(c == KD - 1))
                        last.then_inc(gu_ready, 1)
                        turn_x(1 - s, p + 1 + s, b + 1)
                        if not (isinstance(b, int) and b == 0):
                            down(1 - s, p + s, b - 1)
                        pe.wait_ge(h_ready, b + 1)
                        for c in range(2):
                            last = nc.tensor.transpose(k.ps[:, 4, c * P:(c + 1) * P], hh[:, s, c * P:(c + 1) * P], k.c("ident"))
                        last.then_inc(h_turned, 1)

                turn_x(0, 1, 0)
                n = turns(pe, turn)
                down(1, n, n * 2 - 1)

            @block.scalar
            def _(act):
                def take_x(s, b):
                    act.wait_ge(x_turned, b + 1)
                    for m in range(2):
                        nc.scalar.activation(xT[:, s, 4 * m:4 * m + 4, :], k.ps[:, m, :].rearrange("p (c s) -> p c s", c=4),
                                             ACT.Copy).then_inc(xt_ready, 1)

                def store(s, nth, b):
                    act.wait_ge(y_ready, b + 1)
                    act.wait_ge(y_out[s], nth * 16)
                    nc.scalar.activation(y[:, s, 0:HALF], k.ps[:, 5, :], ACT.Copy).then_inc(y_act, 1)
                    act.wait_ge(y_act, b + 2)
                    act.wait_ge(y_dve, b + 2)
                    rows = k.d_y[b * P:(b + 1) * P, :] if isinstance(b, int) else k.d_y[bass.ds(b * P, P), :]
                    act.dma_start(rows, y[:, s, :]).then_inc(y_out[s], 16)

                def turn(p):
                    for s in range(2):
                        b = p * 2 + s
                        act.wait_ge(gu_ready, b + 1)
                        nc.scalar.activation(sg[:, s, :], k.ps[:, 2 + s, 0:FF], ACT.Silu).then_inc(silued, 1)
                        take_x(1 - s, b + 1)
                        if not (isinstance(b, int) and b == 0):
                            store(1 - s, p + s, b - 1)
                        act.wait_ge(h_turned, b + 1)
                        nc.scalar.activation(hT[:, s], k.ps[:, 4, 0:2 * P].rearrange("p (c s) -> p c s", c=2), ACT.Copy).then_inc(ht_ready, 1)

                act.sem_inc(y_act, 1)
                act.sem_inc(y_out[0], 16)
                act.sem_inc(y_out[1], 16)
                take_x(0, 0)
                n = turns(act, turn)
                store(1, n, n * 2 - 1)
                for s in range(2):
                    act.wait_ge(y_out[s], n * 16 + 16)
                    act.sem_inc(all_stored, 1)
                act.wait_ge(all_stored, 2)

            @block.vector
            def _(dve):
                def take_y(s, nth, b):
                    dve.wait_ge(y_ready, b + 1)
                    dve.wait_ge(y_out[s], nth * 16)
                    nc.vector.tensor_copy(y[:, s, HALF:], k.ps[:, 6, :]).then_inc(y_dve, 1)

                def turn(p):
                    for s in range(2):
                        b = p * 2 + s
                        dve.wait_ge(silued, b + 1)
                        nc.vector.tensor_tensor(hh[:, s, :], sg[:, s, :], k.ps[:, 2 + s, FF:], ALU.mult).then_inc(h_ready, 1)
                        if not (isinstance(b, int) and b == 0):
                            take_y(1 - s, p + s, b - 1)

                dve.sem_inc(y_dve, 1)
                n = turns(dve, turn)
                take_y(1, n, n * 2 - 1)


def combine(nc, k):
    with Stage(nc, pool_dmas=True) as st:
        y_in = [st.sem(f"y_in{i}") for i in range(4)]
        first, added = st.sem("first"), st.sem("added")
        yg = st.sb("yg", [P, 4, D])
        with nc.Block() as block:
            @block.gpsimd
            def _(pool):
                for n in range(2 * T):
                    t, i = n // 2, n % 2
                    if n >= 4:
                        pool.wait_ge((first, added)[i], t - 1)
                    pool.indirect_dma_start(yg[:, n % 4, :], None, k.d_y[:, :],
                                            bass.IndirectOffsetOnAxis(k.pos_i[:, t, i:i + 1], axis=0)).then_inc(y_in[n % 4], 16)
                for n in range(4):
                    pool.wait_ge(y_in[n], 16 * (2 * T // 4))

            @block.vector
            def _(dve):
                for n in range(2 * T):
                    t, i = n // 2, n % 2
                    dve.wait_ge(y_in[n % 4], 16 * (n // 4 + 1))
                    if i:
                        dve.wait_ge(first, t + 1)
                    nc.vector.scalar_tensor_tensor(k.x[:, t, :], yg[:, n % 4, :], k.wts[:, t, i:i + 1], k.x[:, t, :],
                                                   ALU.mult, ALU.add).then_inc((first, added)[i], 1)
                dve.wait_ge(added, T)


def final(nc, k):
    with Stage(nc) as st:
        gain_in, sq, step, ready, stored = st.sem("gain_in"), st.sem("sq"), st.sem("final_step"), st.sem("ready"), st.sem("stored")
        rstd_ready = st.sem("rstd_ready")
        ssq = st.sb("ssq5", [P, T])
        junk = st.sb("junk5", [P, 2, D])
        out = k.out.rearrange("b (t p) n -> p (b t) n", p=P)
        with nc.Block() as block:
            @block.gpsimd
            def _(pool):
                link = linker(pool, step)
                for t in range(T):
                    pool.wait_ge(sq, t + 1)
                    rstd(nc, k, link, ssq[:, t:t + 1], D).then_inc(rstd_ready, 1)

            @block.sync
            def _(sp):
                sp.dma_start(k.gain[:], bc(k.norm_final.unsqueeze(0), P, D)).then_inc(gain_in, 16)
                for t in range(T):
                    sp.wait_ge(ready, t + 1)
                    sp.dma_start(out[:, t, :], k.x[:, t, :]).then_inc(stored, 16)
                sp.wait_ge(stored, 16 * T)

            @block.scalar
            def _(act):
                for t in range(T):
                    if t >= 2:
                        act.wait_ge(sq, t - 1)
                    nc.scalar.activation(junk[:, t % 2, :], k.x[:, t, :], ACT.Square, accum_out=ssq[:, t:t + 1]).then_inc(sq, 1)

            @block.vector
            def _(dve):
                dve.wait_ge(gain_in, 16)
                for t in range(T):
                    dve.wait_ge(rstd_ready, t + 1)
                    nc.vector.scalar_tensor_tensor(k.x[:, t, :], k.x[:, t, :], ssq[:, t:t + 1], k.gain[:],
                                                   ALU.mult, ALU.mult).then_inc(ready, 1)


def program(nc, d_const, x, positions, norm_mix, w_in, conv_a, fox_forget_bias, ssm_conv_w, ssm_conv_b, ssm_dt_bias,
            ssm_a_log, ssm_d, ssm_norm, mla_q_norm, mla_kv_norm, mla_w_uq, mla_w_ukv, w_out, norm_ffn, router_group_w,
            router_group_b, router_expert_w, router_expert_b, expert_w_gate, expert_w_up, expert_w_down, norm_final, out):
    with ExitStack() as ctx:
        def sb(name, shape, dtype=F32):
            return ctx.enter_context(nc.sbuf_tensor(name, shape, dtype))

        k = Core()
        k.d_const, k.d_x, k.positions, k.out = d_const, x, positions, out
        k.norm_mix, k.norm_ffn, k.norm_final = norm_mix, norm_ffn, norm_final
        k.w_in, k.w_out, k.conv_a, k.fox_forget_bias = w_in, w_out, conv_a, fox_forget_bias
        k.ssm_conv_w, k.ssm_conv_b, k.ssm_dt_bias, k.ssm_a_log = ssm_conv_w, ssm_conv_b, ssm_dt_bias, ssm_a_log
        k.ssm_d, k.ssm_norm = ssm_d, ssm_norm
        k.mla_q_norm, k.mla_kv_norm, k.mla_w_uq, k.mla_w_ukv = mla_q_norm, mla_kv_norm, mla_w_uq, mla_w_ukv
        k.router_group_w, k.router_group_b = router_group_w, router_group_b
        k.router_expert_w, k.router_expert_b = router_expert_w, router_expert_b
        k.w_gate, k.w_up, k.w_down = (w.rearrange("l e k n -> (l e) k n") for w in (expert_w_gate, expert_w_up, expert_w_down))
        k.d_h = nc.dram_tensor("h_rows", (S, D), F32).ap()
        k.d_y = nc.dram_tensor("y_rows", (BLOCKS * P, D), F32).ap()
        k.d_xs = nc.dram_tensor("x_saved", (P, T, D), F32).ap()
        k.ps = ctx.enter_context(nc.psum_tensor("banks", [P, 8, HALF], F32))

        k.x = sb("x_res", [P, T, D])
        k.x_end = ends_at(nc)
        k.const = sb("const", [P, CONSTANTS.shape[1]])
        k.c = lambda name: k.const[:, CONST[name][0]:CONST[name][0] + CONST[name][1]]
        k.ident_b = sb("ident_b", [P, P], BF16)
        k.mask_fox = sb("mask_fox", [P, P], BF16)
        k.mask_mla = sb("mask_mla", [P, P], BF16)
        k.mask_ssd = sb("mask_ssd", [P, HEADS * P], BF16)
        k.trig = sb("trig", [P, 2, T, HR])
        k.gain = sb("gain", [P, D])
        k.cw, k.cb, k.ca = sb("cw", [P, 4, TAPS_C]), sb("cb", [P, 4]), sb("ca", [P, 2, TAPS_A])
        k.bias8, k.alog, k.dskip = sb("bias8", [P, 2 * HEADS]), sb("alog", [P, HEADS]), sb("dskip", [P, HEADS])
        k.sng, k.qng, k.kvng = sb("sng", [P, GW]), sb("qng", [P, GW]), sb("kvng", [P, P])
        k.rb, k.rw = sb("rb", [P, G + E]), sb("rw", [P, KD, G + E])
        k.wuq, k.wukv = sb("wuq", [P, 2, HEADS * MLA_D]), sb("wukv", [P, HALF])
        k.logits = sb("logits", [P, T, G + E])
        k.wts, k.pos_i = sb("wts", [P, T, 2]), sb("pos_rows", [P, T, 2], I32)
        k.expert_i, k.npair_i, k.rows_i = sb("expert_i", [P, BLK], I32), sb("npair_i", [P, 1], I32), sb("rows_i", [P, BLK], I32)

        setup(nc, k)
        with nc.Fori(0, DEPTH) as l:
            with ExitStack() as mix:
                def sm(name, shape):
                    return mix.enter_context(nc.sbuf_tensor(name, shape, F32))

                k.hT = sm("hT", [P, KD, S])
                k.hT_end = ends_at(nc)
                k.yT = k.hT[:, 0:6, :]
                k.vm = k.hT[:, 6:8, :].rearrange("p a s -> p (a s)").rearrange("p (t n) -> p t n", t=T)
                k.QK = sm("QK", [P, 2, HEADS, S])
                k.QT, k.KT = k.QK[:, 0], k.QK[:, 1]
                k.yA = sm("yA", [P, 2, S])
                k.xbcT = sm("xbcT", [P, 4, S])
                lows = WMAX + P + ROPE
                k.over = sm("over", [P, T * (GW + WMAX + lows)])
                k.z = k.over[:, 0:T * GW].rearrange("p (t n) -> p t n", t=T)
                k.vf = k.over[:, T * GW:T * (GW + WMAX)].rearrange("p (t n) -> p t n", t=T)
                k.low = k.over[:, T * (GW + WMAX):].rearrange("p (t n) -> p t n", t=T)
                k.dt, k.adec = sm("dt", [P, T, HEADS]), sm("adec", [P, T, HEADS])
                k.decay, k.carry = sm("decay", [P, 2, T * HEADS]), sm("carry", [P, T, 2])

                project(nc, k, l)
                prepare(nc, k)
                attend(nc, k, "fox", FOX_K, lambda b, h: k.vf[:, b, h * HD:(h + 1) * HD], k.mask_fox, 0, fox_loads)
                ssd(nc, k)
                prepare_mla(nc, k)
                attend(nc, k, "mla", MLA_D, lambda b, h: k.vm[:, b, h * HD:(h + 1) * HD], k.mask_mla, 4)
                join(nc, k, l)
            route(nc, k)
            experts(nc, k, l)
            combine(nc, k)
        final(nc, k)


_INS = ['x', 'positions', 'norm_mix', 'w_in', 'conv_a', 'fox_forget_bias', 'ssm_conv_w', 'ssm_conv_b', 'ssm_dt_bias',
        'ssm_a_log', 'ssm_d', 'ssm_norm', 'mla_q_norm', 'mla_kv_norm', 'mla_w_uq', 'mla_w_ukv', 'w_out', 'norm_ffn',
        'router_group_w', 'router_group_b', 'router_expert_w', 'router_expert_b', 'expert_w_gate', 'expert_w_up',
        'expert_w_down', 'norm_final']


def kernel(**inputs):
    import concourse.bacc as _bacc
    from concourse.bass_utils import run_bass_kernel_spmd as _run

    nc = _bacc.Bacc("TRN2", target_bir_lowering=False, num_devices=1)
    arrays = {"in_const_dram": CONSTANTS}
    args = [nc.dram_tensor("in_const_dram", CONSTANTS.shape, F32, kind="ExternalInput").ap()]
    for name in _INS:
        a = np.ascontiguousarray(inputs[name])
        arrays[f"in_{name}_dram"] = a
        args.append(nc.dram_tensor(f"in_{name}_dram", a.shape, mybir.dt.from_np(a.dtype), kind="ExternalInput").ap())
    args.append(nc.dram_tensor("out_0_dram", (1, S, D), F32, kind="ExternalOutput").ap())
    program(nc, *args)
    r = _run(nc, [arrays], core_ids=[0])
    return r.results[0]["out_0_dram"]
```

```python
from contextlib import ExitStack

import numpy as np

import concourse.bass as bass
from concourse import mybir

ALU = mybir.AluOpType
ACT = mybir.ActivationFunctionType
AX = mybir.AxisListType.X
F32 = mybir.dt.float32
BF16 = mybir.dt.bfloat16
F32R = mybir.dt.float32r
I32 = mybir.dt.int32

P = 128
LOG_P = 7
D = 1024
S = 1024
DEPTH = 2
T = S // P
KD = D // P
EPS = 1e-6
HALF = 512

GW = 256
HEADS = 4
HD = 64
FOX_K = HD + 2
MLA_D = 96
ROPE = 32
HR = ROPE // 2
TAPS_A = 3
TAPS_C = 4
STATE = 64

A0 = 0
B0 = 3 * GW
F0 = B0 + 3 * GW
C0 = F0 + HEADS
XBC0 = C0 + GW
DT0 = XBC0 + 512
D0 = DT0 + HEADS
KV0 = D0 + GW
IN_COLS = KV0 + P + ROPE

G = 4
EG = 8
E = G * EG
FF = 256
BLOCKS = 48
LEAST = 2 * S // P
BLK = 50
NEG = -1.0e30

PAIRS = [("xbc", 0, XBC0), ("xbc", 2, XBC0 + GW), ("cgate", 0, A0 + GW), ("val", 0, A0 + 2 * GW),
         ("bgate", 0, A0), ("q", 0, B0), ("k", 0, B0 + GW)]
GROUPS = [("dtq", DT0, HEADS + GW), ("vf", B0 + 2 * GW, GW + HEADS), ("z", C0, GW), ("kv", IN_COLS - GW, GW)]
WMAX = GW + HEADS
KV_AT = GW - P - ROPE

PARAMS = TAPS_C + 1 + TAPS_A + 13

CONST = {}


def constants():
    i = np.arange(P)
    parts = {
        "ident": np.eye(P),
        "le": i[:, None] <= i[None, :],
        "lt": i[:, None] < i[None, :],
        "gt": i[:, None] > i[None, :],
        "ones": np.ones((P, P)),
        "iota": np.broadcast_to(i, (P, P)),
        "mask_fox": np.where(i[None, :] > i[:, None], NEG, 0.0),
        "mask_mla": np.where((i[None, :] // 64) > (i[:, None] // 64), NEG, 0.0),
        "mask_ssd": np.where(i[None, :] < i[:, None], NEG, 0.0),
        "partition": i[:, None],
        "tile": np.broadcast_to(np.arange(T) * P, (P, T)),
        "freq": np.broadcast_to(10000.0 ** (-np.arange(0, ROPE, 2) / ROPE), (P, HR)),
        "power": np.full((P, T), -0.5),
        "sign": np.broadcast_to(np.repeat([-1.0, 1.0], HEADS), (P, 2 * HEADS)),
        "rank4": np.broadcast_to(G - np.arange(G), (P, G)),
        "rank8": np.broadcast_to(EG - np.arange(EG), (P, EG)),
    }
    at = 0
    for name, a in parts.items():
        CONST[name] = (at, a.shape[1])
        at += a.shape[1]
    return np.ascontiguousarray(np.concatenate([np.asarray(a, np.float32) for a in parts.values()], 1))


CONSTANTS = constants()


def linker(eng, sem):
    count = [0]

    def link(ins):
        count[0] += 1
        ins.then_inc(sem, 1)
        eng.wait_ge(sem, count[0])

    return link


class Core:
    pass


class Stage:

    def __init__(self, nc, pool_dmas=False):
        self.nc, self.ctx, self.sems, self.pool_dmas = nc, ExitStack(), [], pool_dmas

    def __enter__(self):
        return self

    def sem(self, name):
        s = self.ctx.enter_context(self.nc.semaphore(name))
        self.sems.append(s)
        return s

    def sb(self, name, shape, dtype=F32):
        return self.ctx.enter_context(self.nc.sbuf_tensor(name, shape, dtype))

    def __exit__(self, *_):
        nums = sorted(s.num for s in self.sems)
        starts = [n for n in nums if n - 1 not in nums]
        for first in starts:
            last = min(n for n in nums if n >= first and n + 1 not in nums)
            if self.pool_dmas:
                self.nc.gpsimd.dma_reset(range(first, last + 1))
            self.nc.all_engine_barrier(sems_to_clear=range(first, last + 1))
        self.ctx.close()


def bc(ap, *shape):
    return ap.broadcast_to(list(shape))


def ends_at(nc):
    return nc.sbuf_base


def over_again(nc, name, shape, dtype, end):
    size = 4 * int(np.prod(shape[1:]))
    return nc.alloc_sbuf_tensor_at(name, shape, dtype, offset=end - size)


def rstd(nc, k, link, ssq, n):
    link(nc.gpsimd.tensor_scalar(ssq, ssq, 1.0 / n, EPS, ALU.mult, ALU.add))
    return nc.gpsimd.tensor_tensor(ssq, ssq, k.c("power")[:, 0:ssq.shape[1]], ALU.pow)


def setup(nc, k):
    with Stage(nc) as st:
        consts_in, pos_in = st.sem("consts_in"), st.sem("pos_in")
        step, angle_ready, trig_done = st.sem("setup_step"), st.sem("angle_ready"), st.sem("trig_done")
        pos_i = st.sb("pos_i", [P, T], I32)
        pos_f = st.sb("pos_f", [P, T])
        ang = st.sb("ang", [P, T, HR])
        turn = st.sb("turn", [P, T, HR])
        cosa = st.sb("cosa", [P, T, HR])
        with nc.Block() as block:
            @block.sync
            def _(sp):
                sp.dma_start(k.const[:, :], k.d_const[:, :]).then_inc(consts_in, 16)
                with nc.allow_non_contiguous_dma("positions, one to a partition"):
                    sp.dma_start(pos_i[:], k.positions.rearrange("b (t p) -> p (b t)", p=P)).then_inc(pos_in, 16)
                for m in range(4):
                    part = slice(m * T // 4, (m + 1) * T // 4)
                    sp.dma_start(k.x[:, part, :], k.d_x.rearrange("b (t p) n -> p (b t) n", p=P)[:, part, :]).then_inc(k.x_in[m], 16)

            @block.vector
            def _(dve):
                link = linker(dve, step)
                dve.wait_ge(consts_in, 16)
                for name, tile, reps in (("ident", k.ident_b, 1), ("mask_fox", k.mask_fox, 1), ("mask_mla", k.mask_mla, 1),
                                         ("mask_ssd", k.mask_ssd, HEADS)):
                    for r in range(reps):
                        nc.vector.tensor_copy(tile[:, r * P:(r + 1) * P], k.c(name))
                dve.wait_ge(pos_in, 16)
                link(nc.vector.tensor_copy(pos_f[:], pos_i[:]))
                link(nc.vector.tensor_tensor(ang[:], bc(pos_f[:].unsqueeze(2), P, T, HR),
                                             bc(k.c("freq").unsqueeze(1), P, T, HR), ALU.mult))
                big = 1.5 * 2.0 ** 23
                link(nc.vector.tensor_scalar(turn[:], ang[:], float(1.0 / (2 * np.pi)), None, ALU.mult))
                link(nc.vector.tensor_scalar(turn[:], turn[:], big, None, ALU.add))
                link(nc.vector.tensor_scalar(turn[:], turn[:], -big, None, ALU.add))
                c1 = 6.28125
                c2 = float(np.round((2 * np.pi - c1) * 2 ** 21) / 2 ** 21)
                c3 = float(2 * np.pi - c1 - c2)
                for c in (c1, c2, c3):
                    link(nc.vector.scalar_tensor_tensor(ang[:], turn[:], -c, ang[:], ALU.mult, ALU.add))
                link(nc.vector.tensor_scalar(cosa[:], ang[:], float(np.pi / 2), None, ALU.add))
                link(nc.vector.tensor_scalar(turn[:], cosa[:], float(np.pi), None, ALU.is_gt))
                link(nc.vector.scalar_tensor_tensor(cosa[:], turn[:], float(-2 * np.pi), cosa[:], ALU.mult, ALU.add))
                lim = 3.1415925
                link(nc.vector.tensor_scalar(cosa[:], cosa[:], lim, -lim, ALU.min, ALU.max))
                nc.vector.tensor_scalar(ang[:], ang[:], lim, -lim, ALU.min, ALU.max).then_inc(angle_ready, 1)

            @block.scalar
            def _(act):
                act.wait_ge(angle_ready, 1)
                nc.scalar.activation(k.trig[:, 1], ang[:], ACT.Sin)
                nc.scalar.activation(k.trig[:, 0], cosa[:], ACT.Sin).then_inc(trig_done, 1)
                act.wait_ge(trig_done, 1)


def project(nc, k, l):
    with Stage(nc) as st:
        params_in, gain_in = st.sem("params_in"), st.sem("gain_in")
        squares, norm_step, h_ready = st.sem("squares"), st.sem("norm_step"), st.sem("h_ready")
        rstd_ready = st.sem("rstd_ready")
        turned, ht_hi, ht_lo = st.sem("turned"), st.sem("ht_hi"), st.sem("ht_lo")
        x_saved, w_hi_set, w_lo_set = [st.sem(f"x_saved{i}") for i in range(4)], st.sem("w_hi_set"), st.sem("w_lo_set")
        w_in_sem = [st.sem("w_in_even"), st.sem("w_in_odd")]
        proj_ready = st.sem("proj_ready")
        act_took, dve_took = st.sem("act_took"), st.sem("dve_took")
        conv_step, conv_done, silu_done, a_done = (st.sem("conv_step"), st.sem("conv_done"), st.sem("silu_done"),
                                                   st.sem("a_done"))
        ring = st.sb("w_ring", [P, 2, KD, WMAX])
        w_lo = over_again(nc, "w_lo", [P, 2, KD, WMAX], F32R, ends_at(nc))
        w_hi = st.sb("w_hi", [P, 2, KD, WMAX], F32R)
        h_hi = over_again(nc, "h_hi", [P, KD, S], F32R, k.hT_end)
        h_lo = over_again(nc, "h_lo", [P, T, KD, P], F32R, k.x_end)
        ssq = st.sb("ssq", [P, T])
        step, exp_in, exp_out = st.sem("gate_step"), st.sem("exp_in"), st.sem("exp_out")
        gates_ready, sums_ready, cum_ready = st.sem("gates_ready"), st.sem("sums_ready"), st.sem("cum_ready")
        rows_turned, rows_ready, rows_in, ones_set = (st.sem("rows_turned"), st.sem("rows_ready"), st.sem("rows_in"),
                                                      st.sem("ones_set"))
        decays_done = st.sem("decays_done")
        N8 = 2 * HEADS
        x8, mx, e8, t8, r8, pl = (st.sb(f"gate{i}", [P, T, N8]) for i in range(6))
        z8, zz = e8, t8
        aneg = st.sb("aneg", [P, HEADS])
        la = st.sb("log_forget", [P, T, HEADS])
        cum = st.sb("cum", [P, T, HEADS])
        rows = ring[0:HEADS, 1].rearrange("p c n -> p (c n)")[:, 0:2 * S].rearrange("p (i s) -> p i s", i=2)
        z_done = sum(4 for _ in PAIRS) + 3 * T
        vf_took = z_done - T - 8
        over = k.over
        cbuf = over[:, 0:2 * S].rearrange("p (j s) -> p j s", j=2)
        upad = over[:, 2 * S:2 * S + 2 * (S + 2)].rearrange("p (j s) -> p j s", j=2)
        r0 = 4 * S + 4
        raw = over[:, r0:r0 + 2 * (S + 3)].rearrange("p (j s) -> p j s", j=2)
        hn = raw[:, :, 3:]
        loads = [(c0, GW) for _, _, c0 in PAIRS] + [(c0, n) for _, c0, n in GROUPS]

        taker = []
        for kind, _, _ in PAIRS:
            taker += [kind in ("val", "bgate")] * 4
        taker += [False] * (len(GROUPS) * T)

        def order(i):
            return [(j, n) for n in range(2) for j in range(2)] if i == 0 else [(j, n) for j in range(2) for n in range(2)]

        def emptied(eng, q):
            sem = dve_took if taker[q] else act_took
            eng.wait_ge(sem, sum(t == taker[q] for t in taker[:q + 1]))

        def low(i, eng, unit):
            n = loads[i][1]
            eng.wait_ge(w_hi_set, i + 1)
            unit.tensor_tensor(w_lo[:, i % 2, :, 0:n], ring[:, i % 2, :, 0:n], w_hi[:, i % 2, :, 0:n],
                               ALU.subtract).then_inc(w_lo_set, 1)

        with nc.Block() as block:
            @block.gpsimd
            def _(pool):
                link = linker(pool, norm_step)
                for t in range(T):
                    pool.wait_ge(squares, t + 1)
                    rstd(nc, k, link, ssq[:, t:t + 1], D).then_inc(rstd_ready, 1)
                    if t == 3:
                        pool.wait_ge(rstd_ready, t + 1)
                        low(0, pool, nc.gpsimd)
                        pool.wait_ge(w_lo_set, 1)
                pool.wait_ge(rstd_ready, T)
                nc.gpsimd.memset(k.QT[HD:HD + 2, :, :], 1.0).then_inc(ones_set, 1)
                nc.gpsimd.memset(k.KT[HD:HD + 2, :, :], 1.0).then_inc(ones_set, 1)

            @block.sync
            def _(sp):
                row = bass.ds(l, 1)
                sp.dma_start(k.gain[:], bc(k.norm_mix[row, :], P, D)).then_inc(gain_in, 16)

                def save(m):
                    part = slice(m * T // 4, (m + 1) * T // 4)
                    sp.wait_ge(k.x_in[m], 16)
                    sp.dma_start(k.d_xs[:, part, :], k.x[:, part, :]).then_inc(x_saved[m], 16)

                save(0)

                def load_params():
                    def load(dst, src):
                        sp.dma_start(dst, src).then_inc(params_in, 16)

                    with nc.allow_non_contiguous_dma("small parameter tables"):
                        for tap in range(TAPS_C):
                            load(k.cw[:, :, tap], k.ssm_conv_w[row, tap].rearrange("a (j p) -> p (a j)", p=P))
                        load(k.cb[:], k.ssm_conv_b[row].rearrange("a (j p) -> p (a j)", p=P))
                        for tap in range(TAPS_A):
                            load(k.ca[:, :, tap], k.conv_a[row, tap].rearrange("a (j p) -> p (a j)", p=P))
                    load(k.bias8[:, 0:HEADS], bc(k.fox_forget_bias[row, :], P, HEADS))
                    load(k.bias8[:, HEADS:], bc(k.ssm_dt_bias[row, :], P, HEADS))
                    load(k.alog[:], bc(k.ssm_a_log[row, :], P, HEADS))
                    load(k.dskip[:], bc(k.ssm_d[row, :], P, HEADS))
                    load(k.sng[:], bc(k.ssm_norm[row, :], P, GW))
                    load(k.qng[:], bc(k.mla_q_norm[row, :], P, GW))
                    load(k.kvng[:], bc(k.mla_kv_norm[row, :], P, P))
                    load(k.rb[:, 0:G], bc(k.router_group_b[row, :], P, G))
                    load(k.rb[:, G:], bc(k.router_expert_b[row, :], P, E))
                    load(k.wuq[:], k.mla_w_uq[row].rearrange("a (c p) n -> p (a c) n", p=P))
                    load(k.wukv[:], k.mla_w_ukv[row].rearrange("a p n -> p (a n)"))
                    load(k.rw[:, :, 0:G], k.router_group_w[row].rearrange("a (c p) n -> p (a c) n", p=P))
                    load(k.rw[:, :, G:], k.router_expert_w[row].rearrange("a (c p) n -> p (a c) n", p=P))

                for i, (c0, n) in enumerate(loads):
                    if i == 1:
                        save(1)
                        save(2)
                        save(3)
                    if i == 2:
                        load_params()
                    if i >= 2:
                        sp.wait_ge(proj_ready, sum(4 if m < len(PAIRS) else T for m in range(i - 1)))
                    src = k.w_in[bass.ds(l, 1), :, c0:c0 + n].rearrange("a (c p) n -> p (a c) n", p=P)
                    sp.dma_start(ring[:, i % 2, :, 0:n], src).then_inc(w_in_sem[i % 2], 16)
                sp.wait_ge(ones_set, 2)
                sp.wait_ge(rows_ready, 4)
                for h in range(HEADS):
                    sp.dma_start(k.QT[HD:HD + 1, h, :], rows[h:h + 1, 0, :]).then_inc(rows_in, 16)
                    sp.dma_start(k.KT[HD + 1:HD + 2, h, :], rows[h:h + 1, 1, :]).then_inc(rows_in, 16)
                sp.wait_ge(rows_in, 16 * 2 * HEADS)

            @block.tensor
            def _(pe):
                def turn(t):
                    pe.wait_ge(h_ready, t + 1)
                    if t >= 2:
                        pe.wait_ge(ht_lo, t - 1)
                    for c in range(KD):
                        last = nc.tensor.transpose(k.ps[:, 2 * (t % 2) + c // 4, (c % 4) * P:(c % 4 + 1) * P],
                                                   hn[:, t % 2, c * P:(c + 1) * P], k.c("ident"))
                    last.then_inc(turned, 1)

                def sums():
                    pe.wait_ge(gates_ready, 2)
                    flat = la[:].rearrange("p t h -> p (t h)")
                    adec = k.adec[:].rearrange("p t h -> p (t h)")
                    nc.tensor.matmul(k.ps[:, 1, 0:32], k.c("le"), flat, start=True, stop=True)
                    nc.tensor.matmul(k.ps[:, 1, 32:64], k.c("ones"), flat, start=True, stop=True)
                    nc.tensor.matmul(k.ps[:, 0, 32:64], k.c("le"), adec, start=True, stop=True)
                    nc.tensor.matmul(k.ps[:, 0, 64:96], k.c("gt"), adec, start=True, stop=True)
                    nc.tensor.matmul(k.ps[:, 0, 96:128], k.c("ones"), adec, start=True, stop=True).then_inc(sums_ready, 1)

                def turn_rows():
                    pe.wait_ge(cum_ready, 1)
                    for t in range(T):
                        last = nc.tensor.transpose(k.ps[0:HEADS, 2 + t // 4, (t % 4) * P:(t % 4 + 1) * P], cum[:, t, :], k.c("ident"))
                    last.then_inc(rows_turned, 1)

                for t in range(T // 2):
                    turn(t)
                q = 0
                for i in range(len(PAIRS)):
                    pe.wait_ge(w_lo_set, i + 1)
                    for step, (j, n) in enumerate(order(i)):
                        if i == 0:
                            pe.wait_ge(ht_lo, T // 2 * (n + 1))
                        if q >= 4:
                            emptied(pe, q - 4)
                        out = k.ps[:, 4 + q % 4, :].rearrange("p (t s) -> p t s", t=T // 2)
                        w = slice(j * P, (j + 1) * P)
                        for c in range(KD):
                            hi = h_hi[:, c, n * HALF:(n + 1) * HALF].rearrange("p (t s) -> p t s", t=T // 2)
                            lo = h_lo[:, n * T // 2:(n + 1) * T // 2, c, :]
                            nc.tensor.matmul(out, w_hi[:, i % 2, c, w], hi, start=(c == 0), stop=False)
                            nc.tensor.matmul(out, w_hi[:, i % 2, c, w], lo, start=False, stop=False)
                            last = nc.tensor.matmul(out, w_lo[:, i % 2, c, w], hi, start=False, stop=(c == KD - 1))
                            if i == 0 and n == 0 and c in (2, 5):
                                turn(T // 2 + 2 * step + c // 4)
                        last.then_inc(proj_ready, 1)
                        q += 1
                for g, (_, _, n) in enumerate(GROUPS):
                    i = len(PAIRS) + g
                    pe.wait_ge(w_lo_set, i + 1)
                    for t in range(T):
                        emptied(pe, q - 4)
                        out = k.ps[:, 4 + q % 4, 0:n]
                        for c in range(KD):
                            hi, lo = h_hi[:, c, t * P:(t + 1) * P], h_lo[:, t, c, :]
                            nc.tensor.matmul(out, hi, w_hi[:, i % 2, c, 0:n], start=(c == 0), stop=False)
                            nc.tensor.matmul(out, hi, w_lo[:, i % 2, c, 0:n], start=False, stop=False)
                            last = nc.tensor.matmul(out, lo, w_hi[:, i % 2, c, 0:n], start=False, stop=(c == KD - 1))
                        last.then_inc(proj_ready, 1)
                        q += 1
                        if g == 2 and t == 4:
                            sums()
                        if g == 3 and t == 0:
                            turn_rows()

            @block.scalar
            def _(act):
                def square(t):
                    act.wait_ge(k.x_in[4 * t // T], 16)
                    if t >= 2:
                        act.wait_ge(squares, t - 1)
                    nc.scalar.activation(cbuf[:, t % 2, :], k.x[:, t, :], ACT.Square,
                                         accum_out=ssq[:, t:t + 1]).then_inc(squares, 1)

                def high(i):
                    n = loads[i][1]
                    act.wait_ge(w_in_sem[i % 2], 16 * (i // 2 + 1))
                    nc.scalar.activation(w_hi[:, i % 2, :, 0:n], ring[:, i % 2, :, 0:n], ACT.Copy).then_inc(w_hi_set, 1)

                square(0)
                square(1)
                for t in range(T):
                    act.wait_ge(turned, t + 1)
                    for m in range(2):
                        ins = nc.scalar.activation(h_hi[:, 4 * m:4 * m + 4, t * P:(t + 1) * P],
                                                   k.ps[:, 2 * (t % 2) + m, :].rearrange("p (c s) -> p c s", c=4), ACT.Copy)
                    ins.then_inc(ht_hi, 1)
                    if t + 2 < T:
                        square(t + 2)
                    if t == 1:
                        high(0)
                q = 0
                act.wait_ge(squares, T)

                def silu(j):
                    if j == 0:
                        act.wait_ge(params_in, 16 * PARAMS)
                    act.wait_ge(conv_done, j + 1)
                    nc.scalar.activation(k.xbcT[:, j, :], k.xbcT[:, j, :], ACT.Silu, bias=k.cb[:, j:j + 1]).then_inc(silu_done, 1)

                for i, (kind, j0, _) in enumerate(PAIRS):
                    for step, (j, n) in enumerate(order(i)):
                        if step == 2:
                            high(i + 1)
                        if kind == "xbc" and j0 == 2 and n == 0:
                            act.wait_ge(conv_done, j + 1)
                        cols = slice(n * HALF, (n + 1) * HALF)
                        src = k.ps[:, 4 + q % 4, :]
                        q += 1
                        if kind in ("val", "bgate"):
                            continue
                        act.wait_ge(proj_ready, q)
                        if kind == "xbc":
                            ins = nc.scalar.activation(raw[:, j, 3 + n * HALF:3 + (n + 1) * HALF], src, ACT.Copy)
                        elif kind == "cgate":
                            ins = nc.scalar.activation(cbuf[:, j, cols], src, ACT.Copy)
                        else:
                            dst, scale = (k.QT, HD ** -0.5) if kind == "q" else (k.KT, 1.0)
                            nc.scalar.activation(dst[0:HD, 2 * j, cols], src[0:HD, :], ACT.Copy, scale=scale)
                            ins = nc.scalar.activation(dst[0:HD, 2 * j + 1, cols], src[HD:P, :], ACT.Copy, scale=scale)
                        ins.then_inc(act_took, 1)
                    if kind == "xbc" and j0 == 2 or kind == "cgate":
                        silu(0 if kind == "xbc" else 2)
                        silu(1 if kind == "xbc" else 3)
                act.wait_ge(a_done, 1)
                for g, (kind, _, n) in enumerate(GROUPS):
                    for t in range(T):
                        if t == T // 2 and g + 1 < len(GROUPS):
                            high(len(PAIRS) + g + 1)
                        if g == 2 and t == 1:
                            act.wait_ge(exp_in, 1)
                            nc.scalar.activation(e8[:], t8[:], ACT.Exp, scale=-1.0).then_inc(exp_out, 1)
                            nc.scalar.activation(aneg[:], k.alog[:], ACT.Exp).then_inc(exp_out, 1)
                        if g == 2 and t == 6:
                            act.wait_ge(sums_ready, 1)
                            nc.scalar.activation(k.decay[:, 0:2], k.ps[:, 0, 32:96].rearrange("p (i n) -> p i n", i=2), ACT.Exp)
                            carry = k.ps[:, 0, 96:128].rearrange("p (c h) -> p c h", h=HEADS)
                            nc.scalar.activation(k.carry[0:64, :, :], carry[0:64, :, 0:2], ACT.Exp)
                            nc.scalar.activation(k.carry[64:P, :, :], carry[64:P, :, 2:4], ACT.Exp).then_inc(decays_done, 1)
                        src = k.ps[:, 4 + q % 4, 0:n]
                        q += 1
                        act.wait_ge(proj_ready, q)
                        if kind == "z":
                            ins = nc.scalar.activation(k.z[:, t, :], src, ACT.Silu)
                        elif kind == "vf":
                            ins = nc.scalar.activation(k.vf[:, t, :], src, ACT.Copy)
                        elif kind == "dtq":
                            ins = nc.scalar.activation(k.low[:, t, 0:n], src, ACT.Copy)
                        else:
                            ins = nc.scalar.activation(k.low[:, t, WMAX:], src[:, KV_AT:], ACT.Copy)
                        ins.then_inc(act_took, 1)

            @block.vector
            def _(dve):
                def low_h(t):
                    dve.wait_ge(x_saved[4 * t // T], 16)
                    dve.wait_ge(ht_hi, t + 1)
                    for m in range(2):
                        ins = nc.vector.tensor_tensor(h_lo[:, t, 4 * m:4 * m + 4, :],
                                                      k.ps[:, 2 * (t % 2) + m, :].rearrange("p (c s) -> p c s", c=4),
                                                      h_hi[:, 4 * m:4 * m + 4, t * P:(t + 1) * P], ALU.subtract)
                    ins.then_inc(ht_lo, 1)

                dve.wait_ge(gain_in, 16)
                for t in range(T):
                    if t == T // 2:
                        low_h(t - 1)
                    dve.wait_ge(rstd_ready, t + 1)
                    if t >= 2:
                        dve.wait_ge(turned, t - 1)
                    nc.vector.scalar_tensor_tensor(hn[:, t % 2, :], k.x[:, t, :], ssq[:, t:t + 1], k.gain[:],
                                                   ALU.mult, ALU.mult).then_inc(h_ready, 1)
                    if t >= 1 and t != T // 2:
                        low_h(t - 1)
                dve.wait_ge(turned, T)
                nc.vector.memset(raw[:, :, 0:3], 0.0)
                nc.vector.memset(upad[:, :, 0:2], 0.0)
                low_h(T - 1)
                link = linker(dve, conv_step)
                dve.wait_ge(ht_lo, T)
                dve.wait_ge(params_in, 16 * PARAMS)
                for j in range(4):
                    if j % 2 == 0:
                        low(1 + j // 2, dve, nc.vector)
                    dve.wait_ge(act_took, (3, 4, 6, 8)[j])
                    acc = k.xbcT[:, j, :]
                    link(nc.vector.tensor_scalar(acc, raw[:, j % 2, 3:3 + S], k.cw[:, j, 3:4], None, ALU.mult))
                    for tap in (2, 1):
                        link(nc.vector.scalar_tensor_tensor(acc, raw[:, j % 2, tap:tap + S], k.cw[:, j, tap:tap + 1], acc,
                                                            ALU.mult, ALU.add))
                    nc.vector.scalar_tensor_tensor(acc, raw[:, j % 2, 0:S], k.cw[:, j, 0:1], acc,
                                                   ALU.mult, ALU.add).then_inc(conv_done, 1)
                low(3, dve, nc.vector)
                q = 12
                for j in range(2):
                    dve.wait_ge(act_took, 12)
                    for n in range(2):
                        dve.wait_ge(proj_ready, q + 1)
                        ins = nc.vector.tensor_tensor(upad[:, j, 2 + n * HALF:2 + (n + 1) * HALF], k.ps[:, 4 + q % 4, :],
                                                cbuf[:, j, n * HALF:(n + 1) * HALF], ALU.mult)
                        ins.then_inc(dve_took, 1)
                        q += 1
                    if j == 0:
                        low(4, dve, nc.vector)
                    dve.wait_ge(dve_took, q - 12)
                    acc = cbuf[:, j, :]
                    link(nc.vector.tensor_scalar(acc, upad[:, j, 2:2 + S], k.ca[:, j, 2:3], None, ALU.mult))
                    for tap in (1, 0):
                        link(nc.vector.scalar_tensor_tensor(acc, upad[:, j, tap:tap + S], k.ca[:, j, tap:tap + 1], acc,
                                                            ALU.mult, ALU.add))
                for j in range(2):
                    for n in range(2):
                        dve.wait_ge(proj_ready, q + 1)
                        cols = slice(n * HALF, (n + 1) * HALF)
                        nc.vector.tensor_tensor(k.yA[:, j, cols], k.ps[:, 4 + q % 4, :], cbuf[:, j, cols],
                                                ALU.mult).then_inc(dve_took, 1)
                        q += 1
                    if j == 0:
                        low(5, dve, nc.vector)
                dve.wait_ge(dve_took, 8)
                dve.sem_inc(a_done, 1)
                for i in range(6, len(loads) - 1):
                    low(i, dve, nc.vector)
                dve.wait_ge(act_took, vf_took)
                link = linker(dve, step)
                link(nc.vector.tensor_copy(x8[:, :, 0:HEADS], k.vf[:, :, GW:GW + HEADS]))
                link(nc.vector.tensor_copy(x8[:, :, HEADS:], k.low[:, :, 0:HEADS]))
                link(nc.vector.tensor_tensor(x8[:], x8[:], bc(k.bias8[:].unsqueeze(1), P, T, N8), ALU.add))
                link(nc.vector.tensor_tensor(x8[:], x8[:], bc(k.c("sign").unsqueeze(1), P, T, N8), ALU.mult))
                link(nc.vector.tensor_scalar(mx[:], x8[:], 0.0, None, ALU.max))
                nc.vector.scalar_tensor_tensor(t8[:], x8[:], -1.0, x8[:], ALU.mult, ALU.max).then_inc(exp_in, 1)
                dve.wait_ge(exp_out, 2)
                link(nc.vector.tensor_scalar(r8[:], e8[:], 2.0, None, ALU.add))
                link(nc.vector.reciprocal(r8[:], r8[:]))
                link(nc.vector.tensor_tensor(z8[:], e8[:], r8[:], ALU.mult))
                link(nc.vector.tensor_tensor(zz[:], z8[:], z8[:], ALU.mult))
                link(nc.vector.tensor_scalar(pl[:], zz[:], 1.0 / 17, 1.0 / 15, ALU.mult, ALU.add))
                for n in (13, 11, 9, 7, 5, 3, 1):
                    link(nc.vector.tensor_tensor(pl[:], pl[:], zz[:], ALU.mult))
                    link(nc.vector.tensor_scalar(pl[:], pl[:], 1.0 / n, None, ALU.add))
                link(nc.vector.tensor_tensor(pl[:], pl[:], z8[:], ALU.mult))
                link(nc.vector.scalar_tensor_tensor(x8[:], pl[:], 2.0, mx[:], ALU.mult, ALU.add))
                nc.vector.tensor_scalar(la[:], x8[:, :, 0:HEADS], -1.0, None, ALU.mult).then_inc(gates_ready, 1)
                link(nc.vector.tensor_copy(k.dt[:], x8[:, :, HEADS:]))
                nc.vector.scalar_tensor_tensor(k.adec[:], k.dt[:], -1.0, bc(aneg[:].unsqueeze(1), P, T, HEADS),
                                               ALU.mult, ALU.mult).then_inc(gates_ready, 1)
                low(len(loads) - 1, dve, nc.vector)
                dve.wait_ge(sums_ready, 1)
                tot = k.ps[:, 1, 32:64].rearrange("p (t h) -> p t h", h=HEADS)
                link(nc.vector.memset(t8[:, 0, 0:HEADS], 0.0))
                for t in range(1, T):
                    link(nc.vector.tensor_tensor(t8[:, t, 0:HEADS], t8[:, t - 1, 0:HEADS], tot[:, t - 1, :], ALU.add))
                nc.vector.tensor_tensor(cum[:], k.ps[:, 1, 0:32].rearrange("p (t h) -> p t h", h=HEADS), t8[:, :, 0:HEADS],
                                        ALU.add).then_inc(cum_ready, 1)
                dve.wait_ge(rows_turned, 1)
                dve.wait_ge(proj_ready, z_done)
                for n in range(2):
                    src = k.ps[0:HEADS, 2 + n, :]
                    nc.vector.tensor_copy(rows[:, 0, n * HALF:(n + 1) * HALF], src).then_inc(rows_ready, 1)
                    nc.vector.tensor_scalar(rows[:, 1, n * HALF:(n + 1) * HALF], src, -1.0, None, ALU.mult).then_inc(rows_ready, 1)
                dve.wait_ge(silu_done, 4)
                dve.wait_ge(decays_done, 1)


def low_parts(k):
    return (k.low[:, :, HEADS:WMAX], k.low[:, :, WMAX:WMAX + P],
            k.low[:, :, WMAX + P:].rearrange("p t (i r) -> p t i r", i=2))


def fox_loads(nc, k, st):
    x_back, zeros_set, spare_filled = st.sem("x_back"), st.sem("zeros_set"), st.sem("spare_filled")
    zeros = st.sb("zeros", [P, D])

    def pool_part(pool):
        nc.gpsimd.memset(zeros[:], 0.0).then_inc(zeros_set, 1)

    def sp_part(sp):
        sp.dma_start(k.x[:], k.d_xs[:, :, :]).then_inc(x_back, 16)
        sp.wait_ge(zeros_set, 1)
        spare = k.d_y[LEAST * P:, :].rearrange("(b p) n -> p b n", p=P)
        sp.dma_start(spare, bc(zeros[:].unsqueeze(1), P, BLOCKS - LEAST, D)).then_inc(spare_filled, 16)
        sp.wait_ge(x_back, 16)
        sp.wait_ge(spare_filled, 16)

    return pool_part, sp_part


def mla_loads(nc, k, st, l):
    wo_in, gain_in = st.sem("wo_in"), st.sem("gain_in")

    def sp_part(sp):
        sp.dma_start(k.wo[:], k.w_out[bass.ds(l, 1)].rearrange("a (c p) n -> p (a c) n", p=P)).then_inc(wo_in, 16)
        sp.dma_start(k.gain[:], bc(k.norm_ffn[bass.ds(l, 1), :], P, D)).then_inc(gain_in, 16)
        sp.wait_ge(wo_in, 16)
        sp.wait_ge(gain_in, 16)

    return None, sp_part


def attend(nc, k, who, K, v, mask, chunk0, loads):
    units = [(i, h) for i in range(T) for h in range(HEADS)]
    N = len(units)
    with Stage(nc) as st:
        scores, maxed, exped, inv, normed = st.sem("scores"), st.sem("maxed"), st.sem("exped"), st.sem("inv"), st.sem("normed")
        p_turned, pt_act, pt_dve = st.sem("p_turned"), st.sem("pt_act"), st.sem("pt_dve")
        out_ready, out_took = st.sem("out_ready"), st.sem("out_took")
        probs = st.sb(f"probs_{who}", [P, 3, S])
        pT = st.sb(f"pT_{who}", [P, 2, T, P])
        nmax = st.sb(f"nmax_{who}", [P, 2])
        total = st.sb(f"total_{who}", [P, 4])

        groups = []
        for u, (i, h) in enumerate(units):
            for b0 in range(0, i + 1, 4):
                groups.append((u, b0, min(4, i + 1 - b0)))
        before = lambda u: sum(g[0] < u for g in groups)

        def emptied(eng, n):
            if (n + 1) // 2:
                eng.wait_ge(pt_act, (n + 1) // 2)
            if n // 2:
                eng.wait_ge(pt_dve, n // 2)

        def empty(eng, unit, u, par):
            for g in range(before(u), before(u + 1)):
                if g % 2 != par:
                    continue
                _, b0, m = groups[g]
                eng.wait_ge(p_turned, g + 1)
                if u >= 2:
                    eng.wait_ge(out_ready, u - 1)
                src = k.ps[:, 4 + g % 2, 0:m * P].rearrange("p (b s) -> p b s", b=m)
                dst = pT[:, u % 2, b0:b0 + m, :]
                if par == 0:
                    unit.activation(dst, src, ACT.Copy).then_inc(pt_act, 1)
                else:
                    unit.tensor_copy(dst, src).then_inc(pt_dve, 1)

        def row(u, buf):
            nk = (units[u][0] + 1) * P
            return buf[:, 0:nk] if buf is not None else k.ps[:, 2 * (u % 2):2 * (u % 2) + 2, :].rearrange("p b n -> p (b n)")[:, 0:nk]

        pool_part, sp_part = loads(st)
        with nc.Block() as block:
            if pool_part:
                @block.gpsimd
                def _(pool):
                    pool_part(pool)

            @block.sync
            def _(sp):
                sp_part(sp)

            @block.tensor
            def _(pe):
                def score(u):
                    i, h = units[u]
                    if u >= 2:
                        pe.wait_ge(exped, u - 1)
                    for n in range(0, i + 1, 4):
                        m = min(4, i + 1 - n)
                        bank = k.ps[:, 2 * (u % 2) + n // 4, :]
                        nc.tensor.matmul(bank[:, 0:m * P], k.QT[0:K, h, i * P:(i + 1) * P], k.KT[0:K, h, n * P:(n + m) * P],
                                         start=True, stop=True)
                    nc.tensor.matmul(bank[:, (m - 1) * P:m * P], k.ident_b[:], mask[:], start=False, stop=True,
                                     skip_group_check=True).then_inc(scores, 1)

                def turn(u):
                    pe.wait_ge(normed, u + 1)
                    for g in range(before(u), before(u + 1)):
                        _, b0, m = groups[g]
                        if g >= 2:
                            emptied(pe, g - 1)
                        for b in range(m):
                            last = nc.tensor.transpose(k.ps[:, 4 + g % 2, b * P:(b + 1) * P],
                                                       probs[:, u % 3, (b0 + b) * P:(b0 + b + 1) * P], k.c("ident"))
                        last.then_inc(p_turned, 1)

                def weigh(u):
                    i, h = units[u]
                    emptied(pe, before(u + 1))
                    if u >= 4 and h % 2 == 0:
                        pe.wait_ge(out_took, u // 2 - 1)
                    r = slice(h % 2 * HD, (h % 2 + 1) * HD)
                    for b in range(i + 1):
                        last = nc.tensor.matmul(k.ps[r, 6 + u // 2 % 2, 0:P], v(b, h), pT[:, u % 2, b, :],
                                                start=(b == 0), stop=(b == i))
                    last.then_inc(out_ready, 1)

                score(0)
                for u in range(N + 2):
                    if u + 1 < N:
                        score(u + 1)
                    if 1 <= u <= N:
                        turn(u - 1)
                    if u >= 2:
                        weigh(u - 2)

            @block.scalar
            def _(act):
                for u in range(N + 4):
                    if 2 <= u < N + 2:
                        empty(act, nc.scalar, u - 2, 0)
                    if u < N:
                        act.wait_ge(maxed, u + 1)
                        if u >= 3:
                            act.wait_ge(p_turned, before(u - 2))
                        nc.scalar.activation(row(u, probs[:, u % 3]), row(u, None), ACT.Exp, bias=nmax[:, u % 2:u % 2 + 1],
                                             accum_out=total[:, u % 4:u % 4 + 1]).then_inc(exped, 1)
                    if u >= 4 and u % 2 == 1:
                        i, h = units[u - 4]
                        act.wait_ge(out_ready, u - 3)
                        nc.scalar.activation(k.yT[:, chunk0 + h // 2, i * P:(i + 1) * P], k.ps[:, 6 + (u - 4) // 2 % 2, 0:P],
                                             ACT.Copy).then_inc(out_took, 1)

            @block.vector
            def _(dve):
                def normalise(u):
                    dve.wait_ge(exped, u + 1)
                    t = total[:, u % 4:u % 4 + 1]
                    nc.vector.reciprocal(t, t).then_inc(inv, 1)
                    dve.wait_ge(inv, u + 1)
                    r = row(u, probs[:, u % 3])
                    nc.vector.tensor_scalar(r, r, t, None, ALU.mult).then_inc(normed, 1)

                for u in range(N + 2):
                    if u < N:
                        dve.wait_ge(scores, u + 1)
                        if u >= 2:
                            dve.wait_ge(exped, u - 1)
                        nc.vector.tensor_reduce(nmax[:, u % 2:u % 2 + 1], row(u, None), AX, ALU.max, negate=True).then_inc(maxed, 1)
                    if 1 <= u <= N:
                        normalise(u - 1)
                    if u >= 2:
                        empty(dve, nc.vector, u - 2, 1)


def prepare_mla(nc, k, st, low_ready, y_took, yt_took):
    step, normed = st.sem("rotate_step"), st.sem("normed")
    c_turned, c_ready, up_ready, qk_ready = st.sem("c_turned"), st.sem("c_ready"), st.sem("up_ready"), st.sem("qk_ready")
    v_took, qk_turned, q_took, k_took = st.sem("v_took"), st.sem("qk_turned"), st.sem("q_took"), st.sem("k_took")
    cn = st.sb("cn", [P, 2, GW + P])
    cT = st.sb("cT", [P, 2, 3, P])
    qn = st.sb("qn", [P, 2, HEADS, MLA_D])
    kn = st.sb("kn", [P, 2, HEADS, MLA_D])
    rot = st.sb("rot", [P, 2, HEADS, 2, HR])
    ssq, kr = k.low_rstd, k.kr
    cq, ckv, _ = low_parts(k)
    cos, sin = k.trig[:, 0], k.trig[:, 1]

    def act_steps(act):
        def take_c(t):
            act.wait_ge(c_turned, t + 1)
            if t >= 2:
                act.wait_ge(up_ready, t - 1)
            nc.scalar.activation(cT[:, t % 2], k.ps[:, t % 2, 0:3 * P].rearrange("p (c s) -> p c s", c=3),
                                 ACT.Copy).then_inc(c_ready, 1)

        def take_kv(t):
            act.wait_ge(up_ready, t + 1)
            kv = k.ps[:, 4 + t % 2, :].rearrange("p (h i d) -> p h i d", h=HEADS, i=2)
            nc.scalar.activation(k.vm[:, t].rearrange("p (h d) -> p h d", h=HEADS), kv[:, :, 1, :], ACT.Copy)
            if t >= 2:
                act.wait_ge(qk_turned, t - 1)
            nc.scalar.activation(kn[:, t % 2, :, 0:HD], kv[:, :, 0, :], ACT.Copy).then_inc(v_took, 1)

        def take_q(t):
            act.wait_ge(qk_turned, t + 1)
            nc.scalar.activation(k.QT[0:MLA_D, :, t * P:(t + 1) * P],
                                 k.ps[0:MLA_D, 6, :].rearrange("p (h s) -> p h s", h=HEADS), ACT.Copy,
                                 scale=MLA_D ** -0.5).then_inc(q_took, 1)

        def rest():
            for t in range(T + 2):
                if t + 1 < T:
                    take_c(t + 1)
                if t < T:
                    take_kv(t)
                if t >= 2:
                    take_q(t - 2)

        return lambda: take_c(0), rest

    def pe_steps(pe):
        def turn_c(t):
            pe.wait_ge(normed, t + 1)
            if t >= 2:
                pe.wait_ge(c_ready, t - 1)
            for c in range(3):
                last = nc.tensor.transpose(k.ps[:, t % 2, c * P:(c + 1) * P], cn[:, t % 2, c * P:(c + 1) * P], k.c("ident"))
            last.then_inc(c_turned, 1)

        def up(t):
            pe.wait_ge(c_ready, t + 1)
            if t >= 2:
                pe.wait_ge(qk_ready, t - 1)
                pe.wait_ge(v_took, t - 1)
            for c in range(2):
                nc.tensor.matmul(k.ps[:, 2 + t % 2, 0:HEADS * MLA_D], cT[:, t % 2, c, :], k.wuq[:, c, :],
                                 start=(c == 0), stop=(c == 1))
            nc.tensor.matmul(k.ps[:, 4 + t % 2, :], cT[:, t % 2, 2, :], k.wukv[:], start=True, stop=True).then_inc(up_ready, 1)

        def turn(t):
            pe.wait_ge(qk_ready, t + 1)
            pe.wait_ge(v_took, t + 1)
            if t >= 1:
                pe.wait_ge(q_took, t)
                pe.wait_ge(k_took, t)
            for h in range(HEADS):
                nc.tensor.transpose(k.ps[0:MLA_D, 6, h * P:(h + 1) * P], qn[:, t % 2, h, :], k.c("ident"))
                last = nc.tensor.transpose(k.ps[0:MLA_D, 7, h * P:(h + 1) * P], kn[:, t % 2, h, :], k.c("ident"))
            last.then_inc(qk_turned, 1)

        def first():
            turn_c(0)
            turn_c(1)
            up(0)

        def rest():
            pe.wait_ge(y_took, T)
            pe.wait_ge(yt_took, T)
            for t in range(1, T + 2):
                if t + 1 < T:
                    turn_c(t + 1)
                if t < T:
                    up(t)
                if t >= 2:
                    turn(t - 2)

        return first, rest

    def dve_steps(dve):
        link = linker(dve, step)
        def norm(t):
            if t >= 2:
                dve.wait_ge(c_turned, t - 1)
            nc.vector.scalar_tensor_tensor(cn[:, t % 2, 0:GW], cq[:, t, :], ssq[:, 0, t:t + 1], k.qng[:], ALU.mult, ALU.mult)
            nc.vector.scalar_tensor_tensor(cn[:, t % 2, GW:], ckv[:, t, :], ssq[:, 1, t:t + 1], k.kvng[:],
                                           ALU.mult, ALU.mult).then_inc(normed, 1)

        def rotate(t):
            dve.wait_ge(up_ready, t + 1)
            if t >= 1:
                dve.wait_ge(qk_ready, t)
            if t >= 2:
                dve.wait_ge(qk_turned, t - 1)
            q = k.ps[:, 2 + t % 2, 0:HEADS * MLA_D].rearrange("p (h d) -> p h d", h=HEADS)
            qr = q[:, :, HD:].rearrange("p h (i r) -> p h i r", i=2)
            nc.vector.tensor_copy(qn[:, t % 2, :, 0:HD], q[:, :, 0:HD])
            c4 = bc(cos[:, t, :].unsqueeze(1).unsqueeze(1), P, HEADS, 2, HR)
            s4 = bc(sin[:, t, :].unsqueeze(1).unsqueeze(1), P, HEADS, 2, HR)
            nc.vector.tensor_tensor(rot[:, 0], qr, c4, ALU.mult)
            link(nc.vector.tensor_tensor(rot[:, 1], qr, s4, ALU.mult))
            nc.vector.tensor_tensor(qn[:, t % 2, :, HD:HD + HR], rot[:, 0, :, 0, :], rot[:, 1, :, 1, :], ALU.subtract)
            nc.vector.tensor_tensor(qn[:, t % 2, :, HD + HR:], rot[:, 0, :, 1, :], rot[:, 1, :, 0, :], ALU.add)
            nc.vector.tensor_copy(kn[:, t % 2, :, HD:],
                                  bc(kr[:, t].rearrange("p i r -> p (i r)").unsqueeze(1), P, HEADS, ROPE)).then_inc(qk_ready, 1)

        def take(t):
            dve.wait_ge(qk_turned, t + 1)
            nc.vector.tensor_copy(k.KT[0:MLA_D, :, t * P:(t + 1) * P],
                                  k.ps[0:MLA_D, 7, :].rearrange("p (h s) -> p h s", h=HEADS)).then_inc(k_took, 1)

        def first():
            dve.wait_ge(low_ready, 1)
            norm(0)
            norm(1)

        def rest():
            for t in range(T + 2):
                if t + 2 < T:
                    norm(t + 2)
                if t < T:
                    rotate(t)
                if t >= 2:
                    take(t - 2)
            dve.wait_ge(q_took, T)

        return first, rest

    return act_steps, pe_steps, dve_steps


def ssd(nc, k):
    with Stage(nc) as st:
        bx_turned, b_took, xs_ready = st.sem("bx_turned"), st.sem("b_took"), st.sem("xs_ready")
        cuts_ready, d_ready, g_ready, exped, m_ready = (st.sem("cuts_ready"), st.sem("d_ready"), st.sem("g_ready"), st.sem("exped"),
                                                         st.sem("m_ready"))
        y_ready, state_ready, step, y_took = st.sem("y_ready"), st.sem("state_ready"), st.sem("ssd_step"), st.sem("y_took")
        yn_ready, yn_turned, yt_took, zeroed = st.sem("yn_ready"), st.sem("yn_turned"), st.sem("yt_took"), st.sem("zeroed")
        cleared, apart, gated = st.sem("cleared"), st.sem("apart"), st.sem("gated")
        squared, rstd_step, rstd_ready = st.sem("squared"), st.sem("rstd_step"), st.sem("rstd_ready")
        Bn = st.sb("Bn", [P, 3, P])
        xdt = st.sb("xdt", [P, 3, HEADS, HD])
        xds = st.sb("xds", [P, 3, HEADS, HD])
        skip = st.sb("skip", [P, 3, HEADS, HD])
        cuts, eD, M = (k.QK[:, 1, i].rearrange("p (b h s) -> p b h s", b=2, h=HEADS) for i in range(3))
        Cg = st.sb("Cg", [P, 2, 2, P])
        prev = st.sb("prev", [P, 2, HEADS, HD])
        yc = st.sb("yc", [P, 3, HEADS, HD])
        ssq = st.sb("ssq3", [P, T])
        junk = st.sb("junk3", [P, GW])
        gt4 = bc(k.c("gt").unsqueeze(1), P, HEADS, P)
        low_sq, krot_step, low_ready = st.sem("low_sq"), st.sem("krot_step"), st.sem("low_ready")
        mla_act, mla_pe, mla_dve = prepare_mla(nc, k, st, low_ready, y_took, yt_took)
        low_junk = k.QK[:, 0, 0, 0:2 * (GW + P)].rearrange("p (b n) -> p b n", b=2)
        krot = k.QK[:, 0, 1, 0:4 * T * HR].rearrange("p (b t i r) -> p b t i r", b=2, t=T, i=2)
        cq, ckv, ckr = low_parts(k)

        def col(ap):
            return bc(ap.unsqueeze(2), P, HEADS, HD)

        with nc.Block() as block:
            @block.gpsimd
            def _(pool):
                link = linker(pool, rstd_step)
                nc.gpsimd.memset(Cg[:], 0.0).then_inc(cleared, 1)
                pool.wait_ge(cleared, 1)
                link_k = linker(pool, krot_step)

                def rotate_keys():
                    bcos = bc(k.trig[:, 0].unsqueeze(2), P, T, 2, HR)
                    bsin = bc(k.trig[:, 1].unsqueeze(2), P, T, 2, HR)
                    kr = k.kr[:]
                    link_k(nc.gpsimd.tensor_tensor(krot[:, 0], ckr, bcos, ALU.mult))
                    link_k(nc.gpsimd.tensor_tensor(krot[:, 1], ckr, bsin, ALU.mult))
                    link_k(nc.gpsimd.tensor_tensor(kr[:, :, 0, :], krot[:, 0, :, 0, :], krot[:, 1, :, 1, :], ALU.subtract))
                    nc.gpsimd.tensor_tensor(kr[:, :, 1, :], krot[:, 0, :, 1, :], krot[:, 1, :, 0, :], ALU.add).then_inc(low_ready, 1)
                    pool.wait_ge(low_ready, 2)

                def cut(c):
                    if c >= 2:
                        pool.wait_ge(d_ready, c - 1)
                    nc.gpsimd.tensor_tensor(cuts[:, c % 2], gt4, bc(k.adec[:, c, :].unsqueeze(2), P, HEADS, P), ALU.mult).then_inc(cuts_ready, 1)
                    pool.wait_ge(cuts_ready, c + 1)

                def part(c):
                    if c >= 2:
                        pool.wait_ge(g_ready, c - 1)
                    for g in range(2):
                        r = slice(g * STATE, (g + 1) * STATE)
                        nc.gpsimd.tensor_copy(Cg[r, c % 2, g, :], k.xbcT[r, 3, c * P:(c + 1) * P]).then_inc(apart, 1)
                    pool.wait_ge(apart, 2 * (c + 1))

                cut(0)
                part(0)
                cut(1)
                for c in range(T + 2):
                    if c + 1 < T:
                        part(c + 1)
                    if c + 2 < T:
                        cut(c + 2)
                    if c == T - 1:
                        pool.wait_ge(low_sq, T)
                        link(rstd(nc, k, link, k.low_rstd[:, 0], GW))
                        rstd(nc, k, link, k.low_rstd[:, 1], P).then_inc(low_ready, 1)
                        pool.wait_ge(low_ready, 1)
                    if c >= 2:
                        pool.wait_ge(squared, c - 1)
                        rstd(nc, k, link, ssq[:, c - 2:c - 1], GW).then_inc(rstd_ready, 1)
                        pool.wait_ge(rstd_ready, c - 1)
                    if c == T - 1:
                        pool.wait_ge(rstd_ready, c - 1)
                        rotate_keys()

            @block.tensor
            def _(pe):
                def turn_x(c):
                    s = slice(c * P, (c + 1) * P)
                    if c >= 1:
                        pe.wait_ge(b_took, c)
                        pe.wait_ge(xs_ready, c)
                    for bank, n, j in ((0, 0, 0), (0, 1, 1), (1, 0, 2)):
                        last = nc.tensor.transpose(k.ps[:, bank, n * P:(n + 1) * P], k.xbcT[:, j, s], k.c("ident"))
                    last.then_inc(bx_turned, 1)

                def products(c):
                    pe.wait_ge(cuts_ready, c + 1)
                    for h in range(HEADS):
                        nc.tensor.matmul(k.ps[:, 3 + c % 2, h * P:(h + 1) * P], cuts[:, c % 2, h, :], k.c("le"),
                                         start=(h == 0), stop=False, skip_group_check=True)
                    nc.tensor.matmul(k.ps[:, 3 + c % 2, :], k.ident_b[:], k.mask_ssd[:],
                                     start=False, stop=True, skip_group_check=True).then_inc(d_ready, 1)
                    if c >= 1:
                        pe.wait_ge(m_ready, c)
                    pe.wait_ge(apart, 2 * (c + 1))
                    nc.tensor.matmul(k.ps[:, 2, 0:2 * P], k.xbcT[:, 2, c * P:(c + 1) * P], Cg[:, c % 2].rearrange("p g s -> p (g s)"),
                                     start=True, stop=True).then_inc(g_ready, 1)

                def back(c):
                    s = slice(c * P, (c + 1) * P)
                    pe.wait_ge(m_ready, c + 1)
                    if c == 0:
                        pe.wait_ge(zeroed, 1)
                    else:
                        pe.wait_ge(y_took, c)
                    pe.wait_ge(xs_ready, c + 1)
                    pe.wait_ge(b_took, c + 1)
                    nc.tensor.matmul(k.ps[:, 6, 0:GW], Bn[:, c % 3], xds[:, c % 3].rearrange("p h d -> p (h d)"), start=True,
                                     stop=True).then_inc(state_ready, 1)
                    for h in range(HEADS):
                        nc.tensor.matmul(k.ps[:, 5, h * HD:(h + 1) * HD], M[:, c % 2, h, :], xdt[:, c % 3, h, :], start=True, stop=True)
                    nc.tensor.matmul(k.ps[:, 5, GW:], k.xbcT[:, 3, s], prev[:, c % 2].rearrange("p h d -> p (h d)"), start=True,
                                     stop=True).then_inc(y_ready, 1)

                def turn_y(c):
                    pe.wait_ge(yn_ready, c + 1)
                    if c >= 1:
                        pe.wait_ge(yt_took, c)
                    for j in range(2):
                        last = nc.tensor.transpose(k.ps[:, 7, j * P:(j + 1) * P],
                                                   yc[:, c % 3].rearrange("p h d -> p (h d)")[:, j * P:(j + 1) * P], k.c("ident"))
                    last.then_inc(yn_turned, 1)

                first, rest = mla_pe(pe)
                for c in range(-2, T + 2):
                    if c == T:
                        first()
                    if c + 2 < T:
                        turn_x(c + 2)
                    if 0 <= c < T:
                        back(c)
                    if c + 2 < T:
                        products(c + 2)
                    if c >= 2:
                        turn_y(c - 2)
                rest()

            @block.scalar
            def _(act):
                def square(c):
                    act.wait_ge(gated, c + 1)
                    if c >= 1:
                        act.wait_ge(squared, c)
                    nc.scalar.activation(junk[:], yc[:, c % 3].rearrange("p h d -> p (h d)"), ACT.Square,
                                         accum_out=ssq[:, c:c + 1]).then_inc(squared, 1)

                def take_yt(c):
                    act.wait_ge(yn_turned, c + 1)
                    nc.scalar.activation(k.yT[:, 2:4, c * P:(c + 1) * P], k.ps[:, 7, 0:2 * P].rearrange("p (j s) -> p j s", j=2),
                                         ACT.Copy).then_inc(yt_took, 1)

                for c in range(T):
                    act.wait_ge(bx_turned, c + 1)
                    if c >= 3:
                        act.wait_ge(y_ready, c - 2)
                    nc.scalar.activation(Bn[:, c % 3, :], k.ps[:, 1, 0:P], ACT.Copy).then_inc(b_took, 1)
                    act.wait_ge(d_ready, c + 1)
                    if c >= 2:
                        act.wait_ge(m_ready, c - 1)
                    nc.scalar.activation(eD[:, c % 2], k.ps[:, 3 + c % 2, :].rearrange("p (h s) -> p h s", h=HEADS), ACT.Exp).then_inc(exped, 1)
                    if c >= 2:
                        square(c - 2)
                    if c >= 4:
                        take_yt(c - 4)
                    if c >= 2:
                        act.wait_ge(low_sq, c - 1)
                    nc.scalar.activation(low_junk[:, c % 2, 0:GW], cq[:, c, :], ACT.Square, accum_out=k.low_rstd[:, 0, c:c + 1])
                    nc.scalar.activation(low_junk[:, c % 2, GW:], ckv[:, c, :], ACT.Square,
                                         accum_out=k.low_rstd[:, 1, c:c + 1]).then_inc(low_sq, 1)
                first, rest = mla_act(act)
                square(T - 2)
                take_yt(T - 4)
                square(T - 1)
                take_yt(T - 3)
                first()
                for c in range(T - 2, T):
                    take_yt(c)
                rest()

            @block.vector
            def _(dve):
                link = linker(dve, step)
                nc.vector.memset(prev[:], 0.0).then_inc(zeroed, 1)

                def inputs(c):
                    dve.wait_ge(bx_turned, c + 1)
                    xs = k.ps[:, 0, 0:2 * P].rearrange("p (h d) -> p h d", h=HEADS)
                    if c >= 3:
                        dve.wait_ge(y_ready, c - 2)
                    link(nc.vector.tensor_tensor(xdt[:, c % 3], xs, col(k.dt[:, c, :]), ALU.mult))
                    nc.vector.tensor_tensor(xds[:, c % 3], xdt[:, c % 3], col(k.decay[:, 1, c * HEADS:(c + 1) * HEADS]), ALU.mult)
                    nc.vector.tensor_tensor(skip[:, c % 3], xs, col(k.dskip[:]), ALU.mult).then_inc(xs_ready, 1)

                def weights(c):
                    dve.wait_ge(exped, c + 1)
                    dve.wait_ge(g_ready, c + 1)
                    if c >= 2:
                        dve.wait_ge(y_ready, c - 1)
                    gg = k.ps[:, 2, 0:2 * P].rearrange("p (g s) -> p g s", g=2)
                    nc.vector.tensor_tensor(M[:, c % 2].rearrange("p (g j) s -> p g j s", g=2),
                                            eD[:, c % 2].rearrange("p (g j) s -> p g j s", g=2),
                                            bc(gg.unsqueeze(2), P, 2, 2, P), ALU.mult).then_inc(m_ready, 1)

                def back(c):
                    dve.wait_ge(state_ready, c + 1)
                    dve.wait_ge(zeroed, 1)
                    if c >= 1:
                        dve.wait_ge(y_ready, c)
                    for h in range(HEADS):
                        r = slice(h // 2 * STATE, (h // 2 + 1) * STATE)
                        ins = nc.vector.scalar_tensor_tensor(prev[r, (c + 1) % 2, h, :], prev[r, c % 2, h, :], k.carry[r, c, h % 2:h % 2 + 1],
                                                             k.ps[r, 6, h * HD:(h + 1) * HD], ALU.mult, ALU.add)
                    link(ins)
                    dve.wait_ge(y_ready, c + 1)
                    if c >= 3:
                        dve.wait_ge(yn_turned, c - 2)
                    yv = yc[:, c % 3]
                    link(nc.vector.tensor_tensor(yv, k.ps[:, 5, GW:].rearrange("p (h d) -> p h d", h=HEADS),
                                                 col(k.decay[:, 0, c * HEADS:(c + 1) * HEADS]), ALU.mult))
                    nc.vector.tensor_tensor(yv, yv, k.ps[:, 5, 0:GW].rearrange("p (h d) -> p h d", h=HEADS), ALU.add).then_inc(y_took, 1)
                    dve.wait_ge(y_took, c + 1)
                    link(nc.vector.tensor_tensor(yv, yv, skip[:, c % 3], ALU.add))
                    flat = yv.rearrange("p h d -> p (h d)")
                    nc.vector.tensor_tensor(flat, flat, k.z[:, c, :], ALU.mult).then_inc(gated, 1)

                def norm(c):
                    flat = yc[:, c % 3].rearrange("p h d -> p (h d)")
                    dve.wait_ge(rstd_ready, c + 1)
                    nc.vector.scalar_tensor_tensor(flat, flat, ssq[:, c:c + 1], k.sng[:], ALU.mult, ALU.mult).then_inc(yn_ready, 1)

                first, rest = mla_dve(dve)
                for c in range(-2, T + 1):
                    if 0 <= c + 1 < T:
                        weights(c + 1)
                    if 0 <= c + 2 < T:
                        inputs(c + 2)
                    if 0 <= c < T:
                        back(c)
                    if c == T - 1:
                        first()
                    if c >= 1:
                        norm(c - 1)
                dve.wait_ge(low_ready, 2)
                rest()


def join(nc, k):
    with Stage(nc) as st:
        w_hi_set, w_lo_set, y_hi_set, y_lo_set = st.sem("w_hi_set"), st.sem("w_lo_set"), st.sem("y_hi_set"), st.sem("y_lo_set")
        o_ready, x_ready, sq, step = st.sem("o_ready"), st.sem("x_ready"), st.sem("sq"), st.sem("join_step")
        h_ready, h_stored, turned, ht_ready, lg_ready, lg_took = (st.sem("h_ready"), st.sem("h_stored"), st.sem("turned"),
                                                         st.sem("ht_ready"), st.sem("lg_ready"), st.sem("lg_took"))
        rstd_ready = st.sem("rstd_ready")
        w_lo = over_again(nc, "wo_lo", [P, KD, D], F32R, k.wo_end)
        w_hi = over_again(nc, "wo_hi", [P, KD, D], F32R, k.QK_end)
        y_hi = st.sb("y_hi", [P, 2, KD, P], F32R)
        y_lo = st.sb("y_lo", [P, 2, KD, P], F32R)
        h = st.sb("h_join", [P, 2, D])
        free = k.over[:, 4 * D:]
        hT2 = free[:, 0:2 * D].rearrange("p (b c s) -> p b c s", b=2, c=KD)
        junk = free[:, 2 * D:3 * D]
        ssq = st.sb("ssq4", [P, T])

        def parts(t):
            cols = slice(t * P, (t + 1) * P)
            return (k.yA[:, :, cols], slice(0, 2)), (k.yT[:, :, cols], slice(2, KD))

        with nc.Block() as block:
            @block.gpsimd
            def _(pool):
                link = linker(pool, step)
                for t in range(T):
                    pool.wait_ge(sq, t + 1)
                    rstd(nc, k, link, ssq[:, t:t + 1], D).then_inc(rstd_ready, 1)

            @block.sync
            def _(sp):
                for t in range(T):
                    sp.wait_ge(h_ready, t + 1)
                    sp.dma_start(k.d_h[t * P:(t + 1) * P, :], h[:, t % 2, :]).then_inc(h_stored, 16)
                    if t + 1 == T:
                        sp.wait_ge(h_stored, 16 * T)

            @block.tensor
            def _(pe):
                def turn(t):
                    pe.wait_ge(h_ready, t + 1)
                    if t >= 1:
                        pe.wait_ge(ht_ready, 2 * t)
                    for c in range(KD):
                        last = nc.tensor.transpose(k.ps[:, 4 + c // 4, (c % 4) * P:(c % 4 + 1) * P], h[:, t % 2, c * P:(c + 1) * P],
                                                   k.c("ident"))
                    last.then_inc(turned, 1)

                def router(t):
                    pe.wait_ge(ht_ready, 2 * (t + 1))
                    if t >= 1:
                        pe.wait_ge(lg_took, t)
                    for c in range(KD):
                        last = nc.tensor.matmul(k.ps[:, 6, 0:G + E], hT2[:, t % 2, c, :], k.rw[:, c, :], start=(c == 0), stop=(c == KD - 1))
                    last.then_inc(lg_ready, 1)

                for t in range(T):
                    if t >= 2:
                        pe.wait_ge(x_ready, t - 1)
                    pe.wait_ge(y_lo_set, 2 * (t + 1))
                    for c in range(KD):
                        if t == 0:
                            pe.wait_ge(w_lo_set, c + 1)
                        hi, lo = y_hi[:, t % 2, c, :], y_lo[:, t % 2, c, :]
                        for n in range(2):
                            out = k.ps[:, 2 * (t % 2) + n, :]
                            cols = slice(n * HALF, (n + 1) * HALF)
                            nc.tensor.matmul(out, hi, w_hi[:, c, cols], start=(c == 0), stop=False)
                            nc.tensor.matmul(out, hi, w_lo[:, c, cols], start=False, stop=False)
                            last = nc.tensor.matmul(out, lo, w_hi[:, c, cols], start=False, stop=(c == KD - 1))
                    last.then_inc(o_ready, 1)
                    if t >= 1:
                        turn(t - 1)
                    if t >= 2:
                        router(t - 2)
                turn(T - 1)
                router(T - 2)
                router(T - 1)

            @block.scalar
            def _(act):
                def high_y(t):
                    if t >= 2:
                        act.wait_ge(o_ready, t - 1)
                    for src, chunks in parts(t):
                        nc.scalar.activation(y_hi[:, t % 2, chunks, :], src, ACT.Copy).then_inc(y_hi_set, 1)

                high_y(0)
                for c in range(KD):
                    nc.scalar.activation(w_hi[:, c, :], k.wo[:, c, :], ACT.Copy).then_inc(w_hi_set, 1)
                high_y(1)
                for t in range(T):
                    act.wait_ge(x_ready, t + 1)
                    if t >= 1:
                        act.wait_ge(sq, t)
                    nc.scalar.activation(junk, k.x[:, t, :], ACT.Square, accum_out=ssq[:, t:t + 1]).then_inc(sq, 1)
                    if t + 2 < T:
                        high_y(t + 2)
                    act.wait_ge(turned, t + 1)
                    for n in range(2):
                        if t >= 2:
                            act.wait_ge(lg_ready, t - 1)
                        nc.scalar.activation(hT2[:, t % 2, 4 * n:4 * n + 4, :], k.ps[:, 4 + n, :].rearrange("p (c s) -> p c s", c=4),
                                             ACT.Copy).then_inc(ht_ready, 1)

            @block.vector
            def _(dve):
                def low_y(t):
                    if t >= 2:
                        dve.wait_ge(o_ready, t - 1)
                    for i, (src, chunks) in enumerate(parts(t)):
                        dve.wait_ge(y_hi_set, 2 * t + i + 1)
                        nc.vector.tensor_tensor(y_lo[:, t % 2, chunks, :], src, y_hi[:, t % 2, chunks, :],
                                                ALU.subtract).then_inc(y_lo_set, 1)

                low_y(0)
                for c in range(KD):
                    dve.wait_ge(w_hi_set, c + 1)
                    nc.vector.tensor_tensor(w_lo[:, c, :], k.wo[:, c, :], w_hi[:, c, :], ALU.subtract).then_inc(w_lo_set, 1)
                low_y(1)

                def take_logits(t):
                    dve.wait_ge(lg_ready, t + 1)
                    nc.vector.tensor_tensor(k.logits[:, t, :], k.ps[:, 6, 0:G + E], k.rb[:], ALU.add).then_inc(lg_took, 1)

                for t in range(T):
                    dve.wait_ge(o_ready, t + 1)
                    nc.vector.tensor_tensor(k.x[:, t, :], k.x[:, t, :],
                                            k.ps[:, 2 * (t % 2):2 * (t % 2) + 2, :].rearrange("p b n -> p (b n)"),
                                            ALU.add).then_inc(x_ready, 1)
                    if t + 2 < T:
                        low_y(t + 2)
                    dve.wait_ge(rstd_ready, t + 1)
                    if t >= 2:
                        dve.wait_ge(h_stored, 16 * t)
                        dve.wait_ge(turned, t - 1)
                    nc.vector.scalar_tensor_tensor(h[:, t % 2, :], k.x[:, t, :], ssq[:, t:t + 1], k.gain[:],
                                                   ALU.mult, ALU.mult).then_inc(h_ready, 1)
                    if t >= 2:
                        take_logits(t - 2)
                take_logits(T - 2)
                take_logits(T - 1)


def route(nc, k, st, plan_ready, rows_ready):
    step, exp_in, exp_out, sel_ready, ranks_ready, hot_ready, scattered = (
        st.sem("route_step"), st.sem("exp_in"), st.sem("exp_out"), st.sem("sel_ready"), st.sem("ranks_ready"),
        st.sem("hot_ready"), st.sem("scattered"))
    gm, gs, gx, m1, m2, ss, e2, den = (st.sb(f"tok{i}", [P, T]) for i in range(8))
    gd, goh = st.sb("gd", [P, T, G]), st.sb("goh", [P, T, G])
    el, el2, o1, o2, t8 = (st.sb(f"exp{i}", [P, T, EG]) for i in range(5))
    big = st.sb("big", [P, T, G, EG])
    M1, M2 = (st.sb(f"sel{i}", [P, T, G, EG]) for i in range(2))
    MM = st.sb("MM", [P, T, G, EG], BF16)
    lt, ones, masks_set = st.sb("lt_b", [P, P], BF16), st.sb("ones_b", [P, P], BF16), st.sem("masks_set")
    R = st.sb("R", [P, T, E])
    cnt, nb, pe_, start = (st.sb(f"cnt{i}", [P, E]) for i in range(4))
    ni = st.sb("ni", [P, E], I32)
    pmi, pbi = st.sb("pmi", [P, T, 2], I32), st.sb("pbi", [P, T, 2], I32)
    pos = st.sb("pos", [P, T, 2])
    pm, pb = st.sb("pm", [P, T, 2]), st.sb("pb", [P, T, 2])
    hotp = st.sb("hotp", [P, T, 2, P], BF16)
    hotb = st.sb("hotb", [P, T, 2, BLK], BF16)
    token = st.sb("token", [P, T, 2, 2, BLK], BF16)
    be = st.sb("be", [P, BLK])
    ends = st.sb("ends", [P, E])
    ended = st.sb("ended", [P, 1])
    ended_ready, ended_turned, totals_ready = st.sem("ended_ready"), st.sem("ended_turned"), st.sem("totals_ready")
    lgG = k.logits[:, :, 0:G]
    lgE = k.logits[:, :, G:].rearrange("p t (g e) -> p t g e", g=G)

    def on_act(act):
        nc.scalar.activation(lt[:], k.c("lt"), ACT.Copy)
        nc.scalar.activation(ones[:], k.c("ones"), ACT.Copy).then_inc(masks_set, 1)
        act.wait_ge(exp_in, 1)
        nc.scalar.activation(gd[:], gd[:], ACT.Exp).then_inc(exp_out, 1)
        act.wait_ge(exp_in, 2)
        nc.scalar.activation(t8[:], t8[:], ACT.Exp).then_inc(exp_out, 1)
        act.wait_ge(exp_in, 3)
        nc.scalar.activation(e2[:], e2[:], ACT.Exp).then_inc(exp_out, 1)

    def on_pe(pe):
        pe.wait_ge(sel_ready, 1)
        flat = MM[:].rearrange("p t g e -> p (t g e)")
        pe.wait_ge(masks_set, 1)
        nc.tensor.matmul(k.ps[:, 1, 0:T * E], ones[:], flat, start=True, stop=True).then_inc(totals_ready, 1)
        nc.tensor.matmul(k.ps[:, 0, 0:T * E], lt[:], flat, start=True, stop=False, skip_group_check=True)
        for t in range(1, T):
            last = nc.tensor.matmul(k.ps[:, 0, t * E:T * E], ones[:], flat[:, 0:(T - t) * E], start=False, stop=(t == T - 1),
                                    skip_group_check=True)
        last.then_inc(ranks_ready, 1)
        pe.wait_ge(ended_ready, 1)
        nc.tensor.transpose(k.ps[0:1, 3, 0:P], ended[:], k.c("ident")).then_inc(ended_turned, 1)
        pe.wait_ge(hot_ready, 1)
        n = 0
        for t in range(T):
            for i in range(2):
                last = nc.tensor.matmul(k.ps[:, 2, 0:2 * BLK], hotp[:, t, i, :], token[:, t, i].rearrange("p a b -> p (a b)"),
                                        start=(n == 0), stop=(n == 2 * T - 1))
                n += 1
        last.then_inc(scattered, 1)

    def on_dve(dve):
        link = linker(dve, step)
        V = nc.vector

        def b3(a, n):
            return bc(a.unsqueeze(2), P, T, n)

        def pick(dst, val, best, rank, n, tmp):
            link(V.tensor_tensor(tmp, val, b3(best, n), ALU.is_equal))
            link(V.tensor_tensor(tmp, tmp, bc(rank.unsqueeze(1), P, T, n), ALU.mult))
            link(V.tensor_reduce(gx[:], tmp, AX, ALU.max))
            link(V.tensor_tensor(dst, tmp, b3(gx[:], n), ALU.is_equal))

        link(V.tensor_reduce(gm[:], lgG, AX, ALU.max))
        pick(goh[:], lgG, gm[:], k.c("rank4"), G, gd[:])
        V.tensor_tensor(gd[:], lgG, b3(gm[:], G), ALU.subtract).then_inc(exp_in, 1)
        link(V.tensor_tensor(big[:], lgE, bc(goh[:].unsqueeze(3), P, T, G, EG), ALU.mult))
        link(V.tensor_reduce(el[:], big[:].rearrange("p t g e -> p t e g"), AX, ALU.add))
        link(V.tensor_reduce(m1[:], el[:], AX, ALU.max))
        pick(o1[:], el[:], m1[:], k.c("rank8"), EG, t8[:])
        link(V.scalar_tensor_tensor(el2[:], o1[:], NEG, el[:], ALU.mult, ALU.add))
        link(V.tensor_reduce(m2[:], el2[:], AX, ALU.max))
        pick(o2[:], el2[:], m2[:], k.c("rank8"), EG, t8[:])
        V.tensor_tensor(t8[:], el[:], b3(m1[:], EG), ALU.subtract).then_inc(exp_in, 1)
        V.tensor_tensor(e2[:], m2[:], m1[:], ALU.subtract).then_inc(exp_in, 1)
        for o, m in ((o1, M1), (o2, M2)):
            link(V.tensor_tensor(m[:], bc(goh[:].unsqueeze(3), P, T, G, EG), bc(o[:].unsqueeze(2), P, T, G, EG), ALU.mult))
        V.tensor_tensor(MM[:], M1[:], M2[:], ALU.add).then_inc(sel_ready, 1)
        dve.wait_ge(totals_ready, 1)
        tot = k.ps[:, 1, 0:T * E].rearrange("p (t e) -> p t e", t=T)
        link(V.tensor_reduce(cnt[:], tot.rearrange("p t e -> p e t"), AX, ALU.add))
        link(V.tensor_scalar(ni[:], cnt[:], float(P - 1), None, ALU.add))
        link(V.tensor_scalar(ni[:], ni[:], LOG_P, None, ALU.arith_shift_right))
        link(V.tensor_copy(nb[:], ni[:]))
        src = nb
        for i in range(5):
            dst, n = (pe_, cnt)[i % 2], 1 << i
            V.tensor_copy(dst[:, 0:n], src[:, 0:n])
            link(V.tensor_tensor(dst[:, n:], src[:, n:], src[:, 0:E - n], ALU.add))
            src = dst
        link(V.tensor_scalar(ends[:], pe_[:], k.c("partition"), None, ALU.is_le))
        V.tensor_reduce(ended[:], ends[:], AX, ALU.add).then_inc(ended_ready, 1)
        link(V.tensor_scalar(k.npair_i[:], pe_[:, E - 1:E], 1.0, None, ALU.add))
        link(V.tensor_scalar(k.npair_i[:], k.npair_i[:], 1, None, ALU.arith_shift_right))
        link(V.tensor_tensor(start[:], pe_[:], nb[:], ALU.subtract))
        dve.wait_ge(ended_turned, 1)
        V.tensor_scalar(k.expert_i[0:1, :], k.ps[0:1, 3, 0:BLK], float(E - 1), None, ALU.min).then_inc(plan_ready, 1)
        link(V.tensor_scalar(start[:], start[:], float(P), None, ALU.mult))
        dve.wait_ge(ranks_ready, 1)
        link(V.tensor_tensor(R[:], bc(start[:].unsqueeze(1), P, T, E), k.ps[:, 0, 0:T * E].rearrange("p (t e) -> p t e", t=T), ALU.add))
        for i, m in enumerate((M1, M2)):
            mf = m[:].rearrange("p t g e -> p t (g e)")
            link(V.tensor_tensor(mf, mf, R[:], ALU.mult))
            link(V.tensor_reduce(pos[:, :, i:i + 1], mf, AX, ALU.add))
        link(V.tensor_copy(k.pos_i[:], pos[:]))
        link(V.tensor_scalar(pmi[:], k.pos_i[:], P - 1, None, ALU.bitwise_and))
        link(V.tensor_scalar(pbi[:], k.pos_i[:], LOG_P, None, ALU.arith_shift_right))
        link(V.tensor_copy(pm[:], pmi[:]))
        link(V.tensor_copy(pb[:], pbi[:]))
        iota = k.c("iota")
        link(V.tensor_tensor(hotp[:], bc(iota.unsqueeze(1).unsqueeze(1), P, T, 2, P), bc(pm[:].unsqueeze(3), P, T, 2, P), ALU.is_equal))
        link(V.tensor_tensor(hotb[:], bc(iota[:, 0:BLK].unsqueeze(1).unsqueeze(1), P, T, 2, BLK), bc(pb[:].unsqueeze(3), P, T, 2, BLK),
                             ALU.is_equal))
        V.tensor_scalar(token[:, :, :, 0, :], hotb[:], k.c("partition"), None, ALU.mult)
        V.tensor_tensor(token[:, :, :, 1, :], hotb[:], bc(k.c("tile").unsqueeze(2).unsqueeze(3), P, T, 2, BLK), ALU.mult).then_inc(hot_ready, 1)
        dve.wait_ge(scattered, 1)
        link(V.tensor_reduce(be[:], k.ps[:, 2, 0:2 * BLK].rearrange("p (a b) -> p b a", a=2), AX, ALU.add))
        V.tensor_copy(k.rows_i[:], be[:]).then_inc(rows_ready, 1)
        dve.wait_ge(exp_out, 1)
        link(V.tensor_reduce(gs[:], gd[:], AX, ALU.add))
        link(V.reciprocal(gs[:], gs[:]))
        dve.wait_ge(exp_out, 3)
        link(V.tensor_reduce(ss[:], t8[:], AX, ALU.add))
        link(V.reciprocal(ss[:], ss[:]))
        link(V.tensor_tensor(e2[:], e2[:], ss[:], ALU.mult))
        link(V.tensor_tensor(den[:], e2[:], ss[:], ALU.add))
        link(V.reciprocal(den[:], den[:]))
        link(V.tensor_tensor(den[:], den[:], gs[:], ALU.mult))
        V.tensor_tensor(k.wts[:, :, 0], ss[:], den[:], ALU.mult)
        V.tensor_tensor(k.wts[:, :, 1], e2[:], den[:], ALU.mult)

    return on_act, on_pe, on_dve


def wait_past(eng, sem, value):
    if not isinstance(value, int) or value > 0:
        eng.wait_ge(sem, value)


def experts(nc, k, l):
    with Stage(nc, pool_dmas=True) as st:
        idx_ready, plan_ready, rows_ready = st.sem("idx_ready"), st.sem("plan_ready"), st.sem("rows_ready")
        route_act, route_pe, route_dve = route(nc, k, st, plan_ready, rows_ready)
        x_in = [st.sem("x_in0"), st.sem("x_in1")]
        gu_in = [st.sem("gu_in0"), st.sem("gu_in1")]
        dn_in = [st.sem("dn_in0"), st.sem("dn_in1")]
        x_turned, xt_ready, gu_ready, silued, h_ready = (st.sem("x_turned"), st.sem("xt_ready"), st.sem("gu_ready"),
                                                         st.sem("silued"), st.sem("h_ready"))
        h_turned, ht_ready, y_ready, y_act, y_dve = (st.sem("h_turned"), st.sem("ht_ready"), st.sem("y_ready"), st.sem("y_act"),
                                                     st.sem("y_dve"))
        y_out = [st.sem("y_out0"), st.sem("y_out1")]
        all_stored, gather_due = st.sem("all_stored"), st.sem("gather_due")
        idx = st.sb("idx", [P, 2], I32)
        xg = st.sb("xg", [P, 2, D])
        xT = st.sb("xT", [P, 2, KD, P])
        wgu = st.sb("wgu", [P, 2, KD, 2 * FF])
        wd = st.sb("wd", [P, 2, 2, D])
        sg = st.sb("sg", [P, 2, FF])
        hh = st.sb("hh", [P, 2, FF])
        hT = st.sb("hT_ff", [P, 2, 2, P])
        y = st.sb("y_out", [P, 2, D])

        def turns(eng, turn):
            eng.wait_ge(plan_ready, 1)
            n = eng.value_load(k.npair_i[0:1, 0:1], min_val=LEAST // 2, max_val=BLOCKS // 2)
            turn(0)
            with eng.Fori(1, n) as p:
                turn(p)
            return n

        def column(table, b):
            return table[:, b:b + 1] if isinstance(b, int) else table[:, bass.ds(b, 1)]

        with nc.Block() as block:
            @block.gpsimd
            def _(pool):
                def gather(s, b):
                    nc.gpsimd.tensor_copy(idx[:, s:s + 1], column(k.rows_i, b)).then_inc(idx_ready, 1)
                    pool.wait_ge(idx_ready, b + 1)
                    pool.sem_inc(gather_due, 1)
                    pool.indirect_dma_start(xg[:, s, :], None, k.d_h[:, :],
                                            bass.IndirectOffsetOnAxis(idx[:, s:s + 1], axis=0)).then_inc(x_in[s], 16)

                def turn(p):
                    for s in range(2):
                        b = p * 2 + s
                        wait_past(pool, x_turned, b)
                        gather(1 - s, b + 1)

                pool.wait_ge(rows_ready, 1)
                gather(0, 0)
                n = turns(pool, turn)
                for s in range(2):
                    pool.wait_ge(x_in[s], (n + 1 - s) * 16)
                    pool.sem_inc(gather_due, 1)

            @block.sync
            def _(sp):
                def turn(p):
                    for s in range(2):
                        b = p * 2 + s
                        e = sp.value_load(column(k.expert_i[0:1, :], b), min_val=0, max_val=E - 1)
                        w = bass.ds(l * E + e, 1)
                        if isinstance(b, int) and b == 1:
                            sp.wait_ge(x_in[1], 16)
                        wait_past(sp, gu_ready, b - 1)
                        sp.dma_start(wgu[:, s, :, 0:FF], k.w_gate[w].rearrange("a (c p) n -> p (a c) n", p=P)).then_inc(gu_in[s], 16)
                        sp.dma_start(wgu[:, s, :, FF:], k.w_up[w].rearrange("a (c p) n -> p (a c) n", p=P)).then_inc(gu_in[s], 16)
                        wait_past(sp, y_ready, b - 1)
                        sp.dma_start(wd[:, s], k.w_down[w].rearrange("a (c p) n -> p (a c) n", p=P)).then_inc(dn_in[s], 16)

                turns(sp, turn)

            @block.tensor
            def _(pe):
                def turn_x(s, nth, b):
                    pe.wait_ge(x_in[s], nth * 16)
                    wait_past(pe, xt_ready, b * 2)
                    for c in range(KD):
                        last = nc.tensor.transpose(k.ps[:, c // 4, (c % 4) * P:(c % 4 + 1) * P], xg[:, s, c * P:(c + 1) * P], k.c("ident"))
                    last.then_inc(x_turned, 1)

                def down(s, nth, b):
                    pe.wait_ge(ht_ready, b + 1)
                    pe.wait_ge(dn_in[s], nth * 16)
                    pe.wait_ge(y_act, b + 1)
                    pe.wait_ge(y_dve, b + 1)
                    for m in range(2):
                        for c in range(2):
                            last = nc.tensor.matmul(k.ps[:, 5 + m, :], hT[:, s, c, :], wd[:, s, c, m * HALF:(m + 1) * HALF],
                                                    start=(c == 0), stop=(c == 1))
                    last.then_inc(y_ready, 1)

                def turn(p):
                    for s in range(2):
                        b = p * 2 + s
                        pe.wait_ge(gu_in[s], p * 32 + 32)
                        pe.wait_ge(xt_ready, b * 2 + 2)
                        for c in range(KD):
                            last = nc.tensor.matmul(k.ps[:, 2 + s, :], xT[:, s, c, :], wgu[:, s, c, :], start=(c == 0), stop=(c == KD - 1))
                        last.then_inc(gu_ready, 1)
                        turn_x(1 - s, p + 1 + s, b + 1)
                        if not (isinstance(b, int) and b == 0):
                            down(1 - s, p + s, b - 1)
                        pe.wait_ge(h_ready, b + 1)
                        for c in range(2):
                            last = nc.tensor.transpose(k.ps[:, 4, c * P:(c + 1) * P], hh[:, s, c * P:(c + 1) * P], k.c("ident"))
                        last.then_inc(h_turned, 1)

                route_pe(pe)
                turn_x(0, 1, 0)
                n = turns(pe, turn)
                down(1, n, n * 2 - 1)

            @block.scalar
            def _(act):
                def take_x(s, b):
                    act.wait_ge(x_turned, b + 1)
                    for m in range(2):
                        nc.scalar.activation(xT[:, s, 4 * m:4 * m + 4, :], k.ps[:, m, :].rearrange("p (c s) -> p c s", c=4),
                                             ACT.Copy).then_inc(xt_ready, 1)

                def store(s, nth, b):
                    act.wait_ge(y_ready, b + 1)
                    act.wait_ge(y_out[s], nth * 16)
                    nc.scalar.activation(y[:, s, 0:HALF], k.ps[:, 5, :], ACT.Copy).then_inc(y_act, 1)
                    act.wait_ge(y_act, b + 2)
                    act.wait_ge(y_dve, b + 2)
                    rows = k.d_y[b * P:(b + 1) * P, :] if isinstance(b, int) else k.d_y[bass.ds(b * P, P), :]
                    act.dma_start(rows, y[:, s, :]).then_inc(y_out[s], 16)

                def turn(p):
                    for s in range(2):
                        b = p * 2 + s
                        act.wait_ge(gu_ready, b + 1)
                        nc.scalar.activation(sg[:, s, :], k.ps[:, 2 + s, 0:FF], ACT.Silu).then_inc(silued, 1)
                        take_x(1 - s, b + 1)
                        if not (isinstance(b, int) and b == 0):
                            store(1 - s, p + s, b - 1)
                        act.wait_ge(h_turned, b + 1)
                        nc.scalar.activation(hT[:, s], k.ps[:, 4, 0:2 * P].rearrange("p (c s) -> p c s", c=2), ACT.Copy).then_inc(ht_ready, 1)

                route_act(act)
                act.sem_inc(y_act, 1)
                act.sem_inc(y_out[0], 16)
                act.sem_inc(y_out[1], 16)
                take_x(0, 0)
                n = turns(act, turn)
                store(1, n, n * 2 - 1)
                for s in range(2):
                    act.wait_ge(y_out[s], n * 16 + 16)
                    act.sem_inc(all_stored, 1)
                act.wait_ge(all_stored, 2)

            @block.vector
            def _(dve):
                def take_y(s, nth, b):
                    dve.wait_ge(y_ready, b + 1)
                    dve.wait_ge(y_out[s], nth * 16)
                    nc.vector.tensor_copy(y[:, s, HALF:], k.ps[:, 6, :]).then_inc(y_dve, 1)

                def turn(p):
                    for s in range(2):
                        b = p * 2 + s
                        dve.wait_ge(silued, b + 1)
                        nc.vector.tensor_tensor(hh[:, s, :], sg[:, s, :], k.ps[:, 2 + s, FF:], ALU.mult).then_inc(h_ready, 1)
                        if not (isinstance(b, int) and b == 0):
                            take_y(1 - s, p + s, b - 1)

                route_dve(dve)
                dve.sem_inc(y_dve, 1)
                n = turns(dve, turn)
                take_y(1, n, n * 2 - 1)


def combine(nc, k):
    with Stage(nc, pool_dmas=True) as st:
        y_in = [st.sem(f"y_in{i}") for i in range(4)]
        first, added = st.sem("first"), st.sem("added")
        yg = st.sb("yg", [P, 4, D])
        with nc.Block() as block:
            @block.gpsimd
            def _(pool):
                for n in range(2 * T):
                    t, i = n // 2, n % 2
                    if n >= 4:
                        pool.wait_ge((first, added)[i], t - 1)
                    pool.indirect_dma_start(yg[:, n % 4, :], None, k.d_y[:, :],
                                            bass.IndirectOffsetOnAxis(k.pos_i[:, t, i:i + 1], axis=0)).then_inc(y_in[n % 4], 16)
                for n in range(4):
                    pool.wait_ge(y_in[n], 16 * (2 * T // 4))

            @block.vector
            def _(dve):
                for n in range(2 * T):
                    t, i = n // 2, n % 2
                    dve.wait_ge(y_in[n % 4], 16 * (n // 4 + 1))
                    if i:
                        dve.wait_ge(first, t + 1)
                    nc.vector.scalar_tensor_tensor(k.x[:, t, :], yg[:, n % 4, :], k.wts[:, t, i:i + 1], k.x[:, t, :],
                                                   ALU.mult, ALU.add).then_inc((first, added)[i], 1)
                dve.wait_ge(added, T)


def final(nc, k):
    with Stage(nc) as st:
        gain_in, sq, step, ready, stored = st.sem("gain_in"), st.sem("sq"), st.sem("final_step"), st.sem("ready"), st.sem("stored")
        rstd_ready = st.sem("rstd_ready")
        ssq = st.sb("ssq5", [P, T])
        junk = st.sb("junk5", [P, 2, D])
        out = k.out.rearrange("b (t p) n -> p (b t) n", p=P)
        with nc.Block() as block:
            @block.gpsimd
            def _(pool):
                link = linker(pool, step)
                for t in range(T):
                    pool.wait_ge(sq, t + 1)
                    rstd(nc, k, link, ssq[:, t:t + 1], D).then_inc(rstd_ready, 1)

            @block.sync
            def _(sp):
                sp.dma_start(k.gain[:], bc(k.norm_final.unsqueeze(0), P, D)).then_inc(gain_in, 16)
                for t in range(T):
                    sp.wait_ge(ready, t + 1)
                    sp.dma_start(out[:, t, :], k.x[:, t, :]).then_inc(stored, 16)
                sp.wait_ge(stored, 16 * T)

            @block.scalar
            def _(act):
                for t in range(T):
                    if t >= 2:
                        act.wait_ge(sq, t - 1)
                    nc.scalar.activation(junk[:, t % 2, :], k.x[:, t, :], ACT.Square, accum_out=ssq[:, t:t + 1]).then_inc(sq, 1)

            @block.vector
            def _(dve):
                dve.wait_ge(gain_in, 16)
                for t in range(T):
                    dve.wait_ge(rstd_ready, t + 1)
                    nc.vector.scalar_tensor_tensor(k.x[:, t, :], k.x[:, t, :], ssq[:, t:t + 1], k.gain[:],
                                                   ALU.mult, ALU.mult).then_inc(ready, 1)


def program(nc, d_const, x, positions, norm_mix, w_in, conv_a, fox_forget_bias, ssm_conv_w, ssm_conv_b, ssm_dt_bias,
            ssm_a_log, ssm_d, ssm_norm, mla_q_norm, mla_kv_norm, mla_w_uq, mla_w_ukv, w_out, norm_ffn, router_group_w,
            router_group_b, router_expert_w, router_expert_b, expert_w_gate, expert_w_up, expert_w_down, norm_final, out):
    with ExitStack() as ctx:
        def sb(name, shape, dtype=F32):
            return ctx.enter_context(nc.sbuf_tensor(name, shape, dtype))

        k = Core()
        k.d_const, k.d_x, k.positions, k.out = d_const, x, positions, out
        k.norm_mix, k.norm_ffn, k.norm_final = norm_mix, norm_ffn, norm_final
        k.w_in, k.w_out, k.conv_a, k.fox_forget_bias = w_in, w_out, conv_a, fox_forget_bias
        k.ssm_conv_w, k.ssm_conv_b, k.ssm_dt_bias, k.ssm_a_log = ssm_conv_w, ssm_conv_b, ssm_dt_bias, ssm_a_log
        k.ssm_d, k.ssm_norm = ssm_d, ssm_norm
        k.mla_q_norm, k.mla_kv_norm, k.mla_w_uq, k.mla_w_ukv = mla_q_norm, mla_kv_norm, mla_w_uq, mla_w_ukv
        k.router_group_w, k.router_group_b = router_group_w, router_group_b
        k.router_expert_w, k.router_expert_b = router_expert_w, router_expert_b
        k.w_gate, k.w_up, k.w_down = (w.rearrange("l e k n -> (l e) k n") for w in (expert_w_gate, expert_w_up, expert_w_down))
        k.d_h = nc.dram_tensor("h_rows", (S, D), F32).ap()
        k.d_y = nc.dram_tensor("y_rows", (BLOCKS * P, D), F32).ap()
        k.x_in = [ctx.enter_context(nc.semaphore(f"x_in_{m}")) for m in range(4)]
        k.d_xs = nc.dram_tensor("x_saved", (P, T, D), F32).ap()
        k.ps = ctx.enter_context(nc.psum_tensor("banks", [P, 8, HALF], F32))

        k.x = sb("x_res", [P, T, D])
        k.x_end = ends_at(nc)
        k.const = sb("const", [P, CONSTANTS.shape[1]])
        k.c = lambda name: k.const[:, CONST[name][0]:CONST[name][0] + CONST[name][1]]
        k.ident_b = sb("ident_b", [P, P], BF16)
        k.mask_fox = sb("mask_fox", [P, P], BF16)
        k.mask_mla = sb("mask_mla", [P, P], BF16)
        k.mask_ssd = sb("mask_ssd", [P, HEADS * P], BF16)
        k.trig = sb("trig", [P, 2, T, HR])
        k.gain = sb("gain", [P, D])
        k.cw, k.cb, k.ca = sb("cw", [P, 4, TAPS_C]), sb("cb", [P, 4]), sb("ca", [P, 2, TAPS_A])
        k.bias8, k.alog, k.dskip = sb("bias8", [P, 2 * HEADS]), sb("alog", [P, HEADS]), sb("dskip", [P, HEADS])
        k.sng, k.qng, k.kvng = sb("sng", [P, GW]), sb("qng", [P, GW]), sb("kvng", [P, P])
        k.rb, k.rw = sb("rb", [P, G + E]), sb("rw", [P, KD, G + E])
        k.wuq, k.wukv = sb("wuq", [P, 2, HEADS * MLA_D]), sb("wukv", [P, HALF])
        k.logits = sb("logits", [P, T, G + E])
        k.wts, k.pos_i = sb("wts", [P, T, 2]), sb("pos_rows", [P, T, 2], I32)
        k.expert_i, k.npair_i, k.rows_i = sb("expert_i", [P, BLK], I32), sb("npair_i", [P, 1], I32), sb("rows_i", [P, BLK], I32)

        setup(nc, k)
        with nc.Fori(0, DEPTH) as l:
            with ExitStack() as mix:
                def sm(name, shape):
                    return mix.enter_context(nc.sbuf_tensor(name, shape, F32))

                k.hT = sm("hT", [P, KD, S])
                k.hT_end = ends_at(nc)
                k.yT = k.hT[:, 0:6, :]
                k.vm = k.hT[:, 6:8, :].rearrange("p a s -> p (a s)").rearrange("p (t n) -> p t n", t=T)
                k.QK = sm("QK", [P, 2, HEADS, S])
                k.QK_end = ends_at(nc)
                k.QT, k.KT = k.QK[:, 0], k.QK[:, 1]
                k.yA = sm("yA", [P, 2, S])
                k.xbcT = sm("xbcT", [P, 4, S])
                k.wo_end = ends_at(nc) + 4 * (KD * D - 4 * S)
                k.wo = over_again(nc, "wo", [P, KD, D], F32, k.wo_end)
                lows = WMAX + P + ROPE
                k.over = sm("over", [P, T * (GW + WMAX + lows)])
                k.z = k.over[:, 0:T * GW].rearrange("p (t n) -> p t n", t=T)
                k.vf = k.over[:, T * GW:T * (GW + WMAX)].rearrange("p (t n) -> p t n", t=T)
                k.low = k.over[:, T * (GW + WMAX):].rearrange("p (t n) -> p t n", t=T)
                k.dt, k.adec = sm("dt", [P, T, HEADS]), sm("adec", [P, T, HEADS])
                k.low_rstd, k.kr = sm("low_rstd", [P, 2, T]), sm("kr", [P, T, 2, HR])
                k.decay, k.carry = sm("decay", [P, 2, T * HEADS]), sm("carry", [P, T, 2])

                project(nc, k, l)
                attend(nc, k, "fox", FOX_K, lambda b, h: k.vf[:, b, h * HD:(h + 1) * HD], k.mask_fox, 0,
                       lambda st: fox_loads(nc, k, st))
                ssd(nc, k)
                attend(nc, k, "mla", MLA_D, lambda b, h: k.vm[:, b, h * HD:(h + 1) * HD], k.mask_mla, 4,
                       lambda st: mla_loads(nc, k, st, l))
                join(nc, k)
            experts(nc, k, l)
            combine(nc, k)
        final(nc, k)


_INS = ['x', 'positions', 'norm_mix', 'w_in', 'conv_a', 'fox_forget_bias', 'ssm_conv_w', 'ssm_conv_b', 'ssm_dt_bias',
        'ssm_a_log', 'ssm_d', 'ssm_norm', 'mla_q_norm', 'mla_kv_norm', 'mla_w_uq', 'mla_w_ukv', 'w_out', 'norm_ffn',
        'router_group_w', 'router_group_b', 'router_expert_w', 'router_expert_b', 'expert_w_gate', 'expert_w_up',
        'expert_w_down', 'norm_final']


def kernel(**inputs):
    import concourse.bacc as _bacc
    from concourse.bass_utils import run_bass_kernel_spmd as _run

    nc = _bacc.Bacc("TRN2", target_bir_lowering=False, num_devices=1)
    arrays = {"in_const_dram": CONSTANTS}
    args = [nc.dram_tensor("in_const_dram", CONSTANTS.shape, F32, kind="ExternalInput").ap()]
    for name in _INS:
        a = np.ascontiguousarray(inputs[name])
        arrays[f"in_{name}_dram"] = a
        args.append(nc.dram_tensor(f"in_{name}_dram", a.shape, mybir.dt.from_np(a.dtype), kind="ExternalInput").ap())
    args.append(nc.dram_tensor("out_0_dram", (1, S, D), F32, kind="ExternalOutput").ap())
    program(nc, *args)
    r = _run(nc, [arrays], core_ids=[0])
    return r.results[0]["out_0_dram"]
```
